# Optimizing a Trainium2 kernel written in Bass

```python
import math
import jax, jax.numpy as jnp
from jax import lax
import numpy as np

D_MODEL = 1024
BATCH = 1
SEQ = 256
DEPTH = 2

HEAD_DIM = 64
SCALE = HEAD_DIM ** -0.5
ROPE_THETA = 10000.0
NORM_EPS = 1e-5
BAND = 128

A_HEADS = 8
A_KV_HEADS = 2
A_GROUP = A_HEADS // A_KV_HEADS
CMP_BLOCK = 32
CMP_STRIDE = 16
CMP_HIDDEN = 256
SEL_BLOCK = 64
SEL_TOPK = 16
NSA_WINDOW = 512
NSA_QBLOCK = 64
N_BRANCH = 3

B_HEADS = 8
B_KV_HEADS = 2
B_GROUP = B_HEADS // B_KV_HEADS
B_WINDOW = 128

C_HEADS = 16
C_PATTERNS = ((128, 1), (512, 4), (2048, 16))

A_Q = A_HEADS * HEAD_DIM
A_KV = A_KV_HEADS * HEAD_DIM
A_GATES = A_HEADS * N_BRANCH
B_Q = B_HEADS * HEAD_DIM
B_KV = B_KV_HEADS * HEAD_DIM
EVEN_IN = A_Q + 6 * A_KV + A_GATES + B_Q + 2 * B_KV
EVEN_MIX = A_Q + B_Q
ODD_IN = 3 * C_HEADS * HEAD_DIM
ODD_MIX = C_HEADS * HEAD_DIM
FFN_HIDDEN = -(-8 * D_MODEL // (3 * 256)) * 256
N_EVEN = (DEPTH + 1) // 2
N_ODD = DEPTH // 2


def rms_norm(x, g):
    xf = x.astype(jnp.float32)
    y = xf * lax.rsqrt(jnp.mean(xf * xf, axis=-1, keepdims=True) + NORM_EPS)
    return (y * g.astype(jnp.float32)).astype(x.dtype)

def rope_tables(seq, dtype):
    inv = 1.0 / (ROPE_THETA ** (jnp.arange(0, HEAD_DIM, 2, dtype=jnp.float32) / HEAD_DIM))
    ang = jnp.arange(seq, dtype=jnp.float32)[:, None] * inv[None, :]
    ang = jnp.concatenate([ang, ang], axis=-1)
    return jnp.cos(ang).astype(dtype), jnp.sin(ang).astype(dtype)

def apply_rope(x, cos, sin):
    x1, x2 = jnp.split(x, 2, axis=-1)
    rot = jnp.concatenate([-x2, x1], axis=-1)
    return x * cos[:, None, :] + rot * sin[:, None, :]

def banded_attention(q, k, v, reach, sink=None):
    L, dh = q.shape[-2], q.shape[-1]
    nb = -(-L // BAND)
    pad = nb * BAND - L
    if pad:
        q = jnp.pad(q, [(0, 0)] * (q.ndim - 2) + [(0, pad), (0, 0)])
        k = jnp.pad(k, [(0, 0)] * (k.ndim - 2) + [(0, pad), (0, 0)])
        v = jnp.pad(v, [(0, 0)] * (v.ndim - 2) + [(0, pad), (0, 0)])
    qb = q.reshape(q.shape[:-2] + (nb, BAND, dh))
    kb = k.reshape(k.shape[:-2] + (nb, BAND, dh))
    vb = v.reshape(v.shape[:-2] + (nb, BAND, dh))

    def with_prev(t):
        prev = jnp.pad(t, [(0, 0)] * (t.ndim - 3) + [(1, 0), (0, 0), (0, 0)])[..., :-1, :, :]
        return jnp.concatenate([prev, t], axis=-2)

    kc, vc = with_prev(kb), with_prev(vb)
    s = jnp.einsum('...gnqd,...nkd->...gnqk', qb, kc, preferred_element_type=jnp.float32) * SCALE
    qi = jnp.arange(BAND)[:, None] + BAND
    kj = jnp.arange(2 * BAND)[None, :]
    diff = qi - kj
    mask = (diff >= 0) & (diff <= reach)
    not_before_start = (jnp.arange(nb)[:, None, None] > 0) | (kj[None] >= BAND)
    mask = mask[None] & not_before_start
    s = jnp.where(mask, s, -jnp.inf)
    m = jnp.max(s, axis=-1)
    if sink is not None:
        m = jnp.maximum(m, sink)
    p = jnp.exp(s - m[..., None])
    den = jnp.sum(p, axis=-1)
    if sink is not None:
        den = den + jnp.exp(sink - m)
    o = jnp.einsum('...gnqk,...nkd->...gnqd', p, vc.astype(jnp.float32)) / den[..., None]
    o = o.reshape(q.shape[:-2] + (nb * BAND, dh))[..., :L, :]
    lse = (m + jnp.log(den)).reshape(q.shape[:-2] + (nb * BAND,))[..., :L]
    return o, lse

def compress_blocks(t, pe, w1, w2):
    bsz, hkv, seq, dh = t.shape
    chunks = t.reshape(bsz, hkv, seq // CMP_STRIDE, CMP_STRIDE, dh)
    blocks = jnp.concatenate([chunks[:, :, :-1], chunks[:, :, 1:]], axis=-2)
    nc = blocks.shape[2]
    blocks = (blocks + pe).reshape(bsz, hkv, nc, CMP_BLOCK * dh)
    return jax.nn.silu(blocks @ w1) @ w2

def nsa_attention(q_plain, q_rot, k_cmp, v_cmp, k_sel, v_sel, k_win, v_win, gates,
                  pe_k, pe_v, wk1, wk2, wv1, wv2):
    bsz, seq = q_plain.shape[:2]
    dh = HEAD_DIM
    nc = seq // CMP_STRIDE - 1
    nb = seq // SEL_BLOCK
    n_sel = min(SEL_TOPK, nb)

    def group_q(t):
        return t.reshape(bsz, seq, A_KV_HEADS, A_GROUP, dh).transpose(0, 2, 3, 1, 4)

    def heads_first(t):
        return t.transpose(0, 2, 1, 3)

    qp, qr = group_q(q_plain), group_q(q_rot)
    g = gates.reshape(bsz, seq, A_KV_HEADS, A_GROUP, N_BRANCH).transpose(0, 2, 3, 1, 4)
    kc = compress_blocks(heads_first(k_cmp), pe_k, wk1, wk2)
    vc = compress_blocks(heads_first(v_cmp), pe_v, wv1, wv2).astype(jnp.float32)
    ks_b = heads_first(k_sel).reshape(bsz, A_KV_HEADS, nb, SEL_BLOCK, dh)
    vs_b = heads_first(v_sel).reshape(bsz, A_KV_HEADS, nb, SEL_BLOCK, dh)
    pad_w = ((0, 0), (0, 0), (NSA_WINDOW, 0), (0, 0))
    kw_p = jnp.pad(heads_first(k_win), pad_w)
    vw_p = jnp.pad(heads_first(v_win), pad_w)

    cmp_end = jnp.arange(nc) * CMP_STRIDE + CMP_BLOCK - 1
    c_start = np.arange(nc) * CMP_STRIDE
    s_start = np.arange(nb) * SEL_BLOCK
    overlap = ((c_start[:, None] <= s_start[None, :] + SEL_BLOCK - 1) &
               (c_start[:, None] + CMP_BLOCK - 1 >= s_start[None, :]))
    cmp_to_sel = jnp.asarray(overlap.astype(np.float32))
    bi = jnp.arange(bsz)[:, None, None, None]
    hi = jnp.arange(A_KV_HEADS)[None, :, None, None]
    blk = jnp.arange(nb)[None, :]

    def query_block(i):
        q0 = i * NSA_QBLOCK
        tq = q0 + jnp.arange(NSA_QBLOCK)
        qp_b = lax.dynamic_slice_in_dim(qp, q0, NSA_QBLOCK, axis=3)
        qr_b = lax.dynamic_slice_in_dim(qr, q0, NSA_QBLOCK, axis=3)
        g_b = lax.dynamic_slice_in_dim(g, q0, NSA_QBLOCK, axis=3).astype(jnp.float32)

        s = jnp.einsum('bhgqd,bhcd->bhgqc', qp_b, kc, preferred_element_type=jnp.float32) * SCALE
        s = jnp.where(cmp_end[None, :] <= tq[:, None], s, -jnp.inf)
        m = jnp.max(s, axis=-1, keepdims=True)
        m = jnp.where(jnp.isfinite(m), m, 0.0)
        p = jnp.exp(s - m)
        den = jnp.sum(p, axis=-1, keepdims=True)
        p = p / jnp.where(den > 0, den, 1.0)
        o_cmp = jnp.einsum('bhgqc,bhcd->bhgqd', p, vc)

        imp = jnp.einsum('bhgqc,cn->bhqn', p, cmp_to_sel)
        cur = (tq // SEL_BLOCK)[:, None]
        forced = (blk == 0) | (blk == cur) | (blk == cur - 1)
        imp = jnp.where(forced, jnp.inf, jnp.where(blk > cur, -jnp.inf, imp))
        _, idx = lax.top_k(imp, n_sel)
        kg = ks_b[bi, hi, idx].reshape(bsz, A_KV_HEADS, NSA_QBLOCK, n_sel * SEL_BLOCK, dh)
        vg = vs_b[bi, hi, idx].reshape(bsz, A_KV_HEADS, NSA_QBLOCK, n_sel * SEL_BLOCK, dh)
        pos = (idx[..., None] * SEL_BLOCK + jnp.arange(SEL_BLOCK)).reshape(
            bsz, A_KV_HEADS, NSA_QBLOCK, n_sel * SEL_BLOCK)
        s = jnp.einsum('bhgqd,bhqkd->bhgqk', qr_b, kg, preferred_element_type=jnp.float32) * SCALE
        s = jnp.where((pos <= tq[:, None])[:, :, None], s, -jnp.inf)
        o_sel = jnp.einsum('bhgqk,bhqkd->bhgqd', jax.nn.softmax(s, axis=-1), vg.astype(jnp.float32))

        kw = lax.dynamic_slice_in_dim(kw_p, q0, NSA_QBLOCK + NSA_WINDOW, axis=2)
        vw = lax.dynamic_slice_in_dim(vw_p, q0, NSA_QBLOCK + NSA_WINDOW, axis=2)
        kpos = q0 - NSA_WINDOW + jnp.arange(NSA_QBLOCK + NSA_WINDOW)
        diff = tq[:, None] - kpos[None, :]
        wmask = (diff >= 0) & (diff < NSA_WINDOW) & (kpos[None, :] >= 0)
        s = jnp.einsum('bhgqd,bhkd->bhgqk', qr_b, kw, preferred_element_type=jnp.float32) * SCALE
        s = jnp.where(wmask, s, -jnp.inf)
        o_win = jnp.einsum('bhgqk,bhkd->bhgqd', jax.nn.softmax(s, axis=-1), vw.astype(jnp.float32))

        return g_b[..., 0:1] * o_cmp + g_b[..., 1:2] * o_sel + g_b[..., 2:3] * o_win

    out = lax.map(query_block, jnp.arange(seq // NSA_QBLOCK))
    out = out.transpose(1, 0, 4, 2, 3, 5)
    return out.reshape(bsz, seq, A_HEADS * dh)

def swa_sink_attention(q, k, v, sinks):
    bsz, seq = q.shape[:2]
    qg = q.reshape(bsz, seq, B_KV_HEADS, B_GROUP, HEAD_DIM).transpose(0, 2, 3, 1, 4)
    sink = sinks.astype(jnp.float32).reshape(B_KV_HEADS, B_GROUP, 1, 1)
    o, _ = banded_attention(qg, k.transpose(0, 2, 1, 3), v.transpose(0, 2, 1, 3), B_WINDOW - 1, sink)
    return o.transpose(0, 3, 1, 2, 4).reshape(bsz, seq, B_HEADS * HEAD_DIM)

def dilated_attention(q, k, v):
    bsz, seq, nh, dh = q.shape
    qt, kt, vt = (t.transpose(0, 2, 1, 3) for t in (q, k, v))
    outs, lses = [], []
    for window, dil in C_PATTERNS:
        sub = seq // dil

        def strided(t):
            return t.reshape(bsz, nh, sub, dil, dh).transpose(0, 1, 3, 2, 4)

        o, lse = banded_attention(strided(qt)[..., None, :, :], strided(kt), strided(vt), window // dil)
        outs.append(o[..., 0, :, :].transpose(0, 1, 3, 2, 4).reshape(bsz, nh, seq, dh))
        lses.append(lse[..., 0, :].transpose(0, 1, 3, 2).reshape(bsz, nh, seq))
    w = jax.nn.softmax(jnp.stack(lses, axis=0), axis=0)
    o = jnp.einsum('pbht,pbhtd->bhtd', w, jnp.stack(outs, axis=0))
    return o.transpose(0, 2, 1, 3).reshape(bsz, seq, nh * dh)

def first_inputs(seed: int = 0) -> dict:
    key = jax.random.key(seed)
    ks = jax.random.split(key, 17)
    nrm = jax.random.normal
    f32 = jnp.float32
    return {
        "x": nrm(ks[0], (BATCH, SEQ, D_MODEL), f32),
        "attn_norm": 1.0 + 0.02 * nrm(ks[1], (DEPTH, D_MODEL), f32),
        "ffn_norm": 1.0 + 0.02 * nrm(ks[2], (DEPTH, D_MODEL), f32),
        "final_norm": 1.0 + 0.02 * nrm(ks[3], (D_MODEL,), f32),
        "w_in_e": nrm(ks[4], (N_EVEN, D_MODEL, EVEN_IN), f32) * D_MODEL ** -0.5,
        "w_out_e": nrm(ks[5], (N_EVEN, EVEN_MIX, D_MODEL), f32) * EVEN_MIX ** -0.5,
        "cmp_pe_k": 0.02 * nrm(ks[6], (N_EVEN, CMP_BLOCK, HEAD_DIM), f32),
        "cmp_pe_v": 0.02 * nrm(ks[7], (N_EVEN, CMP_BLOCK, HEAD_DIM), f32),
        "cmp_k_w1": nrm(ks[8], (N_EVEN, CMP_BLOCK * HEAD_DIM, CMP_HIDDEN), f32) * (CMP_BLOCK * HEAD_DIM) ** -0.5,
        "cmp_k_w2": nrm(ks[9], (N_EVEN, CMP_HIDDEN, HEAD_DIM), f32) * CMP_HIDDEN ** -0.5,
        "cmp_v_w1": nrm(ks[10], (N_EVEN, CMP_BLOCK * HEAD_DIM, CMP_HIDDEN), f32) * (CMP_BLOCK * HEAD_DIM) ** -0.5,
        "cmp_v_w2": nrm(ks[11], (N_EVEN, CMP_HIDDEN, HEAD_DIM), f32) * CMP_HIDDEN ** -0.5,
        "sinks": 0.5 * nrm(ks[12], (N_EVEN, B_HEADS), f32),
        "w_qkv_o": nrm(ks[13], (N_ODD, D_MODEL, ODD_IN), f32) * D_MODEL ** -0.5,
        "w_out_o": nrm(ks[14], (N_ODD, ODD_MIX, D_MODEL), f32) * ODD_MIX ** -0.5,
        "w_gate_up": nrm(ks[15], (DEPTH, D_MODEL, 2 * FFN_HIDDEN), f32) * D_MODEL ** -0.5,
        "w_down": nrm(ks[16], (DEPTH, FFN_HIDDEN, D_MODEL), f32) * FFN_HIDDEN ** -0.5,
    }

def first_block(x, attn_norm, ffn_norm, final_norm, w_in_e, w_out_e, cmp_pe_k, cmp_pe_v,
              cmp_k_w1, cmp_k_w2, cmp_v_w1, cmp_v_w2, sinks, w_qkv_o, w_out_o,
              w_gate_up, w_down):
    bsz, seq, _ = x.shape
    cos, sin = rope_tables(seq, x.dtype)
    for layer in range(DEPTH):
        h = rms_norm(x, attn_norm[layer])
        if layer % 2 == 0:
            i = layer // 2
            z = h @ w_in_e[i]
            o1 = A_Q
            o2 = o1 + 6 * A_KV
            o3 = o2 + A_GATES
            o4 = o3 + B_Q
            aq = z[..., :o1].reshape(bsz, seq, A_HEADS, HEAD_DIM)
            akc, avc, aks, avs, akw, avw = [t.reshape(bsz, seq, A_KV_HEADS, HEAD_DIM)
                                            for t in jnp.split(z[..., o1:o2], 6, axis=-1)]
            gates = jax.nn.sigmoid(z[..., o2:o3].astype(jnp.float32)).reshape(bsz, seq, A_HEADS, N_BRANCH)
            bq = apply_rope(z[..., o3:o4].reshape(bsz, seq, B_HEADS, HEAD_DIM), cos, sin)
            bk, bv = [t.reshape(bsz, seq, B_KV_HEADS, HEAD_DIM) for t in jnp.split(z[..., o4:], 2, axis=-1)]
            bk = apply_rope(bk, cos, sin)
            a_out = nsa_attention(aq, apply_rope(aq, cos, sin), akc, avc,
                                  apply_rope(aks, cos, sin), avs, apply_rope(akw, cos, sin), avw, gates,
                                  cmp_pe_k[i], cmp_pe_v[i], cmp_k_w1[i], cmp_k_w2[i], cmp_v_w1[i], cmp_v_w2[i])
            b_out = swa_sink_attention(bq, bk, bv, sinks[i])
            mix = jnp.concatenate([a_out, b_out], axis=-1).astype(x.dtype)
            x = x + mix @ w_out_e[i]
        else:
            j = layer // 2
            z = h @ w_qkv_o[j]
            q, k, v = [t.reshape(bsz, seq, C_HEADS, HEAD_DIM) for t in jnp.split(z, 3, axis=-1)]
            c_out = dilated_attention(apply_rope(q, cos, sin), apply_rope(k, cos, sin), v)
            x = x + c_out.astype(x.dtype) @ w_out_o[j]
        h = rms_norm(x, ffn_norm[layer])
        gate, up = jnp.split(h @ w_gate_up[layer], 2, axis=-1)
        x = x + (jax.nn.silu(gate) * up) @ w_down[layer]
    return rms_norm(x, final_norm)


D_HEAD = 64
GRID_W = 64
Q_BLOCK = 128
RMS_EPS = 1e-6
H_A = D_MODEL // (2 * D_HEAD)
WIN_R = 8
WIN_C = 16
H_B = D_MODEL // (2 * D_HEAD)
H_B_KV = H_B // 4
AXIAL_THETA = 10000.0
H_C = D_MODEL // (2 * D_HEAD)
Q_LORA = D_MODEL // 4
KV_LORA = D_MODEL // 8
C_NOPE = 64
C_ROPE = 32
C_V = 64
MLA_THETA = 10000.0
H_D = D_MODEL // (4 * D_HEAD)
D_V = 2 * D_HEAD
ROPE_THETA_2 = 500000.0
ROT_DIM = D_HEAD // 4
GATE_E = (H_A + H_B) * D_HEAD
SPLIT_E = [H_A * D_HEAD, H_A * D_HEAD, H_A * D_HEAD,
           H_B * D_HEAD, H_B_KV * D_HEAD, H_B_KV * D_HEAD, GATE_E]
GATE_O = H_C * C_V + H_D * D_V
SPLIT_O = [Q_LORA, KV_LORA, C_ROPE, 2 * H_D * D_HEAD, 2 * H_D * D_HEAD,
           H_D * D_V, GATE_O]
IN_E = sum(SPLIT_E)
IN_O = sum(SPLIT_O)
N_EVEN_2 = (DEPTH + 1) // 2
N_ODD_2 = DEPTH // 2


def _split(x, sizes):
    idx = [int(v) for v in np.cumsum(sizes)[:-1]]
    return jnp.split(x, idx, axis=-1)

def rmsnorm(x, g):
    xf = x.astype(jnp.float32)
    y = xf * lax.rsqrt(jnp.mean(xf * xf, axis=-1, keepdims=True) + RMS_EPS)
    return (y * g.astype(jnp.float32)).astype(x.dtype)

def rope_angles(pos, dim, theta):
    inv = jnp.power(theta, -jnp.arange(0, dim, 2, dtype=jnp.float32) / dim)
    return pos[:, None] * inv[None, :]

def rotate(x, ang):
    shp = (ang.shape[0],) + (1,) * (x.ndim - 3) + (ang.shape[1],)
    c = jnp.cos(ang).reshape(shp).astype(x.dtype)
    s = jnp.sin(ang).reshape(shp).astype(x.dtype)
    x1, x2 = jnp.split(x, 2, axis=-1)
    return jnp.concatenate([x1 * c - x2 * s, x2 * c + x1 * s], axis=-1)

def attend_blocks(q, k, v, scale):
    B, S, Hq, dq = q.shape
    Hk, dv = k.shape[2], v.shape[3]
    G = Hq // Hk
    nb = S // Q_BLOCK
    qb = q.reshape(B, nb, Q_BLOCK, Hk, G, dq).transpose(1, 0, 2, 3, 4, 5)

    def one(qi):
        s = jnp.einsum('bqhgd,bkhd->bhgqk', qi, k).astype(jnp.float32) * scale
        p = jax.nn.softmax(s, axis=-1).astype(v.dtype)
        return jnp.einsum('bhgqk,bkhd->bqhgd', p, v)

    o = lax.map(one, qb)
    return o.transpose(1, 0, 2, 3, 4, 5).reshape(B, S, Hq, dv)

def diff_attend_blocks(q1, q2, k1, k2, v, lam, scale):
    B, S, H, d = q1.shape
    nb = S // Q_BLOCK
    q1b = q1.reshape(B, nb, Q_BLOCK, H, d).transpose(1, 0, 2, 3, 4)
    q2b = q2.reshape(B, nb, Q_BLOCK, H, d).transpose(1, 0, 2, 3, 4)

    def one(args):
        a, b = args
        s1 = jnp.einsum('bqhd,bkhd->bhqk', a, k1).astype(jnp.float32) * scale
        s2 = jnp.einsum('bqhd,bkhd->bhqk', b, k2).astype(jnp.float32) * scale
        p = jax.nn.softmax(s1, axis=-1) - lam * jax.nn.softmax(s2, axis=-1)
        return jnp.einsum('bhqk,bkhd->bqhd', p.astype(v.dtype), v)

    o = lax.map(one, (q1b, q2b))
    return o.transpose(1, 0, 2, 3, 4).reshape(B, S, H, v.shape[-1])

def neighbourhood_attention(q, k, v, rpb):
    B, S, H, d = q.shape
    rows = S // GRID_W
    wr = min(WIN_R, rows)
    wc = WIN_C
    qg = q.reshape(B, rows, GRID_W, H, d)
    kg = k.reshape(B, rows, GRID_W, H, d)
    vg = v.reshape(B, rows, GRID_W, H, d)
    col = jnp.arange(GRID_W)
    c0 = jnp.clip(col - wc // 2, 0, GRID_W - wc)
    cidx = c0[:, None] + jnp.arange(wc)[None, :]
    cb = (cidx - col[:, None] + (WIN_C - 1))[:, None, :]
    scale = d ** -0.5

    def one(r):
        r0 = jnp.clip(r - wr // 2, 0, rows - wr)
        kr = lax.dynamic_slice_in_dim(kg, r0, wr, axis=1)
        vr = lax.dynamic_slice_in_dim(vg, r0, wr, axis=1)
        kw = kr[:, :, cidx]
        vw = vr[:, :, cidx]
        qr = lax.dynamic_index_in_dim(qg, r, axis=1, keepdims=False)
        s = jnp.einsum('bqhd,biqjhd->bhqij', qr, kw).astype(jnp.float32) * scale
        rb = (r0 + jnp.arange(wr) - r + (WIN_R - 1))[None, :, None]
        bias = rpb[:, rb, cb].astype(jnp.float32)
        s = (s + bias[None]).reshape(B, H, GRID_W, wr * wc)
        p = jax.nn.softmax(s, axis=-1).reshape(B, H, GRID_W, wr, wc).astype(v.dtype)
        return jnp.einsum('bhqij,biqjhd->bqhd', p, vw)

    o = lax.map(one, jnp.arange(rows))
    return o.transpose(1, 0, 2, 3, 4).reshape(B, S, H, d)

def even_layer(x, norm, w_in, gq_a, gk_a, rpb, gq_b, gk_b, w_out, ang_row, ang_col):
    B, S, _ = x.shape
    h = rmsnorm(x, norm)
    qa, ka, va, qb, kb, vb, gate = _split(h @ w_in, SPLIT_E)
    qa = rmsnorm(qa.reshape(B, S, H_A, D_HEAD), gq_a)
    ka = rmsnorm(ka.reshape(B, S, H_A, D_HEAD), gk_a)
    va = va.reshape(B, S, H_A, D_HEAD)
    oa = neighbourhood_attention(qa, ka, va, rpb)
    half = D_HEAD // 2
    qb = rmsnorm(qb.reshape(B, S, H_B, D_HEAD), gq_b)
    kb = rmsnorm(kb.reshape(B, S, H_B_KV, D_HEAD), gk_b)
    qb = jnp.concatenate([rotate(qb[..., :half], ang_row), rotate(qb[..., half:], ang_col)], -1)
    kb = jnp.concatenate([rotate(kb[..., :half], ang_row), rotate(kb[..., half:], ang_col)], -1)
    vb = vb.reshape(B, S, H_B_KV, D_HEAD)
    ob = attend_blocks(qb, kb, vb, D_HEAD ** -0.5)
    o = jnp.concatenate([oa.reshape(B, S, -1), ob.reshape(B, S, -1)], -1) * jax.nn.silu(gate)
    return o @ w_out

def odd_layer(x, norm, w_in, g_cq, w_cq_b, g_ckv, w_ckv_b, gq_c, gk_c, gq_d, gk_d,
              lam_q1, lam_k1, lam_q2, lam_k2, g_sub_d, w_out, ang_mla, ang_part, lam_init):
    B, S, _ = x.shape
    h = rmsnorm(x, norm)
    cq, ckv, kpe, qd, kd, vd, gate = _split(h @ w_in, SPLIT_O)
    q = (rmsnorm(cq, g_cq) @ w_cq_b).reshape(B, S, H_C, C_NOPE + C_ROPE)
    kv = (rmsnorm(ckv, g_ckv) @ w_ckv_b).reshape(B, S, H_C, C_NOPE + C_V)
    k_nope, v_c = kv[..., :C_NOPE], kv[..., C_NOPE:]
    k_pe = jnp.broadcast_to(kpe[:, :, None, :], (B, S, H_C, C_ROPE))
    qc = rmsnorm(q, gq_c)
    kc = rmsnorm(jnp.concatenate([k_nope, k_pe], -1), gk_c)
    qc = jnp.concatenate([qc[..., :C_NOPE], rotate(qc[..., C_NOPE:], ang_mla)], -1)
    kc = jnp.concatenate([kc[..., :C_NOPE], rotate(kc[..., C_NOPE:], ang_mla)], -1)
    oc = attend_blocks(qc, kc, v_c, (C_NOPE + C_ROPE) ** -0.5)
    qd = rmsnorm(qd.reshape(B, S, H_D, 2, D_HEAD), gq_d)
    kd = rmsnorm(kd.reshape(B, S, H_D, 2, D_HEAD), gk_d)
    qd = jnp.concatenate([rotate(qd[..., :ROT_DIM], ang_part), qd[..., ROT_DIM:]], -1)
    kd = jnp.concatenate([rotate(kd[..., :ROT_DIM], ang_part), kd[..., ROT_DIM:]], -1)
    vd = vd.reshape(B, S, H_D, D_V)
    f32 = jnp.float32
    lam = (jnp.exp(jnp.sum(lam_q1.astype(f32) * lam_k1.astype(f32)))
           - jnp.exp(jnp.sum(lam_q2.astype(f32) * lam_k2.astype(f32))) + lam_init)
    od = diff_attend_blocks(qd[:, :, :, 0], qd[:, :, :, 1], kd[:, :, :, 0], kd[:, :, :, 1],
                            vd, lam, D_HEAD ** -0.5)
    od = rmsnorm(od, g_sub_d) * (1.0 - lam_init)
    o = jnp.concatenate([oc.reshape(B, S, -1), od.reshape(B, S, -1)], -1) * jax.nn.silu(gate)
    return o @ w_out

def second_inputs(seed: int = 0) -> dict:
    key = jax.random.key(seed)
    ks = iter(jax.random.split(key, 32))
    f32 = jnp.float32

    def w(shape, fan_in):
        return jax.random.normal(next(ks), shape, f32) * (fan_in ** -0.5)

    def gain(shape):
        return 1.0 + 0.1 * jax.random.normal(next(ks), shape, f32)

    def small(shape, s):
        return s * jax.random.normal(next(ks), shape, f32)

    NE, NO = N_EVEN_2, N_ODD_2
    return {
        "x": jax.random.normal(next(ks), (BATCH, SEQ, D_MODEL), f32),
        "norm_e": gain((NE, D_MODEL)),
        "w_in_e": w((NE, D_MODEL, IN_E), D_MODEL),
        "gq_a": gain((NE, D_HEAD)),
        "gk_a": gain((NE, D_HEAD)),
        "rpb_a": small((NE, H_A, 2 * WIN_R - 1, 2 * WIN_C - 1), 0.2),
        "gq_b": gain((NE, D_HEAD)),
        "gk_b": gain((NE, D_HEAD)),
        "w_out_e": w((NE, GATE_E, D_MODEL), GATE_E),
        "norm_o": gain((NO, D_MODEL)),
        "w_in_o": w((NO, D_MODEL, IN_O), D_MODEL),
        "g_cq": gain((NO, Q_LORA)),
        "w_cq_b": w((NO, Q_LORA, H_C * (C_NOPE + C_ROPE)), Q_LORA),
        "g_ckv": gain((NO, KV_LORA)),
        "w_ckv_b": w((NO, KV_LORA, H_C * (C_NOPE + C_V)), KV_LORA),
        "gq_c": gain((NO, C_NOPE + C_ROPE)),
        "gk_c": gain((NO, C_NOPE + C_ROPE)),
        "gq_d": gain((NO, D_HEAD)),
        "gk_d": gain((NO, D_HEAD)),
        "lam_q1": small((NO, D_HEAD), 0.1),
        "lam_k1": small((NO, D_HEAD), 0.1),
        "lam_q2": small((NO, D_HEAD), 0.1),
        "lam_k2": small((NO, D_HEAD), 0.1),
        "g_sub_d": gain((NO, D_V)),
        "w_out_o": w((NO, GATE_O, D_MODEL), GATE_O),
    }

def second_block(x, norm_e, w_in_e, gq_a, gk_a, rpb_a, gq_b, gk_b, w_out_e,
              norm_o, w_in_o, g_cq, w_cq_b, g_ckv, w_ckv_b, gq_c, gk_c, gq_d, gk_d,
              lam_q1, lam_k1, lam_q2, lam_k2, g_sub_d, w_out_o):
    S = x.shape[1]
    t = jnp.arange(S)
    pos = t.astype(jnp.float32)
    row = (t // GRID_W).astype(jnp.float32)
    col = (t % GRID_W).astype(jnp.float32)
    half = D_HEAD // 2
    ang_row = rope_angles(row, half, AXIAL_THETA)
    ang_col = rope_angles(col, half, AXIAL_THETA)
    ang_mla = rope_angles(pos, C_ROPE, MLA_THETA)
    ang_part = rope_angles(pos, ROT_DIM, ROPE_THETA_2)
    for l in range(DEPTH):
        i = l // 2
        if l % 2 == 0:
            x = x + even_layer(x, norm_e[i], w_in_e[i], gq_a[i], gk_a[i], rpb_a[i],
                               gq_b[i], gk_b[i], w_out_e[i], ang_row, ang_col)
        else:
            lam_init = 0.8 - 0.6 * math.exp(-0.3 * l)
            x = x + odd_layer(x, norm_o[i], w_in_o[i], g_cq[i], w_cq_b[i], g_ckv[i],
                              w_ckv_b[i], gq_c[i], gk_c[i], gq_d[i], gk_d[i],
                              lam_q1[i], lam_k1[i], lam_q2[i], lam_k2[i], g_sub_d[i],
                              w_out_o[i], ang_mla, ang_part, lam_init)
    return x


def setup_inputs(seed=0):
    out = dict(first_inputs(seed))
    for name, value in second_inputs(seed + 1).items():
        if name != "x":
            out[name + "_2"] = value
    return out


def reference(
    x, attn_norm, ffn_norm, final_norm, w_in_e, w_out_e, cmp_pe_k, cmp_pe_v, cmp_k_w1, cmp_k_w2,
    cmp_v_w1, cmp_v_w2, sinks, w_qkv_o, w_out_o, w_gate_up, w_down, norm_e_2, w_in_e_2, gq_a_2,
    gk_a_2, rpb_a_2, gq_b_2, gk_b_2, w_out_e_2, norm_o_2, w_in_o_2, g_cq_2, w_cq_b_2, g_ckv_2,
    w_ckv_b_2, gq_c_2, gk_c_2, gq_d_2, gk_d_2, lam_q1_2, lam_k1_2, lam_q2_2, lam_k2_2,
    g_sub_d_2, w_out_o_2,
):
    x = first_block(
        x, attn_norm, ffn_norm, final_norm, w_in_e, w_out_e, cmp_pe_k, cmp_pe_v, cmp_k_w1,
        cmp_k_w2, cmp_v_w1, cmp_v_w2, sinks, w_qkv_o, w_out_o, w_gate_up, w_down,
    )
    return second_block(
        x, norm_e_2, w_in_e_2, gq_a_2, gk_a_2, rpb_a_2, gq_b_2, gk_b_2, w_out_e_2, norm_o_2,
        w_in_o_2, g_cq_2, w_cq_b_2, g_ckv_2, w_ckv_b_2, gq_c_2, gk_c_2, gq_d_2, gk_d_2,
        lam_q1_2, lam_k1_2, lam_q2_2, lam_k2_2, g_sub_d_2, w_out_o_2,
    )


_drawn_inputs = setup_inputs


def setup_inputs(seed=0):
    import zlib

    import numpy as np

    out = dict(_drawn_inputs(seed))
    spreads = {}
    factors = {'attn_norm': 4.511,
     'final_norm': 2.747,
     'cmp_pe_k': 8.0,
     'cmp_pe_v': 7.512,
     'sinks': 6.771,
     'gq_a_2': 6.423,
     'gk_a_2': 6.609,
     'rpb_a_2': 3.394,
     'gq_b_2': 8.0,
     'gk_b_2': 8.0,
     'g_cq_2': 8.0,
     'g_ckv_2': 5.942,
     'gq_c_2': 8.0,
     'gk_c_2': 8.0,
     'gq_d_2': 13.576,
     'lam_q1_2': 36.768,
     'lam_k1_2': 64.0,
     'lam_q2_2': 2.699,
     'lam_k2_2': 37.957,
     'gk_d_2': 4.001,
     'g_sub_d_2': 8.0}
    for name, (base, spread) in spreads.items():
        noise = np.random.default_rng([zlib.crc32(name.encode()), seed]).standard_normal(out[name].shape)
        drawn = base * np.exp(spread * noise) if base else spread * noise
        out[name] = __import__('jax').numpy.asarray(drawn.astype(out[name].dtype))
    for name, factor in factors.items():
        out[name] = (out[name] * factor).astype(out[name].dtype)
    return out
```

```python
import numpy as np
import concourse.bass as bass
from concourse import mybir
from contextlib import ExitStack

F32 = mybir.dt.float32
ALU = mybir.AluOpType
ACT = mybir.ActivationFunctionType
AX = mybir.AxisListType

P = 128
T = 256
NT = T // P
D = 1024
KT = D // P
HD = 64
SCALE = HD ** -0.5
FFN = 2816
FT = FFN // P
NEG = -1.0e30
EPS_1, EPS_2 = 1e-5, 1e-6
MLA_D = 96
LAM_INIT = 0.8 - 0.6 * float(np.exp(-0.3))
CMP = T // 16 - 1
W0, WC, WM, WN = 2072, 3072, 3328, 2976

SLOT = KT * 512
RING = 4


def cut(width):
    return [(a, min(512, width - a)) for a in range(0, width, 512)]


def weight_chunks():
    out = [("w_in_e", c) for c in range(len(cut(W0)))]
    out += [("cmp_k_w1", 0), ("cmp_v_w1", 0)]
    out += [("w_out_e", 0), ("w_out_e", 1)]
    out += [("gu0", c) for c in range(FT // 2)] + [("down0", c) for c in range(6)]
    out += [("w_qkv_o", c) for c in range(6)] + [("w_out_o", 0), ("w_out_o", 1)]
    out += [("gu1", c) for c in range(FT // 2)] + [("down1", c) for c in range(6)]
    out += [("w_in_e_2", c) for c in range(len(cut(WM)))] + [("w_out_e_2", 0), ("w_out_e_2", 1)]
    out += [("w_in_o_2", c) for c in range(len(cut(WN)))] + [("lora", 0)]
    out += [("w_out_o_2", 0), ("w_out_o_2", 1)]
    return out


CHUNKS = weight_chunks()
CHUNK = {}
for _n, _c in enumerate(CHUNKS):
    CHUNK.setdefault(_c[0], _n)

DENSE, _d = {}, 0
for _name, _n in [("w_in_e", 5), ("w_out_e", 2), ("down0", 2), ("w_qkv_o", 6), ("w_out_o", 2), ("down1", 2),
                  ("w_in_e_2", 7), ("w_out_e_2", 2), ("w_in_o_2", 6), ("q_lora", 2), ("kv_lora", 2),
                  ("w_out_o_2", 2)]:
    DENSE[_name] = _d
    _d += _n

FILL, _f = {}, 0
for _name, _n in [("norm0", 4), ("prep0", 11), ("cmp_p", 1), ("attn0", 24), ("mix0", 4), ("norm1", 4),
                  ("norm2", 4), ("prep1", 8), ("attn1", 16), ("mix1", 4), ("norm3", 4),
                  ("norm5", 4), ("prep2", 7), ("attn2", 16), ("mix2", 4),
                  ("norm6", 4), ("lora", 2), ("prep3", 12), ("attn3", 16), ("mix3", 4)]:
    FILL[_name] = _f
    _f += _n

INST0 = {"attn0": 0, "attn1": 24, "attn2": 40, "attn3": 56}
GROUP0 = {"attn0": 0, "attn1": 6, "attn2": 10, "attn3": 14}
LAG = 2


def net(nc, a, out):
    ctx = ExitStack()
    sb = lambda name, shape: ctx.enter_context(nc.sbuf_tensor(name, shape, F32))
    sems = {}

    def sem(name):
        if name not in sems:
            sems[name] = ctx.enter_context(nc.semaphore(name))
        return sems[name]

    ring = sb("ring", [P, RING, SLOT])
    x = sb("x", [P, NT, D])
    hA = sb("hA", [P, NT, D])
    hT = sb("hT", [P, KT, T])
    z = sb("z", [P, NT, WM])
    reg = sb("reg", [P, 6144])
    extra = sb("extra", [P, 3584])
    tmp = sb("tmp", [P, 2048])
    va = sb("va", [P, 2112])
    prob = sb("prob", [P, 3, 512])
    probT = sb("probT", [P, 2, 512])
    silu_g = sb("silu_g", [P, 2, 256])
    gb = sb("gb", [P, D])
    masks = sb("masks", [P, 3, 384])
    cmask = sb("cmask", [P, NT, 16])
    ident = sb("ident", [P, P])
    rope = sb("rope", [P, NT, 2, HD])
    rope_ax = sb("rope_ax", [P, NT, 2, HD])
    rope_mla = sb("rope_mla", [P, NT, 2, 32])
    rope_part = sb("rope_part", [P, NT, 2, 16])
    gtab = sb("gtab", [P, NT, 4, HD])
    gains = sb("gains", [P, 1352])
    negm = sb("negm", [P, 72, 2])
    small = sb("small", [P, 640])
    w2 = sb("w2", [P, 2, 192])
    pe_sb = sb("pe_sb", [P, 2, 16])
    ps = ctx.enter_context(nc.psum_tensor("ps", [P, 8, 512], F32))
    TB, OB = 4, 6
    H1, KC, VC, CS = (3, 0), 3, 6, 1

    zc = lambda lo, hi: z[:, :, lo:hi]
    heads = lambda ap, w=HD: ap.rearrange("p t (h d) -> p t h d", d=w)
    regT = reg[:, :].rearrange("p (b t) -> p b t", t=T)
    hid = reg[:, 0:FT * T].rearrange("p (j t) -> p j t", t=T)
    kd = extra[:, 0:2560].rearrange("p (t h c d) -> p t h c d", t=NT, h=5 * 2, c=2)
    bias_na = extra[:, 0:8 * 6 * 64].rearrange("p (h u c) -> p h (u c)", h=8, u=6)
    bias_dst = extra[:, 0:8 * 6 * 64].rearrange("p (h u c) -> p h u c", h=8, u=6)
    lo_q = extra[:, 0:1536].rearrange("p (t n) -> p t n", t=NT)
    lo_kv = extra[:, 1536:3584].rearrange("p (t n) -> p t n", t=NT)
    tm = lambda h, w=HD: tmp[:, 0:NT * h * w].rearrange("p (t h d) -> p t h d", t=NT, h=h)
    bc = lambda ap, shape: ap.to_broadcast(shape)
    G = {"gq_a": (0, 64), "gk_a": (64, 64), "gq_b": (128, 64), "gk_b": (192, 64), "g_cq": (256, 256),
         "g_ckv": (512, 128), "gq_c": (640, 96), "gk_c": (736, 96), "gq_d": (832, 64), "gk_d": (896, 64),
         "g_sub_d": (960, 128)}
    gain = lambda n: gains[:, G[n][0]:G[n][0] + G[n][1]]
    sinks = gains[:, 1088:1096]
    lams = gains[:, 1096:1352].rearrange("p (a d) -> p a d", a=4)
    ss = small[:, 0:2]
    ms = small[:, 2:4]
    rstd = small[:, 4:6]
    halfs = small[:, 8:72]
    hss = small[:, 72:136]
    hrs = small[:, 136:200]
    gates = small[:, 200:248].rearrange("p (t h b) -> p t h b", t=NT, h=8)
    rden = small[:, 248:264]
    den = small[:, 264:280]
    esink = small[:, 280:296].rearrange("p (h t) -> p h t", t=NT)
    lam = small[:, 296:300]
    cm = small[:, 300:316]
    cden = small[:, 316:332]
    cfac = small[:, 332:348]
    cexp = small[:, 352:592]
    nsink = small[:, 592:600]
    ldot = small[:, 600:604]

    def bank(b, n=512):
        return ps[:, b, 0:n]

    bt = prob[:, 0:2, :]
    btv = tmp[:, 0:960].rearrange("p (s l u i) -> p s l u i", s=2, l=16, u=2)
    h1k = probT[:, 0, 0:60].rearrange("p (f n) -> p f n", f=2)
    h1v = prob[:, 0, 0:512].rearrange("p (f u h c) -> p f u h c", f=2, u=2, h=4)
    kcT = probT[:, 0, 64:94]
    vbd = prob[:, 1, 0:512].rearrange("p (u n) -> p u n", u=2)
    pcmp = prob[:, 2, 0:512].rearrange("p (u t h c) -> p u t h c", u=2, t=2, h=4)
    pcT = probT[:, 1, :].rearrange("p (u t q) -> p u t q", u=2, t=2)

    def flat(ap):
        return ap

    PREP = {
        "prep0": [("cmp", i) for i in range(4)] + [("qp", i) for i in range(4)]
        + [("qr", i) for i in range(4)] + [("ks", i) for i in range(2)] + [("kw", i) for i in range(2)]
        + [("bq", i) for i in range(4)] + [("bk", i) for i in range(2)],
        "prep1": [("q", i) for i in range(8)] + [("k", i) for i in range(8)],
        "prep2": [("qa", i) for i in range(4)] + [("ka", i) for i in range(4)] + [("qb", i) for i in range(4)]
        + [("kb", i) for i in range(2)],
        "prep3": [("qc", i) for i in range(8)] + [("kc", i) for i in range(8)] + [("qd", i) for i in range(4)]
        + [("kd", i) for i in range(4)],
    }

    def source(kind, i, t):
        at = lambda lo, w=128: z[:, t, lo + i * w:lo + (i + 1) * w]
        if kind == "cmp":
            return extra[:, t * 1280 + i * 128:t * 1280 + (i + 1) * 128]
        if kind in ("ks", "kw", "bk"):
            h = {"ks": 4, "kw": 6, "bk": 8}[kind] + i
            return extra[:, t * 1280 + h * 128:t * 1280 + (h + 1) * 128]
        if kind == "qr":
            return hA[:, t, i * 128:(i + 1) * 128]
        if kind == "kb":
            return extra[:, 3072 + (t * 2 + i) * 128:3072 + (t * 2 + i + 1) * 128]
        if kind == "qc":
            return lo_q[:, t, i * 96:(i + 1) * 96]
        if kind == "kc":
            return hA[:, t, i * 96:(i + 1) * 96]
        lo = {"qp": 0, "bq": 1304, "q": 0, "k": 1024, "qa": 0, "ka": 512, "qb": 1536, "qd": 416, "kd": 928}[kind]
        return at(lo)

    BLOCK = {s: {} for s in PREP}
    for _s, _l in PREP.items():
        for _k, (_kind, _i) in enumerate(_l):
            BLOCK[_s][_kind, _i] = _k

    def pair(stage, kind, h):
        lo = HD * (h % 2)
        return regT[lo:lo + HD, BLOCK[stage][kind, h // 2], :]

    def dup(stage, kind, h, like):
        lo = HD * (like % 2)
        return regT[lo:lo + HD, BLOCK[stage][kind, h], :]

    va65 = lambda n: va[:, 0:NT * n * 65].rearrange("p (t h d) -> p t h d", t=NT, h=n)
    va129 = va[:, 1040:1040 + NT * 4 * 129].rearrange("p (t h d) -> p t h d", t=NT, h=4)

    def bias_keys(h, t):
        row = bias_dst[:, h, 2 - 2 * t, 63:64]
        return bass.AP(row.tensor, row.offset, [row.ap[0], [64, 4], [-1, 64]])

    def instances(stage):
        out = []
        if stage == "attn0":
            v = va65(6)
            for u in range(2):
                for kk, vo in (("ks", 0), ("kw", 2)):
                    for h in range(4 * u, 4 * u + 4):
                        out.append((pair("prep0", "qr", h), dup("prep0", kk, u, h), lambda t: (masks[:, 0, :], 1),
                                    (v, vo + u), True))
            for h in range(8):
                out.append((pair("prep0", "bq", h), dup("prep0", "bk", h // 4, h), lambda t: (masks[:, 1, :], 1),
                            (v, 4 + h // 4), True))
        if stage == "attn1":
            v = va65(16)
            for h in range(16):
                out.append((pair("prep1", "q", h), pair("prep1", "k", h), lambda t: (masks[:, 2, :], 1),
                            (v, h), True))
        if stage == "attn2":
            v = va65(10)
            for h in range(8):
                out.append((pair("prep2", "qa", h), pair("prep2", "ka", h), lambda t, h=h: (bias_keys(h, t), 2),
                            (v, h), False))
            for h in range(8):
                out.append((pair("prep2", "qb", h), dup("prep2", "kb", h // 4, h), None, (v, 8 + h // 4), False))
        if stage == "attn3":
            v = va65(8)
            for h in range(8):
                out.append((regT[0:MLA_D, BLOCK["prep3"]["qc", h], :], regT[0:MLA_D, BLOCK["prep3"]["kc", h], :],
                            None, (v, h), False))
            for h in range(8):
                out.append((pair("prep3", "qd", h), pair("prep3", "kd", h), None, (va129, h // 2), False))
        return out

    INST = {s: instances(s) for s in INST0}

    def group_ends(stage):
        n, ends = len(INST[stage]), {}
        g, i = GROUP0[stage], 0
        while i < n:
            k = 2 if stage == "attn3" and i >= 8 else 4
            i += k
            ends[i - 1] = (g, k, 128 if k == 2 else 64)
            g += 1
        return ends

    ENDS = {s: group_ends(s) for s in INST0}

    def slot_of(stage, j):
        first = 0
        for e in sorted(ENDS[stage]):
            if j <= e:
                return j - first, j == first, ENDS[stage][e][0]
            first = e + 1

    slot_full = [sem(f"slot_full_{s}") for s in range(RING)]
    acc_ready = sem("acc_ready")
    acc_free = [sem("acc_free_0"), sem("acc_free_1")]
    t_filled = sem("t_filled")
    t_drained = [sem("t_drained_act"), sem("t_drained_dve")]
    scores_ready, max_ready, probs_ready = sem("scores_ready"), sem("max_ready"), sem("probs_ready")
    pv_done, out_taken = sem("pv_done"), sem("out_taken")
    up_ready, silu_ready, hid_ready = sem("up_ready"), sem("silu_ready"), sem("hid_ready")

    def chunk_view(n):
        name, c = CHUNKS[n]
        s = ring[:, n % RING, :]
        if name in ("cmp_k_w1", "cmp_v_w1"):
            return [(s[:, 0:4096].rearrange("p (l n) -> p l n", l=16),
                     a[name][0].rearrange("(l p) n -> p l n", p=P))]
        if name[:2] == "gu":
            w = a["w_gate_up"][int(name[2])].rearrange("(k p) n -> p k n", p=P)
            d = s[:, 0:4096].rearrange("p (g k n) -> p g k n", g=2, k=KT)
            return [(d[:, g], w[:, :, g * FFN + c * 256:g * FFN + c * 256 + 256]) for g in range(2)]
        if name[:4] == "down":
            k = 4 if c < 5 else 2
            w = a["w_down"][int(name[4])][c * 512:c * 512 + k * P].rearrange("(k p) n -> p k n", p=P)
            return [(s[:, 0:k * D].rearrange("p (k n) -> p k n", k=k), w)]
        if name == "lora":
            return [(s[:, 0:1536].rearrange("p (k n) -> p k n", k=2),
                     a["w_cq_b_2"][0].rearrange("(k p) n -> p k n", p=P)),
                    (s[:, 1536:2560], a["w_ckv_b_2"][0])]
        w = a[name][0].rearrange("(k p) n -> p k n", p=P)
        lo, n_ = cut(w.shape[2])[c]
        return [(s[:, 0:KT * n_].rearrange("p (k n) -> p k n", k=KT), w[:, :, lo:lo + n_])]

    def full_value(n):
        return 16 * sum(len(chunk_view(m)) for m in range(n % RING, n + 1, RING))

    FULL = [full_value(n) for n in range(len(CHUNKS))]
    NORM_G = [("attn_norm", 0), ("ffn_norm", 0), ("attn_norm", 1), ("ffn_norm", 1), ("final_norm", 0),
              ("norm_e_2", 0), ("norm_o_2", 0)]

    def read_by(n):
        name, c = CHUNKS[n]
        if name in ("cmp_k_w1", "cmp_v_w1"):
            return sem("h1k" if name == "cmp_k_w1" else "h1v"), 1
        if name[:2] == "gu":
            return up_ready, int(name[2]) * FT + 2 * c + 2
        if name[:4] == "down" and c < 5:
            return sem("down_step"), 5 * int(name[4]) + c + 1
        if name[:4] == "down":
            return acc_ready, 2 * DENSE[name] + 4
        if name == "lora":
            return acc_ready, 2 * DENSE["kv_lora"] + 4
        return acc_ready, 2 * (DENSE[name] + c) + 2

    def wait_taken(eng, name, count):
        for t in range(NT):
            eng.wait_ge(acc_free[t], DENSE[name] + count)

    block = ctx.enter_context(nc.Block())

    @block.sync
    def _(sp):
        sp.dma_start(x[:, :, :], a["x"][0].rearrange("(t p) n -> p t n", p=P)).then_inc(sem("x_in"), 16)
        for n in range(len(CHUNKS)):
            if n >= RING:
                sp.wait_ge(*read_by(n - RING))
            for dst, src in chunk_view(n):
                sp.dma_start(dst, src).then_inc(slot_full[n % RING], 16)
        sp.wait_ge(sem("x_final"), 1)
        sp.dma_start(out[0].rearrange("(t p) n -> p t n", p=P), x[:, :, :]).then_inc(sem("stored"), 16)
        sp.wait_ge(sem("stored"), 16)

    @block.gpsimd
    def _(pool):
        g = nc.gpsimd
        loads = [(ident[:, :], a["c_ident"]), (rope[:, :, :, :], a["c_rope"]), (masks[:, :, :], a["c_masks"]),
                 (cmask[:, :, :], a["c_cmask"]), (rope_ax[:, :, :, :], a["c_rope_ax"]),
                 (rope_mla[:, :, :, :], a["c_rope_mla"]), (rope_part[:, :, :, :], a["c_rope_part"]),
                 (pe_sb[:, 0, :], a["cmp_pe_k"]), (pe_sb[:, 1, :], a["cmp_pe_v"])]
        for s, name in ((0, "cmp_k_w2"), (1, "cmp_k_w2"), (2, "cmp_v_w2")):
            loads.append((w2[:, :, s * 64:s * 64 + 64], a[name][0].rearrange("(f p) n -> p f n", p=P)))
        for name in G:
            loads.append((gain(name), a[name + "_2"][0:1, :].partition_broadcast(P)))
        loads.append((sinks, a["sinks"][0:1, :].partition_broadcast(P)))
        for k, name in enumerate(("lam_q1_2", "lam_k1_2", "lam_q2_2", "lam_k2_2")):
            loads.append((lams[:, k, :], a[name][0:1, :].partition_broadcast(P)))
        g.memset(halfs, -0.5).then_inc(sem("halfs"), 1)
        g.memset(small[:, 352:592], 0.0).then_inc(sem("pool_chain"), 1)
        chain = [1]

        def link(ins):
            chain[0] += 1
            ins.then_inc(sem("pool_chain"), 1)
            pool.wait_ge(sem("pool_chain"), chain[0])

        link(g.memset(extra[:, :], 0.0))
        for dst, src in loads:
            pool.dma_start(dst, src).then_inc(sem("consts"), 16)
        pool.wait_ge(sem("consts"), 16 * len(loads))
        link(g.memset(prob[:, 0:3, :], 0.0))
        link(g.memset(va[:, :], 1.0))
        pool.sem_inc(sem("consts_ready"), 1)

        def power(name, o, i, n):
            pool.wait_ge(sem(name + "_ms"), 1)
            g.tensor_tensor(o, i, halfs[:, 0:n], ALU.pow).then_inc(sem(name + "_rstd"), 1)

        def values(name, pairs, wait):
            pool.wait_ge(sem(wait), 1)
            for k, (dst, src) in enumerate(pairs):
                ins = g.tensor_copy(dst, src)
            ins.then_inc(sem(name), 1)

        power("norm0", rstd, ms, 2)
        wait_taken(pool, "w_in_e", 5)
        for t in range(NT):
            src = z[:, t, 512:768].rearrange("p (h d) -> p h d", d=HD)
            for c in range(2):
                ins = g.tensor_copy(kd[:, t, 0:4, c, :], src)
        ins.then_inc(sem("cmp_dup"), 1)
        v = va65(6)
        for k, lo in enumerate((896, 1152, 1944)):
            for t in range(NT):
                ins = g.tensor_copy(v[:, t, 2 * k:2 * k + 2, 0:HD], z[:, t, lo:lo + 128].rearrange("p (h d) -> p h d", d=HD))
        ins.then_inc(sem("attn0_v"), 1)
        power("norm1", rstd, ms, 2)
        power("norm2", rstd, ms, 2)
        wait_taken(pool, "w_qkv_o", 6)
        link(g.memset(va[:, :], 1.0))
        v = va65(16)
        for t in range(NT):
            ins = g.tensor_copy(v[:, t, :, 0:HD], z[:, t, 2048:3072].rearrange("p (h d) -> p h d", d=HD))
        ins.then_inc(sem("attn1_v"), 1)
        power("norm3", rstd, ms, 2)
        pool.wait_ge(sem("norm3_ms"), 1)
        link(g.memset(extra[:, 0:3072], 0.0))
        rp = a["rpb_a_2"]
        for half in range(2):
            for u in range(6):
                dr = u - 2 - half
                if dr < -3 or dr > 3:
                    continue
                if True:
                    src = bass.AP(rp.tensor, rp.offset + (dr + 7) * 31 + 15 - 63, [[1, 64], [15 * 31, 8], [1, 64]])
                    pool.dma_start(bias_dst[64 * half:64 * half + 64, :, u, :], src).then_inc(sem("bias_in"), 16)
                    sems["n_bias"] = sems.get("n_bias", 0) + 16
        pool.wait_ge(sem("bias_in"), sems["n_bias"])
        for half in range(2):
            part = bias_dst[64 * half:64 * half + 64]
            for h in range(8):
                lo = part[:, h, :, 16:64]
                link(g.affine_select(out=lo, in_=lo, compare_op=ALU.is_ge, fill=NEG, base=8 + 47,
                                     pattern=[[0, 6], [-1, 48]], channel_multiplier=-1))
                hi = part[:, h, :, 0:48]
                link(g.affine_select(out=hi, in_=hi, compare_op=ALU.is_ge, fill=NEG, base=7 - 63,
                                     pattern=[[0, 6], [1, 48]], channel_multiplier=1))
        pool.sem_inc(sem("bias_ready"), 1)
        power("norm4", rstd, ms, 2)
        power("norm5", rstd, ms, 2)
        wait_taken(pool, "w_in_e_2", 7)
        link(g.memset(va[:, :], 1.0))
        v = va65(10)
        for t in range(NT):
            g.tensor_copy(v[:, t, 0:8, 0:HD], z[:, t, 1024:1536].rearrange("p (h d) -> p h d", d=HD))
            ins = g.tensor_copy(v[:, t, 8:10, 0:HD], z[:, t, 2176:2304].rearrange("p (h d) -> p h d", d=HD))
        ins.then_inc(sem("attn2_v"), 1)
        power("heads2", hrs[:, 0:52], hss[:, 0:52], 52)
        power("norm6", rstd, ms, 2)
        pool.wait_ge(sem("norm6_ms"), 1)
        link(g.memset(va[:, :], 1.0))
        power("lora", hrs[:, 0:4], hss[:, 0:4], 4)
        wait_taken(pool, "w_in_o_2", 6)
        for t in range(NT):
            ins = g.tensor_copy(va129[:, t, :, 0:128], z[:, t, 1440:1952].rearrange("p (h d) -> p h d", d=128))
        wait_taken(pool, "kv_lora", 2)
        v = va65(8)
        for t in range(NT):
            ins = g.tensor_copy(v[:, t, :, 0:HD], lo_kv[:, t, :].rearrange("p (h d) -> p h d", d=128)[:, :, 64:128])
        ins.then_inc(sem("attn3_v"), 1)
        power("mla", hrs[:, 0:32], hss[:, 0:32], 32)
        power("diff", hrs[:, 32:64], hss[:, 32:64], 32)
        power("od", hrs[:, 0:8], hss[:, 0:8], 8)

    @block.scalar
    def _(act):
        n = nc.scalar

        def load_gain(k):
            name, r = NORM_G[k]
            src = a[name][r:r + 1, :] if name != "final_norm" else a[name].rearrange("(o n) -> o n", o=1)
            if k:
                act.wait_ge(sem(f"norm{k - 1}_h"), 2)
            act.dma_start(gb[:, :], src.partition_broadcast(P)).then_inc(sem("gain_in"), 16)

        def drains(stage, count, dst_of):
            for k in range(count):
                f = FILL[stage] + k
                if f % 2 == 0:
                    act.wait_ge(t_filled, f + 1)
                    d = dst_of(k)
                    n.activation(d, ps[0:d.shape[0], TB + f % 2, 0:512], ACT.Copy).then_inc(t_drained[0], 1)

        def copy_out(name, dst, widths):
            for c, (lo, w) in enumerate(widths):
                d = DENSE[name] + c
                act.wait_ge(acc_ready, 2 * d + 1)
                ins = n.activation(dst[:, 0, lo:lo + w], ps[:, 2 * (d % 2), 0:w], ACT.Copy)
                ins.then_inc(acc_free[0], 1)

        def ffn(layer):
            for j in range(FT):
                g = layer * FT + j
                act.wait_ge(up_ready, g + 1)
                if g >= 2:
                    act.wait_ge(hid_ready, g - 1)
                n.activation(silu_g[:, g % 2, :], ps[:, g % 4, 0:256], ACT.Silu).then_inc(silu_ready, 1)

        def attention(stage, before_step=None):
            inst, i0, f0 = INST[stage], INST0[stage], FILL[stage]
            for s in range(len(inst) + LAG):
                if s < len(inst):
                    i = i0 + s
                    act.wait_ge(max_ready, i + 1)
                    if s >= 3:
                        act.wait_ge(t_filled, f0 + s - 2)
                    bk = i % 3
                    causal = inst[s][4]
                    w = 128 if causal else 256
                    n.activation(prob[:, i % 3, 0:w], ps[:, bk, 0:w], ACT.Exp, bias=negm[:, i, 0:1])
                    n.activation(prob[:, i % 3, 256:512], ps[:, bk, 256:512], ACT.Exp, bias=negm[:, i, 1:2])\
                     .then_inc(probs_ready, 1)
                    if stage == "attn0" and s in (19, 23):
                        act.wait_ge(sem("sink_shift"), (s - 15) // 4)
                        h = s - 19
                        n.activation(esink[:, h:h + 4, :], esink[:, h:h + 4, :], ACT.Exp).then_inc(sem("esink"), 1)
                j = s - LAG
                if j >= 0 and (f0 + j) % 2 == 0:
                    drain_probs(act, n.activation, stage, j, 0)

        def drain_probs(eng, op, stage, j, parity):
            i, f = INST0[stage] + j, FILL[stage] + j
            w = 384 if INST[stage][j][4] else 512
            eng.wait_ge(t_filled, f + 1)
            if j >= 2:
                eng.wait_ge(pv_done, i - 1)
            n.activation(probT[:, i % 2, 0:w], ps[:, TB + f % 2, 0:w], ACT.Copy).then_inc(t_drained[0], 1)

        def quad(base):
            return lambda k: base[:, 2 * k:2 * k + 2, :].rearrange("p b t -> p (b t)")

        load_gain(0)
        drains("norm0", 4, quad(hT))
        load_gain(1)
        copy_out("w_in_e", z, cut(W0))
        wait_taken(act, "w_in_e", 5)
        n.activation(small[:, 200:248].rearrange("p (t n) -> p t n", t=2), z[:, :, 1280:1304], ACT.Exp, scale=-1.0)\
         .then_inc(sem("gate_exp"), 1)
        drains("prep0", 11, quad(regT))
        act.wait_ge(sem("h1k"), 1)
        n.activation(h1k, ps[:, H1[0], 0:60].rearrange("p (f n) -> p f n", f=2), ACT.Silu).then_inc(sem("h1k_s"), 1)
        act.wait_ge(sem("h1v"), 1)
        act.wait_ge(sem("consts_ready"), 1)
        for f in range(2):
            for u in range(2):
                ins = n.activation(h1v[:, f, u, :, 0:CMP],
                                   bc(ps[:, H1[1], 30 * f + 15 * u:30 * f + 15 * u + 15].unsqueeze(1), [P, 4, CMP]),
                                   ACT.Silu)
        ins.then_inc(sem("h1v_s"), 1)
        act.wait_ge(sem("cmp_shift"), 1)
        n.activation(cexp, cexp, ACT.Exp).then_inc(sem("cmp_exp"), 1)
        drains("cmp_p", 1, lambda k: pcT.rearrange("p u t q -> p (u t q)"))
        attention("attn0")
        drains("mix0", 4, quad(hT))
        drains("norm1", 4, quad(hT))
        load_gain(2)
        ffn(0)
        drains("norm2", 4, quad(hT))
        load_gain(3)
        copy_out("w_qkv_o", z, cut(WC))
        drains("prep1", 8, quad(regT))
        attention("attn1")
        drains("mix1", 4, quad(hT))
        drains("norm3", 4, quad(hT))
        load_gain(4)
        ffn(1)
        load_gain(5)
        drains("norm5", 4, quad(hT))
        load_gain(6)
        copy_out("w_in_e_2", z, cut(WM))
        wait_taken(act, "w_in_e_2", 7)
        n.activation(z[:, :, 2304:3328], z[:, :, 2304:3328], ACT.Silu).then_inc(sem("gate2"), 1)
        drains("prep2", 7, quad(regT))
        attention("attn2")
        drains("mix2", 4, quad(hT))
        drains("norm6", 4, quad(hT))
        copy_out("w_in_o_2", z, cut(WN))
        wait_taken(act, "w_in_o_2", 6)
        n.activation(z[:, :, 1952:2976], z[:, :, 1952:2976], ACT.Silu).then_inc(sem("gate3"), 1)
        drains("lora", 2, quad(hT))
        copy_out("q_lora", lo_q, cut(768))
        copy_out("kv_lora", lo_kv, cut(1024))
        act.wait_ge(sem("lam_dots"), 1)
        n.activation(lam[:, 0:2], ldot[:, 0:2], ACT.Exp).then_inc(sem("lam_exp"), 1)
        drains("prep3", 8, lambda k: regT[0:MLA_D, 2 * k:2 * k + 2, :].rearrange("p b t -> p (b t)"))
        for k in range(8, 12):
            f = FILL["prep3"] + k
            if f % 2 == 0:
                act.wait_ge(t_filled, f + 1)
                n.activation(quad(regT)(k), ps[:, TB, 0:512], ACT.Copy).then_inc(t_drained[0], 1)
        attention("attn3")
        drains("mix3", 4, quad(hT))

    @block.vector
    def _(dve):
        v = nc.vector
        chain = [0]

        def link(ins):
            chain[0] += 1
            ins.then_inc(sem("dve_chain"), 1)
            dve.wait_ge(sem("dve_chain"), chain[0])

        def signal(ins, name, k=1):
            ins.then_inc(sem(name), 1)
            dve.wait_ge(sem(name), k)

        def norm(k, eps, transposed=True):
            for t in range(NT):
                link(v.tensor_tensor_reduce(out=tmp[:, 0:D], in0=x[:, t, :], in1=x[:, t, :], scale=1.0, scalar=0.0,
                                            op0=ALU.mult, op1=ALU.add, accum_out=ss[:, t:t + 1]))
            signal(v.tensor_scalar(ms, ss, 1.0 / D, eps, ALU.mult, ALU.add), f"norm{k}_ms")
            dve.wait_ge(sem(f"norm{k}_rstd"), 1)
            dve.wait_ge(sem("gain_in"), 16 * (k + 1))
            for t in range(NT):
                dst = hA[:, t, :] if transposed else x[:, t, :]
                signal(v.scalar_tensor_tensor(out=dst, in0=x[:, t, :], scalar=rstd[:, t:t + 1], in1=gb[:, :],
                                              op0=ALU.mult, op1=ALU.mult), f"norm{k}_h", t + 1)

        def drains(stage, count, dst_of, first=0):
            for k in range(first, count):
                f = FILL[stage] + k
                if f % 2:
                    dve.wait_ge(t_filled, f + 1)
                    d = dst_of(k)
                    v.tensor_copy(d, ps[0:d.shape[0], TB + f % 2, 0:512]).then_inc(t_drained[1], 1)

        def quad(base):
            return lambda k: base[:, 2 * k:2 * k + 2, :].rearrange("p b t -> p (b t)")

        def copy_out(name, dst, widths):
            for c, (lo, w) in enumerate(widths):
                d = DENSE[name] + c
                dve.wait_ge(acc_ready, 2 * d + 2)
                v.tensor_copy(dst[:, 1, lo:lo + w], ps[:, 2 * (d % 2) + 1, 0:w]).then_inc(acc_free[1], 1)

        def add_residual(name, halves=2):
            for c in range(2):
                d = DENSE[name] + c
                for t in range(NT):
                    dve.wait_ge(acc_ready, 2 * d + 1 + t)
                    v.tensor_tensor(x[:, t, c * 512:c * 512 + 512], x[:, t, c * 512:c * 512 + 512],
                                    ps[:, 2 * (d % 2) + t, :], ALU.add).then_inc(acc_free[t], 1)
            for t in range(NT):
                dve.wait_ge(acc_free[t], DENSE[name] + 2)

        def rotate(src, dst_list, table, H, half, width, swap_src=None):
            t_ = tm(H, width)
            cos, sin = table
            sh = [P, NT, H, half]
            link(v.tensor_tensor(t_[:, :, :, 0:half], src[:, :, :, half:2 * half],
                                 bc(sin[:, :, 0:half].unsqueeze(2), sh), ALU.mult))
            link(v.tensor_tensor(t_[:, :, :, half:2 * half], src[:, :, :, 0:half],
                                 bc(sin[:, :, half:2 * half].unsqueeze(2), sh), ALU.mult))
            full = [P, NT, H, 2 * half]
            first = dst_list[0]
            link(v.tensor_tensor(first, src[:, :, :, 0:2 * half], bc(cos.unsqueeze(2), full), ALU.mult))
            for dst in reversed(dst_list):
                link(v.tensor_tensor(dst, first, t_[:, :, :, 0:2 * half], ALU.add))

        def ffn(layer):
            for j in range(FT):
                g = layer * FT + j
                dve.wait_ge(silu_ready, g + 1)
                v.tensor_tensor(hid[:, j, :], silu_g[:, g % 2, :], ps[:, g % 4, 256:512], ALU.mult)\
                 .then_inc(hid_ready, 1)

        def attention(stage, after=None):
            inst, i0, f0, ends = INST[stage], INST0[stage], FILL[stage], ENDS[stage]
            for s in range(len(inst) + LAG + 1):
                if s < len(inst):
                    i = i0 + s
                    dve.wait_ge(scores_ready, i + 1)
                    w = 128 if inst[s][4] else 256
                    bk = i % 3
                    v.tensor_reduce(out=negm[:, i, 0:1], in_=ps[:, bk, 0:w], axis=AX.X, op=ALU.max, negate=True)
                    ins = v.tensor_reduce(out=negm[:, i, 1:2], in_=ps[:, bk, 256:512], axis=AX.X, op=ALU.max,
                                          negate=True)
                    if stage == "attn0" and s >= 16:
                        link(ins)
                        h = s - 16
                        ins = v.tensor_tensor(negm[:, i, :], negm[:, i, :], bc(nsink[:, h:h + 1], [P, 2]), ALU.min)
                    ins.then_inc(max_ready, 1)
                    if stage == "attn0" and s in (19, 23):
                        h = s - 19
                        dve.wait_ge(max_ready, i + 1)
                        v.tensor_tensor(esink[:, h:h + 4, :], negm[:, i - 3:i + 1, :],
                                        bc(sinks[:, h:h + 4].unsqueeze(2), [P, 4, 2]), ALU.add)\
                         .then_inc(sem("sink_shift"), 1)
                j = s - LAG
                if 0 <= j < len(inst) and (f0 + j) % 2:
                    f, i = f0 + j, i0 + j
                    w = 384 if inst[j][4] else 512
                    dve.wait_ge(t_filled, f + 1)
                    if j >= 2:
                        dve.wait_ge(pv_done, i - 1)
                    v.tensor_copy(probT[:, i % 2, 0:w], ps[:, TB + f % 2, 0:w]).then_inc(t_drained[1], 1)
                e = s - LAG - 1
                if e in ends:
                    take(stage, e, *ends[e])

        def take(stage, e, g, k, w):
            dve.wait_ge(pv_done, INST0[stage] + e + 1)
            o = ps[:, OB:OB + 2, 0:k * (w + 1)].rearrange("p t (s d) -> p t s d", s=k)
            r = rden[:, 0:2 * k].rearrange("p (t s) -> p t s", t=2)
            dn = den[:, 0:2 * k].rearrange("p (t s) -> p t s", t=2)
            sh = [P, NT, k, w]
            if stage == "attn0" and e >= 16:
                h0 = e - 16 - 3
                dve.wait_ge(sem("esink"), 1 + h0 // 4)
                link(v.tensor_tensor(dn, o[:, :, :, w], esink[:, h0:h0 + 4, :].rearrange("p h t -> p t h"), ALU.add))
                link(v.reciprocal(r, dn))
                dst = hA[:, :, 512 + h0 * 64:512 + h0 * 64 + 256]
                v.tensor_tensor(heads(dst), o[:, :, :, 0:w], bc(r.unsqueeze(3), sh), ALU.mult).then_inc(out_taken, 1)
                dve.wait_ge(out_taken, g + 1)
                return
            link(v.reciprocal(r, o[:, :, :, w]))
            if stage == "attn0":
                u, br = (e // 8), 1 + (e // 4) % 2
                link(v.tensor_tensor(r, r, gates[:, :, 4 * u:4 * u + 4, br], ALU.mult))
                dst = hA[:, :, u * 256:u * 256 + 256]
                t_ = tm(4)
                v.tensor_tensor(t_, o[:, :, :, 0:w], bc(r.unsqueeze(3), sh), ALU.mult).then_inc(out_taken, 1)
                dve.wait_ge(out_taken, g + 1)
                link(v.tensor_tensor(heads(dst), heads(dst), t_, ALU.add))
            elif k == 2:
                hh = (e - 8) // 2
                link(v.tensor_tensor(r[:, :, 1], r[:, :, 1], bc(lam[:, 2:3], [P, 2]), ALU.mult))
                t_ = tmp[:, 0:512].rearrange("p (t s d) -> p t s d", t=2, s=2)
                v.tensor_tensor(t_, o[:, :, :, 0:w], bc(r.unsqueeze(3), sh), ALU.mult).then_inc(out_taken, 1)
                dve.wait_ge(out_taken, g + 1)
                link(v.tensor_tensor(hA[:, :, 512 + hh * 128:640 + hh * 128], t_[:, :, 0, :], t_[:, :, 1, :],
                                     ALU.subtract))
            else:
                h0 = e - 3
                v.tensor_tensor(heads(hA[:, :, h0 * 64:h0 * 64 + 256]), o[:, :, :, 0:w], bc(r.unsqueeze(3), sh),
                                ALU.mult).then_inc(out_taken, 1)
                dve.wait_ge(out_taken, g + 1)

        def head_squares(src, ssq, H, w):
            link(v.tensor_tensor(tm(H, w), src, src, ALU.mult))
            link(v.tensor_reduce(out=ssq, in_=tm(H, w), axis=AX.X, op=ALU.add))

        dve.wait_ge(sem("x_in"), 16)
        dve.wait_ge(sem("halfs"), 1)
        norm(0, EPS_1)
        drains("norm0", 4, quad(hT))
        copy_out("w_in_e", z, cut(W0))
        wait_taken(dve, "w_in_e", 5)
        dve.wait_ge(sem("consts_ready"), 1)
        sinv = rope[:, :, 1, :]
        cosv = rope[:, :, 0, :]
        link(v.tensor_scalar(nsink, sinks, -1.0, None, ALU.mult))
        dve.wait_ge(sem("gate_exp"), 1)
        link(v.tensor_scalar(small[:, 200:248], small[:, 200:248], 1.0, None, ALU.add))
        link(v.reciprocal(small[:, 200:248], small[:, 200:248]))
        drains("prep0", 2, quad(regT))
        dve.wait_ge(t_drained[0], (FILL["prep0"] + 2 + 1) // 2)
        dve.wait_ge(t_drained[1], (FILL["prep0"] + 2) // 2)
        for s in range(2):
            for u in range(2):
                for l2 in range(2):
                    pr = slice(64 * l2, 64 * l2 + 64)
                    blk = regT[pr, BLOCK["prep0"]["cmp", 2 * s + u], :]
                    src = bass.AP(blk.tensor, blk.offset + l2, [blk.ap[0], [2, 16], [16, CMP]])
                    ins = v.tensor_tensor(btv[pr, s, :, u, :], src, bc(pe_sb[pr, s, :].unsqueeze(2), [64, 16, CMP]),
                                          ALU.add)
        signal(ins, "blocks")
        dve.wait_ge(sem("h1v"), 1)
        link(v.tensor_scalar(zc(0, 512), zc(0, 512), SCALE, None, ALU.mult))
        dve.sem_inc(sem("qp_ready"), 1)
        rotate(heads(zc(0, 512)), [heads(hA[:, :, 0:512])], (cosv, sinv), 8, 32, HD)
        rotate(heads(zc(768, 896)), [kd[:, :, 4:6, 0, :], kd[:, :, 4:6, 1, :]], (cosv, sinv), 2, 32, HD)
        rotate(heads(zc(1024, 1152)), [kd[:, :, 6:8, 0, :], kd[:, :, 6:8, 1, :]], (cosv, sinv), 2, 32, HD)
        link(v.tensor_scalar(zc(1304, 1816), zc(1304, 1816), SCALE, None, ALU.mult))
        rotate(heads(zc(1304, 1816)), [heads(zc(1304, 1816))], (cosv, sinv), 8, 32, HD)
        rotate(heads(zc(1816, 1944)), [kd[:, :, 8:10, 0, :], kd[:, :, 8:10, 1, :]], (cosv, sinv), 2, 32, HD)
        dve.sem_inc(sem("prep0_ready"), 1)
        drains("prep0", 11, quad(regT), first=2)
        dve.wait_ge(sem("kc"), 1)
        v.tensor_copy(kcT, ps[:, KC, 0:30]).then_inc(sem("kc_sb"), 1)
        dve.wait_ge(sem("vc"), 1)
        for u in range(2):
            for h in range(4):
                ins = v.tensor_copy(vbd[32 * h:32 * h + 32, u, 64 * h:64 * h + 64],
                                    ps[32 * h:32 * h + 32, VC, 64 * u:64 * u + 64])
        ins.then_inc(sem("vc_sb"), 1)
        dve.wait_ge(sem("cmp_scores"), 1)
        ce = cexp.rearrange("p (g c) -> p g c", c=CMP)
        for odd in range(2):
            sc = ps[:, CS + odd, 0:256].rearrange("p (u t h c) -> p u t h c", u=2, t=2, h=2)
            cs = cexp.rearrange("p (u t h o c) -> p u t h o c", u=2, t=2, h=2, o=2)
            for u in range(2):
                link(v.tensor_tensor(cs[:, u, :, :, odd, :], sc[:, u, :, :, 0:CMP],
                                     bc(cmask[:, :, 0:CMP].unsqueeze(2), [P, 2, 2, CMP]), ALU.add))
        link(v.tensor_reduce(out=cm, in_=ce, axis=AX.X, op=ALU.max))
        link(v.tensor_scalar(cm, cm, NEG / 2, None, ALU.max))
        signal(v.tensor_tensor(ce, ce, bc(cm.unsqueeze(2), [P, 16, CMP]), ALU.subtract), "cmp_shift")
        dve.wait_ge(sem("cmp_exp"), 1)
        link(v.tensor_reduce(out=cden, in_=ce, axis=AX.X, op=ALU.add))
        link(v.tensor_scalar(cden, cden, 1e-30, None, ALU.max))
        link(v.reciprocal(cfac, cden))
        for u in range(2):
            link(v.tensor_tensor(cfac[:, 8 * u:8 * u + 8].rearrange("p (t h) -> p t h", t=2),
                                 cfac[:, 8 * u:8 * u + 8].rearrange("p (t h) -> p t h", t=2),
                                 gates[:, :, 4 * u:4 * u + 4, 0], ALU.mult))
        signal(v.tensor_tensor(pcmp.rearrange("p u t h c -> p (u t h) c")[:, :, 0:CMP], ce,
                               bc(cfac.unsqueeze(2), [P, 16, CMP]), ALU.mult), "pcmp")
        drains("cmp_p", 1, lambda k: pcT.rearrange("p u t q -> p (u t q)"))
        dve.wait_ge(sem("cmp_out"), 1)
        v.tensor_copy(hA[:, :, 0:512], ps[:, OB:OB + 2, :]).then_inc(sem("cmp_taken"), 1)
        dve.wait_ge(sem("cmp_taken"), 1)
        attention("attn0")
        dve.sem_inc(sem("mix0_ready"), 1)
        drains("mix0", 4, quad(hT))
        add_residual("w_out_e")
        norm(1, EPS_1)
        drains("norm1", 4, quad(hT))
        ffn(0)
        add_residual("down0")
        norm(2, EPS_1)
        drains("norm2", 4, quad(hT))
        copy_out("w_qkv_o", z, cut(WC))
        wait_taken(dve, "w_qkv_o", 6)
        link(v.tensor_scalar(zc(0, 1024), zc(0, 1024), SCALE, None, ALU.mult))
        rotate(heads(zc(0, 1024)), [heads(zc(0, 1024))], (cosv, sinv), 16, 32, HD)
        rotate(heads(zc(1024, 2048)), [heads(zc(1024, 2048))], (cosv, sinv), 16, 32, HD)
        dve.sem_inc(sem("prep1_ready"), 1)
        drains("prep1", 8, quad(regT))
        attention("attn1")
        dve.sem_inc(sem("mix1_ready"), 1)
        drains("mix1", 4, quad(hT))
        add_residual("w_out_o")
        norm(3, EPS_1)
        drains("norm3", 4, quad(hT))
        ffn(1)
        add_residual("down1")
        norm(4, EPS_1, transposed=False)
        norm(5, EPS_2)
        drains("norm5", 4, quad(hT))
        copy_out("w_in_e_2", z, cut(WM))
        wait_taken(dve, "w_in_e_2", 7)
        h16, h10 = heads(zc(0, 1024)), heads(zc(1536, 2176))
        q1 = hss[:, 0:32].rearrange("p (t h) -> p t h", t=2)
        q2 = hss[:, 32:52].rearrange("p (t h) -> p t h", t=2)
        head_squares(h16, q1, 16, HD)
        head_squares(h10, q2, 10, HD)
        signal(v.tensor_scalar(hss[:, 0:52], hss[:, 0:52], 1.0 / HD, EPS_2, ALU.mult, ALU.add), "heads2_ms")
        def gain_tables(dst_c, dst_s, table, g, half, blocks, scale):
            w = 2 * half * blocks
            link(v.tensor_tensor(dst_c, table[:, :, 0, :], bc(g[:, 0:w].unsqueeze(1), [P, NT, w]), ALU.mult))
            for b in range(blocks):
                lo = b * 2 * half
                for s in range(2):
                    o, i = lo + s * half, lo + (1 - s) * half
                    link(v.tensor_tensor(dst_s[:, :, o:o + half], table[:, :, 1, o:o + half],
                                         bc(g[:, i:i + half].unsqueeze(1), [P, NT, half]), ALU.mult))
            if scale != 1.0:
                link(v.tensor_scalar(dst_c, dst_c, scale, None, ALU.mult))
                link(v.tensor_scalar(dst_s, dst_s, scale, None, ALU.mult))
        gain_tables(gtab[:, :, 0, :], gtab[:, :, 1, :], rope_ax, gain("gq_b"), 16, 2, SCALE)
        gain_tables(gtab[:, :, 2, :], gtab[:, :, 3, :], rope_ax, gain("gk_b"), 16, 2, 1.0)
        link(v.tensor_scalar(gain("gq_a"), gain("gq_a"), SCALE, None, ALU.mult))
        dve.wait_ge(sem("heads2_rstd"), 1)
        r1 = hrs[:, 0:32].rearrange("p (t h) -> p t h", t=2)
        r2 = hrs[:, 32:52].rearrange("p (t h) -> p t h", t=2)
        for t in range(NT):
            link(v.tensor_tensor(h16[:, t], h16[:, t], bc(r1[:, t].unsqueeze(2), [P, 16, HD]), ALU.mult))
            link(v.tensor_tensor(h16[:, t, 0:8], h16[:, t, 0:8], bc(gain("gq_a").unsqueeze(1), [P, 8, HD]), ALU.mult))
            link(v.tensor_tensor(h16[:, t, 8:16], h16[:, t, 8:16], bc(gain("gk_a").unsqueeze(1), [P, 8, HD]),
                                 ALU.mult))
            link(v.tensor_tensor(h10[:, t], h10[:, t], bc(r2[:, t].unsqueeze(2), [P, 10, HD]), ALU.mult))

        def rotate_axial(src, dst, table, H):
            cos, sin = table
            t_ = tm(H).rearrange("p t h (b c) -> p t h b c", b=4)
            s_ = src.rearrange("p t h (b c) -> p t h b c", b=4)
            for b in range(4):
                link(v.tensor_tensor(t_[:, :, :, b, :], s_[:, :, :, b ^ 1, :],
                                     bc(sin[:, :, 16 * b:16 * b + 16].unsqueeze(2), [P, NT, H, 16]), ALU.mult))
            link(v.tensor_tensor(src, src, bc(cos.unsqueeze(2), [P, NT, H, HD]), ALU.mult))
            for d_ in dst:
                link(v.tensor_tensor(d_, src, tm(H), ALU.add))
        rotate_axial(h10[:, :, 0:8], [h10[:, :, 0:8]], (gtab[:, :, 0, :], gtab[:, :, 1, :]), 8)
        kb_dup = extra[:, 3072:3584].rearrange("p (t h c d) -> p t h c d", t=2, h=2, c=2)
        rotate_axial(h10[:, :, 8:10], [kb_dup[:, :, :, 0, :], kb_dup[:, :, :, 1, :]],
                     (gtab[:, :, 2, :], gtab[:, :, 3, :]), 2)
        dve.sem_inc(sem("prep2_ready"), 1)
        drains("prep2", 7, quad(regT))
        attention("attn2")
        dve.wait_ge(sem("gate2"), 1)
        for t in range(NT):
            signal(v.tensor_tensor(hA[:, t, :], hA[:, t, :], z[:, t, 2304:3328], ALU.mult), "mix2_ready", t + 1)
        drains("mix2", 4, quad(hT))
        add_residual("w_out_e_2")
        norm(6, EPS_2)
        drains("norm6", 4, quad(hT))
        copy_out("w_in_o_2", z, cut(WN))
        wait_taken(dve, "w_in_o_2", 6)
        for t in range(NT):
            for k, (lo, w) in enumerate(((0, 256), (256, 128))):
                link(v.tensor_tensor_reduce(out=tmp[:, 0:w], in0=z[:, t, lo:lo + w], in1=z[:, t, lo:lo + w],
                                            scale=1.0 / w, scalar=0.0, op0=ALU.mult, op1=ALU.add,
                                            accum_out=hss[:, 2 * t + k:2 * t + k + 1]))
        signal(v.tensor_scalar(hss[:, 0:4], hss[:, 0:4], EPS_2, None, ALU.add), "lora_ms")
        dve.wait_ge(sem("lora_rstd"), 1)
        for t in range(NT):
            for k, (lo, w, gn) in enumerate(((0, 256, "g_cq"), (256, 128, "g_ckv"))):
                link(v.scalar_tensor_tensor(out=z[:, t, lo:lo + w], in0=z[:, t, lo:lo + w],
                                            scalar=hrs[:, 2 * t + k:2 * t + k + 1], in1=gain(gn),
                                            op0=ALU.mult, op1=ALU.mult))
        dve.sem_inc(sem("lora_ready"), 1)
        for k in range(2):
            f = FILL["lora"] + k
            if f % 2:
                dve.wait_ge(t_filled, f + 1)
                v.tensor_copy(quad(hT)(k), ps[:, TB + 1, :]).then_inc(t_drained[1], 1)
        for k in range(2):
            link(v.tensor_tensor_reduce(out=tmp[:, 0:HD], in0=lams[:, 2 * k, :], in1=lams[:, 2 * k + 1, :], scale=1.0,
                                        scalar=0.0, op0=ALU.mult, op1=ALU.add, accum_out=ldot[:, k:k + 1]))
        dve.sem_inc(sem("lam_dots"), 1)
        copy_out("q_lora", lo_q, cut(768))
        copy_out("kv_lora", lo_kv, cut(1024))
        wait_taken(dve, "q_lora", 2)
        wait_taken(dve, "kv_lora", 2)
        dve.wait_ge(sem("lam_exp"), 1)
        link(v.tensor_tensor(lam[:, 3:4], lam[:, 0:1], lam[:, 1:2], ALU.subtract))
        link(v.tensor_scalar(lam[:, 2:3], lam[:, 3:4], LAM_INIT, None, ALU.add))
        kcat = hA[:, :, 0:768].rearrange("p t (h d) -> p t h d", d=MLA_D)
        link(v.tensor_copy(kcat[:, :, :, 0:64], lo_kv.rearrange("p t (h d) -> p t h d", d=128)[:, :, :, 0:64]))
        link(v.tensor_copy(kcat[:, :, :, 64:96], bc(z[:, :, 384:416].unsqueeze(2), [P, NT, 8, 32])))
        qh = heads(lo_q, MLA_D)
        q1 = hss[:, 0:16].rearrange("p (t h) -> p t h", t=2)
        q2 = hss[:, 16:32].rearrange("p (t h) -> p t h", t=2)
        head_squares(qh, q1, 8, MLA_D)
        head_squares(kcat, q2, 8, MLA_D)
        signal(v.tensor_scalar(hss[:, 0:32], hss[:, 0:32], 1.0 / MLA_D, EPS_2, ALU.mult, ALU.add), "mla_ms")
        qd_, kd_ = heads(zc(416, 928)), heads(zc(928, 1440))
        head_squares(heads(zc(416, 1440)), hss[:, 32:64].rearrange("p (t h) -> p t h", t=2), 16, HD)
        signal(v.tensor_scalar(hss[:, 32:64], hss[:, 32:64], 1.0 / HD, EPS_2, ALU.mult, ALU.add), "diff_ms")
        dve.wait_ge(sem("mla_rstd"), 1)
        link(v.tensor_scalar(gain("gq_c"), gain("gq_c"), float(MLA_D) ** -0.5, None, ALU.mult))
        link(v.tensor_scalar(gain("gq_d"), gain("gq_d"), SCALE, None, ALU.mult))
        link(v.tensor_scalar(gain("g_sub_d"), gain("g_sub_d"), 1.0 - LAM_INIT, None, ALU.mult))
        for src, ro, gn in ((qh, 0, "gq_c"), (kcat, 16, "gk_c")):
            r_ = hrs[:, ro:ro + 16].rearrange("p (t h) -> p t h", t=2)
            for t in range(NT):
                link(v.tensor_tensor(src[:, t], src[:, t], bc(r_[:, t].unsqueeze(2), [P, 8, MLA_D]), ALU.mult))
                link(v.tensor_tensor(src[:, t], src[:, t], bc(gain(gn).unsqueeze(1), [P, 8, MLA_D]), ALU.mult))
            part = src[:, :, :, 64:96]
            rotate(part, [part], (rope_mla[:, :, 0, :], rope_mla[:, :, 1, :]), 8, 16, 32)
        dve.wait_ge(sem("diff_rstd"), 1)
        allh = heads(zc(416, 1440))
        r_ = hrs[:, 32:64].rearrange("p (t h) -> p t h", t=2)
        for t in range(NT):
            link(v.tensor_tensor(allh[:, t], allh[:, t], bc(r_[:, t].unsqueeze(2), [P, 16, HD]), ALU.mult))
            link(v.tensor_tensor(qd_[:, t], qd_[:, t], bc(gain("gq_d").unsqueeze(1), [P, 8, HD]), ALU.mult))
            link(v.tensor_tensor(kd_[:, t], kd_[:, t], bc(gain("gk_d").unsqueeze(1), [P, 8, HD]), ALU.mult))
        part = allh[:, :, :, 0:16]
        rotate(part, [part], (rope_part[:, :, 0, :], rope_part[:, :, 1, :]), 16, 8, 16)
        dve.sem_inc(sem("prep3_ready"), 1)
        for k in range(12):
            f = FILL["prep3"] + k
            if f % 2:
                np_ = MLA_D if k < 8 else P
                dve.wait_ge(t_filled, f + 1)
                v.tensor_copy(regT[0:np_, 2 * k:2 * k + 2, :].rearrange("p b t -> p (b t)"),
                              ps[0:np_, TB + 1, :]).then_inc(t_drained[1], 1)
        attention("attn3")
        od = hA[:, :, 512:1024].rearrange("p t (h d) -> p t h d", d=128)
        head_squares(od, hss[:, 0:8].rearrange("p (t h) -> p t h", t=2), 4, 128)
        signal(v.tensor_scalar(hss[:, 0:8], hss[:, 0:8], 1.0 / 128, EPS_2, ALU.mult, ALU.add), "od_ms")
        dve.wait_ge(sem("od_rstd"), 1)
        r_ = hrs[:, 0:8].rearrange("p (t h) -> p t h", t=2)
        dve.wait_ge(sem("gate3"), 1)
        for t in range(NT):
            link(v.tensor_tensor(od[:, t], od[:, t], bc(r_[:, t].unsqueeze(2), [P, 4, 128]), ALU.mult))
            link(v.tensor_tensor(od[:, t], od[:, t], bc(gain("g_sub_d").unsqueeze(1), [P, 4, 128]), ALU.mult))
            signal(v.tensor_tensor(hA[:, t, :], hA[:, t, :], z[:, t, 1952:2976], ALU.mult), "mix3_ready", t + 1)
        drains("mix3", 4, quad(hT))
        add_residual("w_out_o_2")
        dve.sem_inc(sem("x_final"), 1)

    @block.tensor
    def _(pe):
        m = nc.tensor

        def open_fill(f):
            if f >= 2:
                pe.wait_ge(t_drained[f % 2], f // 2)

        def drained(f):
            pe.wait_ge(t_drained[0], (f + 2) // 2)
            if f >= 1:
                pe.wait_ge(t_drained[1], (f + 1) // 2)

        def transposes(stage, blocks, first=0, to=None):
            for k in range(first, to if to is not None else (len(blocks) + 1) // 2):
                f = FILL[stage] + k
                open_fill(f)
                for b, blk in enumerate(blocks[2 * k:2 * k + 2]):
                    for t in range(NT):
                        src = blk(t)
                        w = src.shape[1]
                        ins = m.transpose(ps[0:w, TB + f % 2, b * T + t * P:b * T + t * P + P], src, ident[:, :])
                ins.then_inc(t_filled, 1)

        def hA_blocks():
            return [lambda t, k=k: hA[:, t, k * P:(k + 1) * P] for k in range(KT)]

        def use_chunk(n):
            pe.wait_ge(slot_full[n % RING], FULL[n])

        def dense(name, chunks, widths, kts, lhs, wview):
            for c, (lo, w) in enumerate(widths):
                d = DENSE[name] + c
                if chunks:
                    use_chunk(CHUNK[name] + c)
                for t in range(NT):
                    if d >= 2:
                        pe.wait_ge(acc_free[t], d - 1)
                    for k in range(kts):
                        ins = m.matmul(ps[:, 2 * (d % 2) + t, 0:w], lhs[:, k, t * P:(t + 1) * P], wview(c, k, lo, w),
                                       start=k == 0, stop=k == kts - 1)
                    ins.then_inc(acc_ready, 1)

        def ring_view(n, w):
            return ring[:, n % RING, 0:KT * w].rearrange("p (k n) -> p k n", k=KT)

        def project(name, width):
            dense(name, True, cut(width), KT, hT,
                  lambda c, k, lo, w: ring_view(CHUNK[name] + c, w)[:, k, :])

        def ffn(layer):
            base = CHUNK[f"gu{layer}"]
            for j in range(FT):
                g = layer * FT + j
                nchunk = base + j // 2
                if j % 2 == 0:
                    use_chunk(nchunk)
                if j >= 4:
                    pe.wait_ge(hid_ready, g - 3)
                w = ring[:, nchunk % RING, :].rearrange("p (g k n) -> p g k n", g=2, k=KT)
                for gate in range(2):
                    for k in range(KT):
                        ins = m.matmul(ps[:, g % 4, 256 * gate:256 * gate + 256],
                                       w[:, gate, k, (j % 2) * P:(j % 2) * P + P], hT[:, k, :],
                                       start=k == 0, stop=k == KT - 1)
                ins.then_inc(up_ready, 1)
            d = DENSE[f"down{layer}"]
            pe.wait_ge(hid_ready, (layer + 1) * FT)
            for c in range(6):
                nchunk = CHUNK[f"down{layer}"] + c
                use_chunk(nchunk)
                ks = 4 if c < 5 else 2
                w = ring[:, nchunk % RING, 0:ks * D].rearrange("p (k n) -> p k n", k=ks)
                for half in range(2):
                    for t in range(NT):
                        for k in range(ks):
                            kk = 4 * c + k
                            ins = m.matmul(ps[:, 2 * ((d + half) % 2) + t, :], hid[:, kk, t * P:(t + 1) * P],
                                           w[:, k, half * 512:half * 512 + 512], start=kk == 0, stop=kk == FT - 1)
                        if c == 5:
                            ins.then_inc(acc_ready, 1)
                if c < 5:
                    ins.then_inc(sem("down_step"), 1)

        def attention(stage):
            inst, i0, f0, ends = INST[stage], INST0[stage], FILL[stage], ENDS[stage]
            pe.wait_ge(sem(stage + "_v"), 1)
            for s in range(len(inst) + LAG + 1):
                if s < len(inst):
                    i = i0 + s
                    q, k, bias, _, causal = inst[s]
                    if s >= 3:
                        pe.wait_ge(probs_ready, i - 2)
                    for t in range(NT):
                        w = P * (t + 1) if causal else T
                        o = ps[:, i % 3, 256 * t:256 * t + w]
                        if bias is not None:
                            bt_, kind = bias(t)
                            if kind == 1:
                                bt_ = bt_[:, P * t:P * t + w]
                            m.matmul(o, ident[:, :], bt_, start=True, stop=False)
                        ins = m.matmul(o, q[:, t * P:(t + 1) * P], k[:, 0:w], start=bias is None, stop=True)
                    ins.then_inc(scores_ready, 1)
                j = s - LAG
                if 0 <= j < len(inst):
                    i, f = i0 + j, f0 + j
                    causal = inst[j][4]
                    pe.wait_ge(probs_ready, i + 1)
                    open_fill(f)
                    for kt in range(NT):
                        for t in range(NT):
                            if causal and kt > t:
                                continue
                            col = {(0, 0): 0, (0, 1): 128, (1, 1): 256}[kt, t] if causal else kt * 256 + t * 128
                            ins = m.transpose(ps[:, TB + f % 2, col:col + P],
                                              prob[:, i % 3, 256 * t + kt * P:256 * t + kt * P + P], ident[:, :])
                    ins.then_inc(t_filled, 1)
                j = s - LAG - 1
                if 0 <= j < len(inst):
                    i, f = i0 + j, f0 + j
                    slot, first, g = slot_of(stage, j)
                    causal = inst[j][4]
                    vt, vh = inst[j][3]
                    w = vt.shape[3]
                    pe.wait_ge(t_drained[f % 2], f // 2 + 1)
                    if first and g > 0:
                        pe.wait_ge(out_taken, g)
                    for t in range(NT):
                        kts = [0] if causal and t == 0 else [0, 1]
                        for kt in kts:
                            col = {(0, 0): 0, (0, 1): 128, (1, 1): 256}[kt, t] if causal else kt * 256 + t * 128
                            ins = m.matmul(ps[:, OB + t, slot * w:slot * w + w], probT[:, i % 2, col:col + P],
                                           vt[:, kt, vh, :], start=kt == 0, stop=kt == kts[-1])
                    ins.then_inc(pv_done, 1)

        def from_norm(k, stage):
            pe.wait_ge(sem(f"norm{k}_h"), 2)
            transposes(stage, hA_blocks())
            drained(FILL[stage] + 3)

        def prep_blocks(stage):
            return [lambda t, kind=kind, i=i: source(kind, i, t) for kind, i in PREP[stage]]

        def mix(stage, k, need=1):
            pe.wait_ge(sem(f"mix{k}_ready"), need)
            transposes(stage, hA_blocks())
            drained(FILL[stage] + 3)

        pe.wait_ge(sem("consts_ready"), 1)
        from_norm(0, "norm0")
        project("w_in_e", W0)
        pe.wait_ge(sem("cmp_dup"), 1)
        transposes("prep0", prep_blocks("prep0"), 0, 2)
        pe.wait_ge(sem("blocks"), 1)
        for s, name in enumerate(("cmp_k_w1", "cmp_v_w1")):
            n_ = CHUNK[name]
            use_chunk(n_)
            w1 = ring[:, n_ % RING, :].rearrange("p (l n) -> p l n", l=16)
            for f in range(2):
                for l in range(16):
                    ins = m.matmul(ps[:, H1[s], 30 * f:30 * f + 30], w1[:, l, f * P:(f + 1) * P],
                                   btv[:, s, l, :, :], start=l == 0, stop=l == 15)
            ins.then_inc(sem("h1k" if s == 0 else "h1v"), 1)
        pe.wait_ge(sem("qp_ready"), 1)
        pe.wait_ge(sem("prep0_ready"), 1)
        transposes("prep0", prep_blocks("prep0"), 2)
        pe.wait_ge(sem("h1k_s"), 1)
        for f in range(2):
            ins = m.matmul(ps[:, KC, 0:30], w2[:, f, 0:128], h1k[:, f, :], start=f == 0, stop=f == 1)
        ins.then_inc(sem("kc"), 1)
        pe.wait_ge(sem("h1v_s"), 1)
        for u in range(2):
            for f in range(2):
                ins = m.matmul(ps[:, VC, 64 * u:64 * u + 64],
                               h1v[:, f, u, :, :].rearrange("p h c -> p (h c)"), w2[:, f, 128:192],
                               start=f == 0, stop=f == 1)
        ins.then_inc(sem("vc"), 1)
        drained(FILL["prep0"] + 10)
        pe.wait_ge(sem("kc_sb"), 1)
        for u in range(2):
            for t in range(NT):
                for h in range(4):
                    hh = 4 * u + h
                    q = pair("prep0", "qp", hh)
                    lo = HD * (hh % 2)
                    col = ((u * 2 + t) * 2 + h // 2) * 32
                    ins = m.matmul(ps[:, CS + h % 2, col:col + CMP], q[:, t * P:(t + 1) * P],
                                   kcT[lo:lo + HD, u * CMP:(u + 1) * CMP], start=True, stop=True)
        ins.then_inc(sem("cmp_scores"), 1)
        pe.wait_ge(sem("pcmp"), 1)
        f = FILL["cmp_p"]
        open_fill(f)
        for u in range(2):
            for t in range(NT):
                ins = m.transpose(ps[:, TB + f % 2, (2 * u + t) * P:(2 * u + t + 1) * P],
                                  pcmp[:, u, t, :, :].rearrange("p h c -> p (h c)"), ident[:, :])
        ins.then_inc(t_filled, 1)
        drained(f)
        pe.wait_ge(sem("vc_sb"), 1)
        for u in range(2):
            for t in range(NT):
                ins = m.matmul(ps[:, OB + t, 256 * u:256 * u + 256], pcT[:, u, t, :], vbd[:, u, :], start=True,
                               stop=True)
        ins.then_inc(sem("cmp_out"), 1)
        pe.wait_ge(sem("cmp_taken"), 1)
        attention("attn0")
        mix("mix0", 0)
        project("w_out_e", D)
        from_norm(1, "norm1")
        ffn(0)
        from_norm(2, "norm2")
        project("w_qkv_o", WC)
        pe.wait_ge(sem("prep1_ready"), 1)
        transposes("prep1", prep_blocks("prep1"))
        drained(FILL["prep1"] + 7)
        attention("attn1")
        mix("mix1", 1)
        project("w_out_o", D)
        from_norm(3, "norm3")
        ffn(1)
        from_norm(5, "norm5")
        project("w_in_e_2", WM)
        pe.wait_ge(sem("prep2_ready"), 1)
        transposes("prep2", prep_blocks("prep2"))
        drained(FILL["prep2"] + 6)
        pe.wait_ge(sem("bias_ready"), 1)
        attention("attn2")
        mix("mix2", 2, 2)
        project("w_out_e_2", D)
        from_norm(6, "norm6")
        project("w_in_o_2", WN)
        pe.wait_ge(sem("lora_ready"), 1)
        for k in range(2):
            f = FILL["lora"] + k
            open_fill(f)
            for b in range(2):
                for t in range(NT):
                    c = min(2 * k + b, 2)
                    ins = m.transpose(ps[:, TB + f % 2, b * T + t * P:b * T + t * P + P],
                                      z[:, t, c * P:(c + 1) * P], ident[:, :])
            ins.then_inc(t_filled, 1)
        drained(FILL["lora"] + 1)
        n_ = CHUNK["lora"]
        use_chunk(n_)
        s_ = ring[:, n_ % RING, :]
        wq = s_[:, 0:1536].rearrange("p (k n) -> p k n", k=2)
        dense("q_lora", False, cut(768), 2, hT, lambda c, k, lo, w: wq[:, k, lo:lo + w])
        dense("kv_lora", False, cut(1024), 1, hT[:, 2:3, :], lambda c, k, lo, w: s_[:, 1536 + lo:1536 + lo + w])
        pe.wait_ge(sem("prep3_ready"), 1)
        transposes("prep3", prep_blocks("prep3"))
        drained(FILL["prep3"] + 11)
        attention("attn3")
        mix("mix3", 3, 2)
        project("w_out_o_2", D)

    ctx.close()


def rotation(angles, signs):
    t = np.stack([np.cos(angles), np.sin(angles) * signs], axis=1).astype(np.float32)
    return np.ascontiguousarray(t.reshape(NT, P, 2, -1).transpose(1, 0, 2, 3))


def tables():
    f = np.float32
    pos = np.arange(T, dtype=f)

    def freqs(dim, theta):
        return (1.0 / (f(theta) ** (np.arange(0, dim, 2, dtype=f) / f(dim)))).astype(f)

    def turned(p, dim, theta):
        a = (p[:, None] * freqs(dim, theta)[None, :]).astype(f)
        return np.concatenate([a, a], 1), np.concatenate([-np.ones(dim // 2, f), np.ones(dim // 2, f)])

    out = {"c_ident": np.eye(P, dtype=f), "c_rope": rotation(*turned(pos, HD, 10000.0))}
    row, col = np.floor(pos / 64), pos % 64
    ar, sg = turned(row.astype(f), 32, 10000.0)
    ac, _ = turned(col.astype(f), 32, 10000.0)
    out["c_rope_ax"] = rotation(np.concatenate([ar, ac], 1), np.concatenate([sg, sg]))
    out["c_rope_mla"] = rotation(*turned(pos, 32, 10000.0))
    out["c_rope_part"] = rotation(*turned(pos, 16, 500000.0))
    i, j = np.arange(T)[:, None], np.arange(T)[None, :]
    causal = np.where(j <= i, 0.0, NEG)
    window = np.where((j <= i) & (i - j < 128), 0.0, NEG)
    count = (i - j <= 128).astype(int) + ((i - j) % 4 == 0) + ((i - j) % 16 == 0)
    dilated = np.where((j <= i) & (count > 0), np.log(np.maximum(count, 1)), NEG)
    m = [np.concatenate([b[0:P, 0:P], b[P:T, :]], axis=1) for b in (causal, window, dilated)]
    out["c_masks"] = np.ascontiguousarray(np.stack(m, axis=1).astype(f))
    c = np.arange(16)[None, :]
    cm = np.where((c * 16 + 31 <= i) & (c < CMP), 0.0, NEG).astype(f)
    out["c_cmask"] = np.ascontiguousarray(cm.reshape(NT, P, 16).transpose(1, 0, 2))
    return out


def kernel(**inputs):
    import concourse.bacc as _bacc
    from concourse.bass_utils import run_bass_kernel_spmd as _run

    arrays = {}
    for name, value in inputs.items():
        v = np.ascontiguousarray(value)
        if name == "rpb_a_2":
            v = np.ascontiguousarray(v[..., ::-1])
        if name in ("cmp_pe_k", "cmp_pe_v"):
            v = np.ascontiguousarray(v.reshape(16, P).T)
        arrays[name] = v
    arrays.update(tables())
    nc = _bacc.Bacc("TRN2", target_bir_lowering=False, num_devices=1)
    aps = {name: nc.dram_tensor("in_" + name, v.shape, F32, kind="ExternalInput").ap() for name, v in arrays.items()}
    out = nc.dram_tensor("out_0", (1, T, D), F32, kind="ExternalOutput").ap()
    net(nc, aps, out)
    r = _run(nc, [{"in_" + name: v for name, v in arrays.items()}], core_ids=[0])
    return r.results[0]["out_0"]
```

```python
import numpy as np
import concourse.bass as bass
from concourse import mybir
from contextlib import ExitStack

F32 = mybir.dt.float32
F32R = mybir.dt.float32r
BF16 = mybir.dt.bfloat16
ALU = mybir.AluOpType
ACT = mybir.ActivationFunctionType
AX = mybir.AxisListType

P = 128
T = 256
NT = T // P
D = 1024
KT = D // P
HD = 64
SCALE = HD ** -0.5
FFN = 2816
FT = FFN // P
NEG = -1.0e30
EPS_1, EPS_2 = 1e-5, 1e-6
MLA_D = 96
LAM_INIT = 0.8 - 0.6 * float(np.exp(-0.3))
CMP = T // 16 - 1

UNIT = 1024
RING = 8
AHEAD = 4


def cut(lo, hi):
    return [(a, min(512, hi - a)) for a in range(lo, hi, 512)]


COLS = {
    "w_in_e": (cut(0, 2072), []),
    "w_out_e": (cut(0, D), []),
    "w_qkv_o": (cut(0, 3072), []),
    "w_out_o": (cut(0, D), []),
    "w_in_e_2": (cut(0, 2304), cut(2304, 3328)),
    "w_out_e_2": (cut(0, D), []),
    "w_in_o_2": ([(0, 416), (416, 512), (928, 512), (1440, 512)], cut(1952, 2976)),
    "w_out_o_2": (cut(0, D), []),
}


def stream():
    out = []

    def chunk(name, c, tiles, width):
        per = max(k for k in (1, 2, 4, 8) if k * width <= UNIT and tiles % k == 0)
        for k in range(0, tiles, per):
            out.append((name, c, k, per, width))

    def projection(name, which=None):
        tok, feat = COLS[name]
        for c, (_, w) in enumerate(tok + feat):
            if which is None or c in which:
                chunk(name, c, KT, w)

    def ffn(layer):
        for c in range(FT // 2):
            chunk(f"gu{layer}", c, KT, 512)
        for c in range(FT):
            chunk(f"down{layer}", c, 1, D)

    projection("w_in_e")
    chunk("cmp_k_w1", 0, 16, 256)
    chunk("cmp_v_w1", 0, 16, 256)
    projection("w_out_e")
    ffn(0)
    projection("w_qkv_o")
    projection("w_out_o")
    ffn(1)
    projection("w_in_e_2")
    projection("w_out_e_2")
    projection("w_in_o_2", (0, 1, 2))
    chunk("w_cq_b_2", 0, 2, 768)
    chunk("w_ckv_b_2", 0, 1, D)
    projection("w_in_o_2", (3, 4, 5))
    projection("w_out_o_2")
    return out


UNITS = stream()
FIRST, LAST = {}, {}
for _n, _u in enumerate(UNITS):
    FIRST.setdefault(_u[:2], _n)
    LAST[_u[:2]] = _n + 1

DENSE, _d = {}, 0
for _name, _n in [("w_in_e", 5), ("w_out_e", 2), ("down0", 2), ("w_qkv_o", 6), ("w_out_o", 2), ("down1", 2),
                  ("w_in_e_2", 5), ("gate_e", 4), ("w_out_e_2", 2), ("w_in_o_2", 3), ("w_cq_b_2", 2),
                  ("w_ckv_b_2", 2), ("w_in_o_2b", 1), ("gate_o", 4), ("w_out_o_2", 2)]:
    DENSE[_name] = _d
    _d += _n

FILL, _f = {}, 0
for _name, _n in [("norm0", 4), ("prep0", 11), ("cmp_p", 1), ("attn0", 24), ("norm1", 4), ("norm2", 4),
                  ("prep1", 8), ("attn1", 16), ("norm3", 4), ("norm5", 4), ("prep2", 7), ("attn2", 16),
                  ("norm6", 4), ("lora", 2), ("prep3", 12), ("attn3", 16)]:
    FILL[_name] = _f
    _f += _n
NORM_HI = {"norm0": 0, "norm1": 4, "norm2": 8, "norm3": 12, "norm5": 16, "norm6": 20}

STAGES = ("attn0", "attn1", "attn2", "attn3")
INST0 = {"attn0": 0, "attn1": 24, "attn2": 40, "attn3": 56}
PAIR0 = {"attn0": 0, "attn1": 8, "attn2": 16, "attn3": 24}
LAG = 2

TAB, _c = {}, 0
for _name, _n in [("ident", 128), ("masks", 1152), ("cmask", 32), ("rope", 256), ("rope_q", 256), ("rope_ax", 256),
                  ("rope_mla", 128), ("rope_part", 64)]:
    TAB[_name] = (_c, _n)
    _c += _n
TABLE_COLS = _c
GAIN, _c = {}, 0
for _name, _n in [("gq_a_2", 64), ("gk_a_2", 64), ("gq_b_2", 64), ("gk_b_2", 64), ("g_cq_2", 256), ("g_ckv_2", 128),
                  ("gq_c_2", 96), ("gk_c_2", 96), ("gq_d_2", 64), ("gk_d_2", 64), ("sinks", 8), ("lam_q1_2", 64),
                  ("lam_k1_2", 64), ("lam_q2_2", 64), ("lam_k2_2", 64)]:
    GAIN[_name] = (_c, _n)
    _c += _n
GAIN_COLS = _c


def net(nc, a, out):
    ctx = ExitStack()
    sems = {}

    def sem(name):
        if name not in sems:
            sems[name] = ctx.enter_context(nc.semaphore(name))
        return sems[name]

    BASE = 16896
    cursor = [BASE]

    def place(name, shape, dtype=F32, at=None):
        size = 2 if dtype == BF16 else 4
        for n in shape[1:]:
            size *= n
        where = cursor[0] if at is None else at
        t = nc.alloc_sbuf_tensor_at(name, shape, dtype, offset=where)
        if at is None:
            cursor[0] = where + (size + 31) // 32 * 32
        return t

    x = place("x", [P, NT, D])
    hT_hi = place("hT_hi", [P, KT, T], F32R)
    hT_lo = place("hT_lo", [P, KT, T], F32R)
    w_hi = place("w_hi", [P, RING, UNIT], F32R)
    w_at = cursor[0]
    w_raw = place("w_raw", [P, RING, UNIT])
    w_lo = place("w_lo", [P, RING, UNIT], F32R, at=w_at)
    table = place("table", [P, TABLE_COLS])
    gains = place("gains", [P, GAIN_COLS])
    gtab = place("gtab", [P, NT, 4, HD])
    gb = place("gb", [P, D])
    negm = place("negm", [P, 72, 2])
    den = place("den", [P, 72, 2])
    fac = place("fac", [P, 72, 2])
    small = place("small", [P, 736])
    w2 = place("w2", [P, 2, 192])
    pe_sb = place("pe_sb", [P, 2, 16])
    gsub = place("gsub", [P, 1])
    mask_b = place("mask_b", [P, 2, 384], BF16)
    ident_b = place("ident_b", [P, P], BF16)
    ident_r = place("ident_r", [P, P], F32R)
    logc = place("logc", [P, 2, 384], F32R)
    phase_at = cursor[0]
    z = place("z", [P, 6656])
    hA = place("hA", [P, NT, D])
    tmp = place("tmp", [P, 1536])
    extra = place("extra", [P, 3584])
    reg = place("reg", [P, 24, T])
    prob_at = cursor[0]
    prob = place("prob", [P, 3, 512])
    probT = place("probT", [P, 2, 512])
    assert cursor[0] <= 229368, cursor[0]
    hid_hi = place("hid_hi", [P, FT, T], F32R, at=phase_at)
    hid_lo = place("hid_lo", [P, FT, T], F32R, at=phase_at + 4 * FT * T)
    silu_g = place("silu_g", [P, 2, T], at=phase_at + 8 * FT * T)
    hid32 = place("hid32", [P, 2, T], at=phase_at + 8 * FT * T + 2048)
    bt_hi = place("bt_hi", [P, 2, 16, 2 * CMP], F32R, at=prob_at)
    bt_lo = place("bt_lo", [P, 2, 16, 2 * CMP], F32R, at=prob_at + 3840)
    lr_hi = place("lr_hi", [P, 4, T], F32R, at=prob_at)
    lr_lo = place("lr_lo", [P, 4, T], F32R, at=prob_at + 4096)
    ps = ctx.enter_context(nc.psum_tensor("ps", [P, 8, 512], F32))
    TB, OB, SUM = 4, 6, 3

    tab = lambda n: table[:, TAB[n][0]:TAB[n][0] + TAB[n][1]]
    ident = tab("ident")
    rt = lambda n, w: tab(n).rearrange("p (t s d) -> p t s d", t=NT, s=2, d=w)
    rope, rope_q, rope_ax = rt("rope", HD), rt("rope_q", HD), rt("rope_ax", HD)
    rope_mla, rope_part = rt("rope_mla", 32), rt("rope_part", 16)
    cmask = tab("cmask").rearrange("p (t c) -> p t c", t=NT)
    masks = tab("masks").rearrange("p (m c) -> p m c", m=3)
    gain = lambda n: gains[:, GAIN[n][0]:GAIN[n][0] + GAIN[n][1]]
    sinks = gain("sinks")
    zw = lambda w: z[:, 0:NT * w].rearrange("p (t n) -> p t n", t=NT)
    z0, z1, z2, z3 = zw(2072), zw(3072), zw(2304), zw(1952)
    gT = z[:, 4608:6656].rearrange("p (k t) -> p k t", k=KT)
    heads = lambda ap, w=HD: ap.rearrange("p t (h d) -> p t h d", d=w)
    kd = extra[:, 0:2560].rearrange("p (t h c d) -> p t h c d", t=NT, h=10, c=2)
    pcmp = extra[:, 2560:3072].rearrange("p (u t h c) -> p u t h c", u=2, t=2, h=4)
    pcT = extra[:, 3072:3584].rearrange("p (u q) -> p u q", u=2)
    bias_na = extra[:, 0:3072].rearrange("p (h u c) -> p h u c", h=8, u=6)
    kb_dup = extra[:, 3072:3584].rearrange("p (t h c d) -> p t h c d", t=2, h=2, c=2)
    lo_q = extra[:, 0:1536].rearrange("p (t n) -> p t n", t=NT)
    lo_kv = extra[:, 1536:3584].rearrange("p (t n) -> p t n", t=NT)
    kcat = hA[:, :, 0:768].rearrange("p t (h d) -> p t h d", d=MLA_D)
    h1v = hA[:, 0, 512:1024].rearrange("p (f u h c) -> p f u h c", f=2, u=2, h=4)
    vbd = hA[:, 1, 512:1024].rearrange("p (u n) -> p u n", u=2)
    od = z[:, 0:1024].rearrange("p (h t) -> p h t", h=4)
    ones = extra[:, 0:P]
    gain_final = prob[:, 0:2, :].rearrange("p b n -> p (b n)")
    tm = lambda h, w=HD: tmp[:, 0:NT * h * w].rearrange("p (t h d) -> p t h d", t=NT, h=h)
    tmp_heads = lambda ap: tm(ap.shape[2], ap.shape[3])
    bc = lambda ap, shape: ap.to_broadcast(shape)
    ss, ms, rstd = small[:, 0:2], small[:, 2:4], small[:, 4:6]
    halfs = small[:, 8:72]
    hss, hrs = small[:, 72:136], small[:, 136:200]
    gates = small[:, 200:248].rearrange("p (t h b) -> p t h b", t=NT, h=8)
    esink = small[:, 280:296].rearrange("p (h t) -> p h t", t=NT)
    lam = small[:, 296:300]
    cm, cden, cfac = small[:, 300:316], small[:, 316:332], small[:, 332:348]
    cexp = small[:, 352:592]
    nsink, ldot = small[:, 592:600], small[:, 600:602]
    h1k = small[:, 604:664].rearrange("p (f n) -> p f n", f=2)
    kcT = small[:, 664:694]
    H1, KC, VC, CS = ((2, 3), (0, 1)), 6, 7, 0

    slot_full = [sem(f"slot_full_{s}") for s in range(RING)]
    hi_ready, lo_ready = sem("hi_ready"), sem("lo_ready")
    units_used = sem("units_used")
    acc_free = [sem("acc_free_0"), sem("acc_free_1")]
    t_filled = sem("t_filled")
    t_drained = [sem("t_drained_even"), sem("t_drained_odd")]
    t_hi = sem("t_hi")
    scores_ready, max_ready, exp_ready = sem("scores_ready"), sem("max_ready"), sem("exp_ready")
    probs_ready, pv_done = sem("probs_ready"), sem("pv_done")
    mix_prod, mix_hi, mix_lo = sem("mix_prod"), sem("mix_hi"), sem("mix_lo")
    even_up, silu_ready, hid_ready = sem("even_up"), sem("silu_ready"), sem("hid_ready")
    hid32_ready, hid_hi_ready = sem("hid32_ready"), sem("hid_hi_ready")

    def unit_parts(n):
        name, c, k0, ks, w = UNITS[n]
        s = w_raw[:, n % RING, 0:ks * w].rearrange("p (k n) -> p k n", k=ks)
        rows = slice(k0 * P, (k0 + ks) * P)
        if name[:2] == "gu":
            src = a["w_gate_up"][int(name[2])][rows].rearrange("(k p) n -> p k n", p=P)
            return [(s[:, :, 256 * g:256 * g + 256], src[:, :, g * FFN + c * 256:g * FFN + c * 256 + 256])
                    for g in range(2)]
        if name[:4] == "down":
            return [(s, a["w_down"][int(name[4])][c * P:c * P + P].rearrange("(k p) n -> p k n", p=P))]
        src = a[name][0][rows].rearrange("(k p) n -> p k n", p=P)
        if name in COLS:
            lo = (COLS[name][0] + COLS[name][1])[c][0]
            src = src[:, :, lo:lo + w]
        return [(s, src)]

    LANDED = []
    for n in range(len(UNITS)):
        LANDED.append((LANDED[n - RING] if n >= RING else 0) + 16 * len(unit_parts(n)))

    def halves(n):
        _, _, _, ks, w = UNITS[n]
        return tuple(t[:, n % RING, 0:ks * w].rearrange("p (k n) -> p k n", k=ks) for t in (w_hi, w_lo))

    PREP = {
        "prep0": [("qp", i) for i in range(4)] + [("qr", i) for i in range(4)] + [("cmp", i) for i in range(4)]
        + [("ks", i) for i in range(2)] + [("kw", i) for i in range(2)] + [("bq", i) for i in range(4)]
        + [("bk", i) for i in range(2)],
        "prep1": [("q", i) for i in range(8)] + [("k", i) for i in range(8)],
        "prep2": [("qa", i) for i in range(4)] + [("ka", i) for i in range(4)] + [("qb", i) for i in range(4)]
        + [("kb", i) for i in range(2)],
        "prep3": [("qd", i) for i in range(4)] + [("kd", i) for i in range(4)]
        + [("qc", i) for i in range(8)] + [("kc", i) for i in range(8)],
    }
    BLOCK = {s: {key: n for n, key in enumerate(blocks)} for s, blocks in PREP.items()}

    def source(kind, i, t):
        if kind in ("cmp", "ks", "kw", "bk"):
            h = {"cmp": 0, "ks": 4, "kw": 6, "bk": 8}[kind] + i
            return extra[:, t * 1280 + h * P:t * 1280 + (h + 1) * P]
        if kind == "kb":
            return extra[:, 3072 + (t * 2 + i) * P:3072 + (t * 2 + i + 1) * P]
        w, buf, lo = {"qp": (P, z0, 0), "qr": (P, hA, 0), "bq": (P, z0, 1304), "q": (P, z1, 0), "k": (P, z1, 1024),
                      "qa": (P, z2, 0), "ka": (P, z2, 512), "qb": (P, z2, 1536), "qd": (P, z3, 416),
                      "kd": (P, z3, 928), "qc": (MLA_D, lo_q, 0), "kc": (MLA_D, hA, 0)}[kind]
        return buf[:, t, lo + i * w:lo + (i + 1) * w]

    def pair_row(stage, kind, h):
        lo = HD * (h % 2)
        return reg[lo:lo + HD, BLOCK[stage][kind, h // 2], :]

    def dup_row(stage, kind, h, like):
        lo = HD * (like % 2)
        return reg[lo:lo + HD, BLOCK[stage][kind, h], :]

    def mask_passes(m):
        return lambda t: [(ident_b[:, :], mask_b[:, m, P * t:P * t + P * (t + 1)])]

    def count_passes(t):
        return [(ident_r[:, :], logc[:, part, P * t:P * t + P * (t + 1)]) for part in range(2)]

    def bias_passes(h):
        def f(t):
            row = bias_na[:, h, 2 - 2 * t, 63:64]
            return [(ident, bass.AP(row.tensor, row.offset, [row.ap[0], [64, 4], [-1, 64]]))]
        return f

    def instances(stage):
        out = []
        if stage == "attn0":
            for h in range(8):
                for br, (kk, vlo) in enumerate((("ks", 896), ("kw", 1152))):
                    out.append(dict(q=pair_row("prep0", "qr", h), k=dup_row("prep0", kk, h // 4, h),
                                    bias=mask_passes(0), v=(z0, vlo + HD * (h // 4), HD), causal=True, half=h % 2,
                                    pair=h // 2, first=False, last=br == 1, gate=(h, br + 1)))
            for h in range(8):
                out.append(dict(q=pair_row("prep0", "bq", h), k=dup_row("prep0", "bk", h // 4, h),
                                bias=mask_passes(1), v=(z0, 1944 + HD * (h // 4), HD), causal=True, half=h % 2,
                                pair=4 + h // 2, first=True, last=True, sink=h))
        if stage == "attn1":
            for h in range(16):
                out.append(dict(q=pair_row("prep1", "q", h), k=pair_row("prep1", "k", h), bias=count_passes,
                                v=(z1, 2048 + HD * h, HD), causal=True, half=h % 2, pair=h // 2, first=True,
                                last=True))
        if stage == "attn2":
            for h in range(8):
                out.append(dict(q=pair_row("prep2", "qa", h), k=pair_row("prep2", "ka", h), bias=bias_passes(h),
                                v=(z2, 1024 + HD * h, HD), causal=False, half=h % 2, pair=h // 2, first=True,
                                last=True))
            for h in range(8):
                out.append(dict(q=pair_row("prep2", "qb", h), k=dup_row("prep2", "kb", h // 4, h), bias=None,
                                v=(z2, 2176 + HD * (h // 4), HD), causal=False, half=h % 2, pair=4 + h // 2,
                                first=True, last=True))
        if stage == "attn3":
            for h in range(8):
                out.append(dict(q=pair_row("prep3", "qd", h), k=pair_row("prep3", "kd", h), bias=None,
                                v=(z3, 1440 + P * (h // 2), P), causal=False, half=0, pair=h // 2,
                                first=h % 2 == 0, last=h % 2 == 1, lam=h % 2 == 1))
            for h in range(8):
                out.append(dict(q=reg[0:MLA_D, BLOCK["prep3"]["qc", h], :], k=reg[0:MLA_D, BLOCK["prep3"]["kc", h], :],
                                bias=None, v=(lo_kv, P * h + HD, HD), causal=False, half=h % 2, pair=4 + h // 2,
                                first=True, last=True))
        return out

    INST = {s: instances(s) for s in STAGES}
    for s in STAGES:
        for n, i in enumerate(INST[s]):
            i["opens"] = n == 0 or INST[s][n - 1]["pair"] != i["pair"]
            i["ends"] = n + 1 == len(INST[s]) or INST[s][n + 1]["pair"] != i["pair"]

    def inst_pair(stage, e):
        return PAIR0[stage] + INST[stage][e]["pair"]

    def prods(stage, p):
        return p - PAIR0["attn2"] + 1 if stage == "attn2" else 8 + p - PAIR0["attn3"] - 3

    def lows(p):
        return p + 1 if p < 24 else p - 3

    def mix_tile(stage, p):
        k = p - PAIR0[stage]
        return k if stage != "attn3" else (k + 4) % 8

    def bank_taken(p):
        return (mix_hi, p + 1) if 24 <= p < 28 else (mix_lo, lows(p))

    def column(kt, t, causal):
        if causal:
            return {(0, 0): 0, (0, 1): P, (1, 1): 2 * P}[kt, t]
        return kt * T + t * P

    def next_units(stage):
        return FIRST[{"attn0": "w_out_e", "attn1": "w_out_o", "attn2": "w_out_e_2", "attn3": "w_out_o_2"}[stage], 0]

    NORM_G = [("attn_norm", 0), ("ffn_norm", 0), ("attn_norm", 1), ("ffn_norm", 1), ("final_norm", 0),
              ("norm_e_2", 0), ("norm_o_2", 0)]

    def norm_dst(stage):
        def f(buf, k):
            t, k4 = k // 2, 4 * (k % 2)
            return buf[:, k4:k4 + 4, t * P:(t + 1) * P]
        return f

    block = ctx.enter_context(nc.Block())

    @block.sync
    def _(sp):
        sp.dma_start(x[:, :, :], a["x"][0].rearrange("(t p) n -> p t n", p=P)).then_inc(sem("x_in"), 16)
        for n in range(len(UNITS)):
            if n >= RING:
                sp.wait_ge(units_used, n - RING + 1)
            for dst, src in unit_parts(n):
                sp.dma_start(dst, src).then_inc(slot_full[n % RING], 16)
        sp.wait_ge(sem("x_final"), 1)
        sp.dma_start(out[0].rearrange("(t p) n -> p t n", p=P), x[:, :, :]).then_inc(sem("stored"), 16)
        sp.wait_ge(sem("stored"), 16)

    @block.gpsimd
    def _(pool):
        g = nc.gpsimd
        chain = [0]

        def link(ins):
            chain[0] += 1
            ins.then_inc(sem("pool_chain"), 1)
            pool.wait_ge(sem("pool_chain"), chain[0])

        def power(name, o, i, n):
            pool.wait_ge(sem(name + "_ms"), 1)
            g.tensor_tensor(o, i, halfs[:, 0:n], ALU.pow).then_inc(sem(name + "_rstd"), 1)

        link(g.memset(halfs, -0.5))
        power("norm0", rstd, ms, 2)
        g.memset(extra[:, 2560:3072], 0.0).then_inc(sem("zeros"), 1)
        pool.wait_ge(sem("norm0_used"), 1)
        g.memset(hA[:, :, 512:1024], 0.0).then_inc(sem("zeros"), 1)
        for t in range(NT):
            pool.wait_ge(acc_free[t], DENSE["w_in_e"] + 2)
            src = z0[:, t, 512:768].rearrange("p (h d) -> p h d", d=HD)
            for c in range(2):
                ins = g.tensor_copy(kd[:, t, 0:4, c, :], src)
        ins.then_inc(sem("cmp_dup"), 1)
        power("norm1", rstd, ms, 2)
        power("norm2", rstd, ms, 2)
        power("norm3", rstd, ms, 2)
        power("norm4", rstd, ms, 2)
        power("norm5", rstd, ms, 2)
        rp = a["rpb_a_2"]
        n_bias = 0
        for half in range(2):
            for u in range(6):
                dr = u - 2 - half
                src = bass.AP(rp.tensor, rp.offset + (dr + 7) * 31 + 15 - 63, [[1, 64], [15 * 31, 8], [1, 64]])
                pool.dma_start(bias_na[64 * half:64 * half + 64, :, u, :], src).then_inc(sem("bias_in"), 16)
                n_bias += 16
        pool.wait_ge(sem("bias_in"), n_bias)
        for half in range(2):
            for h in range(8):
                part = bias_na[64 * half:64 * half + 64, h]
                lo = part[:, :, 16:64]
                link(g.affine_select(out=lo, in_=lo, compare_op=ALU.is_ge, fill=NEG, base=8 + 47,
                                     pattern=[[0, 6], [-1, 48]], channel_multiplier=-1))
                hi = part[:, :, 0:48]
                link(g.affine_select(out=hi, in_=hi, compare_op=ALU.is_ge, fill=NEG, base=7 - 63,
                                     pattern=[[0, 6], [1, 48]], channel_multiplier=1))
        pool.sem_inc(sem("bias_ready"), 1)
        power("qa", hrs[:, 0:16], hss[:, 0:16], 16)
        power("ka", hrs[:, 16:32], hss[:, 16:32], 16)
        power("qb", hrs[:, 32:48], hss[:, 32:48], 16)
        power("kb", hrs[:, 48:52], hss[:, 48:52], 4)
        power("norm6", rstd, ms, 2)
        power("lora", hrs[:, 0:4], hss[:, 0:4], 4)
        power("qd", hrs[:, 4:20], hss[:, 4:20], 16)
        power("kd", hrs[:, 20:36], hss[:, 20:36], 16)
        power("mla", hrs[:, 0:32], hss[:, 0:32], 32)

    @block.scalar
    def _(act):
        n = nc.scalar
        split_to = [0]

        def split(upto):
            for u in range(split_to[0], min(upto, len(UNITS))):
                act.wait_ge(slot_full[u % RING], LANDED[u])
                if u >= RING:
                    act.wait_ge(units_used, u - RING + 1)
                size = UNITS[u][3] * UNITS[u][4]
                n.activation(w_hi[:, u % RING, 0:size], w_raw[:, u % RING, 0:size], ACT.Copy).then_inc(hi_ready, 1)
            split_to[0] = max(split_to[0], min(upto, len(UNITS)))

        def load_gain(k, wait, dst=None):
            name, r = NORM_G[k]
            src = a[name][r:r + 1, :] if name != "final_norm" else a[name].rearrange("(o n) -> o n", o=1)
            if wait is not None:
                act.wait_ge(sem(f"norm{wait}_h"), 2)
            act.dma_start(gb[:, :] if dst is None else dst, src.partition_broadcast(P))\
               .then_inc(sem(f"gain{k}_in"), 16)

        def square_sum(k):
            act.wait_ge(sem(f"norm{k}_x"), 1)
            n.activation(hA[:, 0, :], x[:, 0, :], ACT.Square, accum_out=ss[:, 0:1]).then_inc(sem(f"norm{k}_ss"), 1)

        def norm_high(stage):
            for k in range(4):
                f = FILL[stage] + k
                act.wait_ge(t_filled, f + 1)
                n.activation(norm_dst(stage)(hT_hi, k), ps[:, TB + f % 2, :].rearrange("p (b t) -> p b t", b=4),
                             ACT.Copy).then_inc(t_hi, 1)

        def drain(stage, fills):
            for k in fills:
                f = FILL[stage] + k
                if f % 2 == 0:
                    act.wait_ge(t_filled, f + 1)
                    rows = MLA_D if stage == "prep3" and k >= 4 else P
                    n.activation(reg[0:rows, 2 * k:2 * k + 2, :].rearrange("p b t -> p (b t)"),
                                 ps[0:rows, TB, :], ACT.Copy).then_inc(t_drained[0], 1)

        def take(name, c, dst, dense=None, done=None):
            d = DENSE[name] + c if dense is None else dense
            act.wait_ge(units_used, done)
            lo, w = dst[1:]
            n.activation(dst[0][:, 0, lo:lo + w], ps[:, 2 * (d % 2), 0:w], ACT.Copy).then_inc(acc_free[0], 1)

        def chunk(name, c, buf):
            done = LAST[name, c]
            split(done + AHEAD)
            take(name, c, (buf, *COLS[name][0][c]), done=done)

        def gate_chunks(name, which, dense):
            for g, c in enumerate(which):
                done = LAST[name, c]
                split(done + AHEAD)
                act.wait_ge(units_used, done)
                for b in range(4):
                    d = dense + 2 * g + b // 2
                    n.activation(gT[:, 4 * g + b, :], ps[:, 2 * (d % 2) + b % 2, 0:T], ACT.Silu)\
                     .then_inc(acc_free[b % 2], 1)

        def ffn(layer):
            for j in range(FT):
                g = layer * FT + j
                done = LAST[f"gu{layer}", j // 2]
                if j % 2 == 0:
                    split(done + AHEAD)
                    act.wait_ge(even_up, layer * FT // 2 + j // 2 + 1)
                else:
                    act.wait_ge(units_used, done)
                if g >= 2:
                    act.wait_ge(hid32_ready, g - 1)
                n.activation(silu_g[:, g % 2, :], ps[:, g % 4, 0:T], ACT.Silu).then_inc(silu_ready, 1)
                act.wait_ge(hid32_ready, g + 1)
                n.activation(hid_hi[:, j, :], hid32[:, g % 2, :], ACT.Copy).then_inc(hid_hi_ready, 1)
            for j in range(FT):
                split(LAST[f"down{layer}", j] + AHEAD)

        def attention(stage):
            inst, i0, f0 = INST[stage], INST0[stage], FILL[stage]
            base = next_units(stage)
            for s in range(len(inst) + LAG + 4):
                if s < len(inst):
                    i, it = i0 + s, inst[s]
                    act.wait_ge(max_ready, i + 1)
                    if s >= 3:
                        act.wait_ge(t_filled, f0 + s - 2)
                    w = P if it["causal"] else T
                    n.activation(prob[:, i % 3, 0:w], ps[:, i % 3, 0:w], ACT.Exp, bias=negm[:, i, 0:1],
                                 accum_out=den[:, i, 0:1])
                    n.activation(prob[:, i % 3, 256:512], ps[:, i % 3, 256:512], ACT.Exp, bias=negm[:, i, 1:2],
                                 accum_out=den[:, i, 1:2]).then_inc(exp_ready, 1)
                    if "sink" in it:
                        h = it["sink"]
                        act.wait_ge(sem("sink_shift"), h + 1)
                        n.activation(esink[:, h, :], esink[:, h, :], ACT.Exp).then_inc(sem("esink"), 1)
                j = s - LAG
                if 0 <= j < len(inst) and (f0 + j) % 2 == 0:
                    i, f = i0 + j, f0 + j
                    w = 384 if inst[j]["causal"] else 512
                    act.wait_ge(t_filled, f + 1)
                    if j >= 2:
                        act.wait_ge(pv_done, i - 1)
                    n.activation(probT[:, i % 2, 0:w], ps[:, TB, 0:w], ACT.Copy).then_inc(t_drained[0], 1)
                e = s - LAG - 3
                if e >= 0 and e < len(inst) and inst[e]["ends"]:
                    mix_high(stage, e)
                if s >= 3 and s % 2:
                    split(base + min(RING, (s - 1) // 2))
                if stage == "attn3" and s in (15, 17):
                    act.wait_ge(sem("od_ms"), s // 2 - 6)
                    n.activation(tmp[:, 1024:1536], tmp[:, 1024:1536], ACT.Sqrt).then_inc(sem("od_rms"), 1)

        def mix_high(stage, e):
            p = inst_pair(stage, e)
            if stage in ("attn0", "attn1"):
                act.wait_ge(pv_done, INST0[stage] + e + 1)
                src = ps[:, OB + p % 2, 0:T]
            elif stage == "attn3" and p - PAIR0[stage] < 4:
                k = p - PAIR0[stage]
                act.wait_ge(pv_done, INST0[stage] + e + 1)
                n.activation(od[:, k, :], ps[:, OB + p % 2, 0:T], ACT.Copy).then_inc(mix_hi, 1)
                return
            else:
                act.wait_ge(mix_prod, prods(stage, p))
                src = tmp[:, (p % 2) * T:(p % 2) * T + T]
            n.activation(hT_hi[:, mix_tile(stage, p), :], src, ACT.Copy).then_inc(mix_hi, 1)

        act.dma_start(table[:, :], a["tables"]).then_inc(sem("table_in"), 16)
        load_gain(0, None)
        act.dma_start(gains[:, :], a["gains"].partition_broadcast(P)).then_inc(sem("gains_in"), 16)
        for s, name in ((0, "cmp_k_w2"), (1, "cmp_k_w2"), (2, "cmp_v_w2")):
            act.dma_start(w2[:, :, s * 64:s * 64 + 64], a[name][0].rearrange("(f p) n -> p f n", p=P))\
               .then_inc(sem("small_in"), 16)
        act.dma_start(pe_sb[:, 0, :], a["cmp_pe_k"]).then_inc(sem("small_in"), 16)
        act.dma_start(pe_sb[:, 1, :], a["cmp_pe_v"]).then_inc(sem("small_in"), 16)
        act.dma_start(gsub[:, :], a["g_sub_d_2"].rearrange("o n -> n o")).then_inc(sem("small_in"), 16)
        square_sum(0)
        split(4)
        act.wait_ge(sem("table_in"), 16)
        n.activation(ident_b[:, :], ident, ACT.Copy)
        n.activation(ident_r[:, :], ident, ACT.Copy)
        n.activation(mask_b[:, :, :], masks[:, 0:2, :], ACT.Copy)
        n.activation(logc[:, 0, :], masks[:, 2, :], ACT.Copy).then_inc(sem("narrow"), 1)
        norm_high("norm0")
        load_gain(1, 0)
        chunk("w_in_e", 0, z0)
        chunk("w_in_e", 1, z0)
        drain("prep0", range(0, 4))
        chunk("w_in_e", 2, z0)
        drain("prep0", range(4, 7))
        act.wait_ge(acc_free[1], DENSE["w_in_e"] + 3)
        n.activation(small[:, 200:248].rearrange("p (t n) -> p t n", t=2), z0[:, :, 1280:1304], ACT.Exp, scale=-1.0)\
         .then_inc(sem("gate_exp"), 1)
        chunk("w_in_e", 3, z0)
        drain("prep0", range(7, 8))
        chunk("w_in_e", 4, z0)
        done = LAST["cmp_k_w1", 0]
        split(done + AHEAD)
        act.wait_ge(units_used, done)
        for f in range(2):
            ins = n.activation(h1k[:, f, :], ps[:, H1[0][f], 0:2 * CMP], ACT.Silu)
        ins.then_inc(sem("h1k"), 1)
        done = LAST["cmp_v_w1", 0]
        split(done + AHEAD)
        act.wait_ge(units_used, done)
        act.wait_ge(sem("zeros"), 2)
        for f in range(2):
            for u in range(2):
                ins = n.activation(h1v[:, f, u, :, 0:CMP],
                                   bc(ps[:, H1[1][f], CMP * u:CMP * u + CMP].unsqueeze(1), [P, 4, CMP]), ACT.Silu)
        ins.then_inc(sem("h1v"), 1)
        drain("prep0", range(8, 11))
        act.wait_ge(sem("cmp_shift"), 1)
        n.activation(cexp, cexp, ACT.Exp).then_inc(sem("cmp_exp"), 1)
        attention("attn0")

        def projection_out(name):
            for c in range(2):
                split(LAST[name, c] + AHEAD)

        projection_out("w_out_e")
        square_sum(1)
        norm_high("norm1")
        load_gain(2, 1)
        ffn(0)
        square_sum(2)
        norm_high("norm2")
        load_gain(3, 2)
        for c in range(6):
            chunk("w_qkv_o", c, z1)
            if 1 <= c < 5:
                drain("prep1", range(2 * c - 2, 2 * c))
        attention("attn1")
        projection_out("w_out_o")
        square_sum(3)
        norm_high("norm3")
        load_gain(5, 3)
        load_gain(4, 3, dst=gain_final)
        ffn(1)
        square_sum(4)
        square_sum(5)
        norm_high("norm5")
        load_gain(6, 5)

        def squares(name, src, count):
            act.wait_ge(sem(name + "_in"), 1)
            n.activation(tmp_heads(src), src, ACT.Square).then_inc(sem(name + "_sq"), 1)

        chunk("w_in_e_2", 0, z2)
        squares("qa", heads(z2[:, :, 0:512]), 8)
        chunk("w_in_e_2", 1, z2)
        squares("ka", heads(z2[:, :, 512:1024]), 8)
        chunk("w_in_e_2", 2, z2)
        drain("prep2", range(0, 2))
        chunk("w_in_e_2", 3, z2)
        squares("qb", heads(z2[:, :, 1536:2048]), 8)
        drain("prep2", range(2, 4))
        chunk("w_in_e_2", 4, z2)
        squares("kb", heads(z2[:, :, 2048:2176]), 2)
        gate_chunks("w_in_e_2", (5, 6), DENSE["gate_e"])
        drain("prep2", range(4, 7))
        attention("attn2")
        projection_out("w_out_e_2")
        square_sum(6)
        norm_high("norm6")
        chunk("w_in_o_2", 0, z3)
        chunk("w_in_o_2", 1, z3)
        squares("qd", heads(z3[:, :, 416:928]), 8)
        for k in range(2):
            f = FILL["lora"] + k
            act.wait_ge(t_filled, f + 1)
            n.activation(lr_hi[:, 2 * k:2 * k + 2, :].rearrange("p b t -> p (b t)"), ps[:, TB + f % 2, :], ACT.Copy)\
             .then_inc(sem("lora_hi"), 1)
        chunk("w_in_o_2", 2, z3)
        squares("kd", heads(z3[:, :, 928:1440]), 8)
        split(LAST["w_cq_b_2", 0] + AHEAD)
        act.wait_ge(units_used, LAST["w_cq_b_2", 0])
        for c, (lo, w) in enumerate(cut(0, 768)):
            d = DENSE["w_cq_b_2"] + c
            n.activation(lo_q[:, 0, lo:lo + w], ps[:, 2 * (d % 2), 0:w], ACT.Copy).then_inc(acc_free[0], 1)
        split(LAST["w_ckv_b_2", 0] + AHEAD)
        act.wait_ge(units_used, LAST["w_ckv_b_2", 0])
        for c, (lo, w) in enumerate(cut(0, 1024)):
            d = DENSE["w_ckv_b_2"] + c
            n.activation(lo_kv[:, 0, lo:lo + w], ps[:, 2 * (d % 2), 0:w], ACT.Copy).then_inc(acc_free[0], 1)
        act.wait_ge(sem("lam_dots"), 1)
        n.activation(lam[:, 0:2], ldot, ACT.Exp).then_inc(sem("lam_exp"), 1)
        split(LAST["w_in_o_2", 3] + AHEAD)
        take("w_in_o_2b", 0, (z3, *COLS["w_in_o_2"][0][3]), done=LAST["w_in_o_2", 3])
        drain("prep3", range(0, 4))
        for name, src in (("qc", heads(lo_q, MLA_D)), ("kc", kcat)):
            act.wait_ge(sem(name + "_in"), 1)
            n.activation(tmp_heads(src), src, ACT.Square).then_inc(sem(name + "_sq"), 1)
        gate_chunks("w_in_o_2", (4, 5), DENSE["gate_o"])
        drain("prep3", range(4, 12))
        attention("attn3")
        projection_out("w_out_o_2")

    @block.vector
    def _(dve):
        v = nc.vector
        chain = [0]
        split_to = [0]

        def link(ins):
            chain[0] += 1
            ins.then_inc(sem("dve_chain"), 1)
            dve.wait_ge(sem("dve_chain"), chain[0])

        def signal(ins, name, k=1):
            ins.then_inc(sem(name), 1)
            dve.wait_ge(sem(name), k)

        def split(upto):
            for u in range(split_to[0], min(upto, len(UNITS))):
                dve.wait_ge(hi_ready, u + 1)
                size = UNITS[u][3] * UNITS[u][4]
                v.tensor_tensor(w_lo[:, u % RING, 0:size], w_raw[:, u % RING, 0:size],
                                w_hi[:, u % RING, 0:size].bitcast(F32), ALU.subtract).then_inc(lo_ready, 1)
            split_to[0] = max(split_to[0], min(upto, len(UNITS)))

        def norm(k, eps, transposed=True, g=None):
            link(v.tensor_tensor_reduce(out=hA[:, 1, :], in0=x[:, 1, :], in1=x[:, 1, :], scale=1.0, scalar=0.0,
                                        op0=ALU.mult, op1=ALU.add, accum_out=ss[:, 1:2]))
            dve.wait_ge(sem(f"norm{k}_ss"), 1)
            signal(v.tensor_scalar(ms, ss, 1.0 / D, eps, ALU.mult, ALU.add), f"norm{k}_ms")
            dve.wait_ge(sem(f"norm{k}_rstd"), 1)
            dve.wait_ge(sem(f"gain{k}_in"), 16)
            for t in range(NT):
                dst = hA[:, t, :] if transposed else x[:, t, :]
                v.scalar_tensor_tensor(out=dst, in0=x[:, t, :], scalar=rstd[:, t:t + 1],
                                       in1=gb[:, :] if g is None else g, op0=ALU.mult, op1=ALU.mult)\
                 .then_inc(sem(f"norm{k}_h"), 1)
            dve.wait_ge(sem(f"norm{k}_h"), 2)

        def norm_low(stage):
            for k in range(4):
                f = FILL[stage] + k
                dve.wait_ge(t_hi, NORM_HI[stage] + k + 1)
                dst = norm_dst(stage)
                v.tensor_tensor(dst(hT_lo, k), ps[:, TB + f % 2, :].rearrange("p (b t) -> p b t", b=4),
                                dst(hT_hi, k).bitcast(F32), ALU.subtract).then_inc(t_drained[f % 2], 1)

        def drain(stage, fills):
            for k in fills:
                f = FILL[stage] + k
                if f % 2:
                    dve.wait_ge(t_filled, f + 1)
                    rows = MLA_D if stage == "prep3" and k >= 4 else P
                    v.tensor_copy(reg[0:rows, 2 * k:2 * k + 2, :].rearrange("p b t -> p (b t)"),
                                  ps[0:rows, TB + 1, :]).then_inc(t_drained[1], 1)

        def wait_taken(name, count):
            for t in range(NT):
                dve.wait_ge(acc_free[t], DENSE[name] + count)

        def take(d, buf, lo, w, done):
            dve.wait_ge(units_used, done)
            v.tensor_copy(buf[:, 1, lo:lo + w], ps[:, 2 * (d % 2) + 1, 0:w]).then_inc(acc_free[1], 1)

        def chunk(name, c, buf):
            done = LAST[name, c]
            split(done + AHEAD)
            take(DENSE[name] + c, buf, *COLS[name][0][c], done)
            wait_taken(name, c + 1)

        def add_residual(name, k, done):
            for t in range(NT):
                for c in range(2):
                    d = DENSE[name] + c
                    if t == 0:
                        dve.wait_ge(units_used, done[c])
                    v.tensor_tensor(x[:, t, c * 512:c * 512 + 512], x[:, t, c * 512:c * 512 + 512],
                                    ps[:, 2 * (d % 2) + t, :], ALU.add).then_inc(acc_free[t], 1)
                dve.wait_ge(acc_free[t], DENSE[name] + 2)
                if t == 0 and k is not None:
                    dve.sem_inc(sem(f"norm{k}_x"), 1)

        def rotate(src, dst_list, rt_, H, half):
            t_ = tm(H, 2 * half)
            cos, sin = rt_[:, :, 0, :], rt_[:, :, 1, :]
            sh = [P, NT, H, half]
            v.tensor_tensor(t_[:, :, :, 0:half], src[:, :, :, half:2 * half],
                            bc(sin[:, :, 0:half].unsqueeze(2), sh), ALU.mult)
            link(v.tensor_tensor(t_[:, :, :, half:2 * half], src[:, :, :, 0:half],
                                 bc(sin[:, :, half:2 * half].unsqueeze(2), sh), ALU.mult))
            first = dst_list[0]
            link(v.tensor_tensor(first, src, bc(cos.unsqueeze(2), [P, NT, H, 2 * half]), ALU.mult))
            for dst in reversed(dst_list):
                link(v.tensor_tensor(dst, first, t_, ALU.add))

        def ffn(layer):
            for j in range(FT):
                g = layer * FT + j
                if j % 2 == 0:
                    split(LAST[f"gu{layer}", j // 2] + AHEAD)
                dve.wait_ge(silu_ready, g + 1)
                v.tensor_tensor(hid32[:, g % 2, :], silu_g[:, g % 2, :], ps[:, g % 4, T:2 * T], ALU.mult)\
                 .then_inc(hid32_ready, 1)
                dve.wait_ge(hid_hi_ready, g + 1)
                v.tensor_tensor(hid_lo[:, j, :], hid32[:, g % 2, :], hid_hi[:, j, :].bitcast(F32), ALU.subtract)\
                 .then_inc(hid_ready, 1)
            for j in range(FT):
                split(LAST[f"down{layer}", j] + AHEAD)

        def attention(stage, at_step=None):
            inst, i0, f0 = INST[stage], INST0[stage], FILL[stage]
            base = next_units(stage)
            for s in range(len(inst) + LAG + 4):
                if s < len(inst):
                    i, it = i0 + s, inst[s]
                    dve.wait_ge(scores_ready, i + 1)
                    logits = ps[:, i % 3, :].rearrange("p (t k) -> p t k", t=2)
                    if it["causal"]:
                        v.tensor_reduce(out=negm[:, i, 0:1], in_=logits[:, 0, 0:P], axis=AX.X, op=ALU.max, negate=True)
                        ins = v.tensor_reduce(out=negm[:, i, 1:2], in_=logits[:, 1, :], axis=AX.X, op=ALU.max,
                                              negate=True)
                    else:
                        ins = v.tensor_reduce(out=negm[:, i, :], in_=logits, axis=AX.X, op=ALU.max, negate=True)
                    if "sink" in it:
                        h = it["sink"]
                        link(ins)
                        v.tensor_tensor(negm[:, i, :], negm[:, i, :], bc(nsink[:, h:h + 1], [P, 2]), ALU.min)\
                         .then_inc(max_ready, 1)
                        dve.wait_ge(max_ready, i + 1)
                        v.tensor_tensor(esink[:, h, :], negm[:, i, :], bc(sinks[:, h:h + 1], [P, 2]), ALU.add)\
                         .then_inc(sem("sink_shift"), 1)
                    else:
                        ins.then_inc(max_ready, 1)
                j = s - LAG
                if 0 <= j < len(inst) and (f0 + j) % 2:
                    f, i = f0 + j, i0 + j
                    w = 384 if inst[j]["causal"] else 512
                    dve.wait_ge(t_filled, f + 1)
                    if j >= 2:
                        dve.wait_ge(pv_done, i - 1)
                    v.tensor_copy(probT[:, i % 2, 0:w], ps[:, TB + 1, 0:w]).then_inc(t_drained[1], 1)
                j = s - 1
                if 0 <= j < len(inst):
                    scale_probs(stage, j)
                e = s - LAG - 3
                if 0 <= e < len(inst) and inst[e]["ends"]:
                    mix_low(stage, e)
                if s >= 3 and s % 2:
                    split(base + min(RING, (s - 1) // 2))
                if at_step:
                    at_step(s)

        def scale_probs(stage, j):
            i, it = INST0[stage] + j, INST[stage][j]
            dve.wait_ge(exp_ready, i + 1)
            if "sink" in it:
                dve.wait_ge(sem("esink"), it["sink"] + 1)
                link(v.tensor_tensor(den[:, i, :], den[:, i, :], esink[:, it["sink"], :], ALU.add))
            link(v.reciprocal(fac[:, i, :], den[:, i, :]))
            if "gate" in it:
                h, br = it["gate"]
                link(v.tensor_tensor(fac[:, i, :], fac[:, i, :], gates[:, :, h, br], ALU.mult))
            if it.get("lam"):
                link(v.tensor_tensor(fac[:, i, :], fac[:, i, :], bc(lam[:, 2:3], [P, 2]), ALU.mult))
            w = P if it["causal"] else T
            v.tensor_scalar(prob[:, i % 3, 0:w], prob[:, i % 3, 0:w], fac[:, i, 0:1], None, ALU.mult)
            v.tensor_scalar(prob[:, i % 3, 256:512], prob[:, i % 3, 256:512], fac[:, i, 1:2], None, ALU.mult)\
             .then_inc(probs_ready, 1)

        def mix_low(stage, e):
            p = inst_pair(stage, e)
            if stage in ("attn0", "attn1"):
                src = ps[:, OB + p % 2, 0:T]
            elif stage == "attn3" and p - PAIR0[stage] < 4:
                return
            else:
                dve.wait_ge(pv_done, INST0[stage] + e + 1)
                if prods(stage, p) > 2:
                    dve.wait_ge(mix_lo, lows(p) - 2)
                src = tmp[:, (p % 2) * T:(p % 2) * T + T]
                v.tensor_tensor(src, ps[:, OB + p % 2, 0:T], gT[:, mix_tile(stage, p), :], ALU.mult)\
                 .then_inc(mix_prod, 1)
            dve.wait_ge(mix_hi, p + 1)
            k = mix_tile(stage, p)
            v.tensor_tensor(hT_lo[:, k, :], src, hT_hi[:, k, :].bitcast(F32), ALU.subtract).then_inc(mix_lo, 1)

        dve.wait_ge(sem("x_in"), 16)
        dve.sem_inc(sem("norm0_x"), 1)
        norm(0, EPS_1)
        split(4)
        dve.wait_ge(sem("narrow"), 1)
        link(v.tensor_tensor(logc[:, 1, :], masks[:, 2, :], logc[:, 0, :].bitcast(F32), ALU.subtract))
        norm_low("norm0")
        chunk("w_in_e", 0, z0)
        rotate(heads(z0[:, :, 0:512]), [heads(hA[:, :, 0:512])], rope_q, 8, 32)
        dve.sem_inc(sem("q0_ready"), 1)
        chunk("w_in_e", 1, z0)
        rotate(heads(z0[:, :, 768:896]), [kd[:, :, 4:6, 0, :], kd[:, :, 4:6, 1, :]], rope, 2, 32)
        dve.sem_inc(sem("ks_ready"), 1)
        drain("prep0", range(0, 4))
        chunk("w_in_e", 2, z0)
        rotate(heads(z0[:, :, 1024:1152]), [kd[:, :, 6:8, 0, :], kd[:, :, 6:8, 1, :]], rope, 2, 32)
        dve.sem_inc(sem("kw_ready"), 1)
        drain("prep0", range(4, 7))
        dve.wait_ge(t_drained[0], (FILL["prep0"] + 6 + 1) // 2)
        dve.wait_ge(t_drained[1], (FILL["prep0"] + 6) // 2)
        dve.wait_ge(sem("small_in"), 96)
        bt32 = tmp[:, 0:960].rearrange("p (s l n) -> p s l n", s=2, l=16)
        for s in range(2):
            for u in range(2):
                for l2 in range(2):
                    pr = slice(64 * l2, 64 * l2 + 64)
                    blk = reg[pr, BLOCK["prep0"]["cmp", 2 * s + u], :]
                    src = bass.AP(blk.tensor, blk.offset + l2, [blk.ap[0], [2, 16], [16, CMP]])
                    ins = v.tensor_tensor(bt32[pr, s, :, u * CMP:(u + 1) * CMP], src,
                                          bc(pe_sb[pr, s, :].unsqueeze(2), [64, 16, CMP]), ALU.add)
        link(ins)
        link(v.tensor_copy(bt_hi[:, :, :, :], bt32))
        signal(v.tensor_tensor(bt_lo[:, :, :, :], bt32, bt_hi[:, :, :, :].bitcast(F32), ALU.subtract), "blocks")
        chunk("w_in_e", 3, z0)
        rotate(heads(z0[:, :, 1304:1816]), [heads(z0[:, :, 1304:1816])], rope_q, 8, 32)
        rotate(heads(z0[:, :, 1816:1944]), [kd[:, :, 8:10, 0, :], kd[:, :, 8:10, 1, :]], rope, 2, 32)
        dve.sem_inc(sem("b_ready"), 1)
        drain("prep0", range(7, 8))
        chunk("w_in_e", 4, z0)
        link(v.tensor_scalar(nsink, sinks, -1.0, None, ALU.mult))
        dve.wait_ge(sem("gate_exp"), 1)
        link(v.tensor_scalar(small[:, 200:248], small[:, 200:248], 1.0, None, ALU.add))
        link(v.reciprocal(small[:, 200:248], small[:, 200:248]))
        split(LAST["cmp_v_w1", 0])
        drain("prep0", range(8, 11))
        dve.wait_ge(sem("kc"), 1)
        v.tensor_scalar(kcT, ps[:, KC, 0:2 * CMP], SCALE, None, ALU.mult).then_inc(sem("kc_sb"), 1)
        dve.wait_ge(sem("vc"), 1)
        for u in range(2):
            for h in range(4):
                ins = v.tensor_copy(vbd[32 * h:32 * h + 32, u, 64 * h:64 * h + 64],
                                    ps[32 * h:32 * h + 32, VC, 64 * u:64 * u + 64])
        ins.then_inc(sem("vc_sb"), 1)
        dve.wait_ge(sem("cmp_scores"), 1)
        ce = cexp.rearrange("p (g c) -> p g c", c=CMP)
        cs = cexp.rearrange("p (u t h o c) -> p u t h o c", u=2, t=2, h=2, o=2)
        for odd in range(2):
            sc = ps[:, CS + odd, 0:256].rearrange("p (u t h c) -> p u t h c", u=2, t=2, h=2)
            for u in range(2):
                ins = v.tensor_tensor(cs[:, u, :, :, odd, :], sc[:, u, :, :, 0:CMP],
                                      bc(cmask[:, :, 0:CMP].unsqueeze(2), [P, 2, 2, CMP]), ALU.add)
        link(ins)
        link(v.tensor_reduce(out=cm, in_=ce, axis=AX.X, op=ALU.max))
        link(v.tensor_scalar(cm, cm, NEG / 2, None, ALU.max))
        signal(v.tensor_tensor(ce, ce, bc(cm.unsqueeze(2), [P, 16, CMP]), ALU.subtract), "cmp_shift")
        dve.wait_ge(sem("cmp_exp"), 1)
        link(v.tensor_reduce(out=cden, in_=ce, axis=AX.X, op=ALU.add))
        link(v.tensor_scalar(cden, cden, 1e-30, None, ALU.max))
        link(v.reciprocal(cfac, cden))
        for u in range(2):
            ins = v.tensor_tensor(cfac[:, 8 * u:8 * u + 8].rearrange("p (t h) -> p t h", t=2),
                                  cfac[:, 8 * u:8 * u + 8].rearrange("p (t h) -> p t h", t=2),
                                  gates[:, :, 4 * u:4 * u + 4, 0], ALU.mult)
        link(ins)
        signal(v.tensor_tensor(pcmp.rearrange("p u t h c -> p (u t h) c")[:, :, 0:CMP], ce,
                               bc(cfac.unsqueeze(2), [P, 16, CMP]), ALU.mult), "pcmp")
        f = FILL["cmp_p"]
        dve.wait_ge(t_filled, f + 1)
        v.tensor_copy(pcT.rearrange("p u q -> p (u q)"), ps[:, TB + f % 2, :]).then_inc(t_drained[f % 2], 1)
        attention("attn0")

        def projection_out(name, k):
            split(LAST[name, 0] + AHEAD)
            split(LAST[name, 1] + AHEAD)
            add_residual(name, k, [LAST[name, c] for c in range(2)])

        projection_out("w_out_e", 1)
        norm(1, EPS_1)
        norm_low("norm1")
        ffn(0)
        add_residual("down0", 2, [LAST["down0", FT - 1]] * 2)
        norm(2, EPS_1)
        norm_low("norm2")
        for c in range(6):
            chunk("w_qkv_o", c, z1)
            if c < 4:
                sec = heads(z1[:, :, 512 * c:512 * c + 512])
                rotate(sec, [sec], rope_q if c < 2 else rope, 8, 32)
                dve.sem_inc(sem("qk1_ready"), 1)
            if 1 <= c < 5:
                drain("prep1", range(2 * c - 2, 2 * c))
        attention("attn1")
        projection_out("w_out_o", 3)
        norm(3, EPS_1)
        norm_low("norm3")
        ffn(1)
        add_residual("down1", 4, [LAST["down1", FT - 1]] * 2)
        norm(4, EPS_1, transposed=False, g=gain_final)
        dve.sem_inc(sem("norm5_x"), 1)
        norm(5, EPS_2)
        norm_low("norm5")

        def head_stats(name, at, H, w, src):
            dve.sem_inc(sem(name + "_in"), 1)
            dve.wait_ge(sem(name + "_sq"), 1)
            sq = tmp_heads(src)
            link(v.tensor_reduce(out=hss[:, at:at + NT * H].rearrange("p (t h) -> p t h", t=NT), in_=sq, axis=AX.X,
                                 op=ALU.add))
            signal(v.tensor_scalar(hss[:, at:at + NT * H], hss[:, at:at + NT * H], 1.0 / w, EPS_2, ALU.mult, ALU.add),
                   name + "_ms")

        def head_scale(name, at, H, w, src, g=None):
            dve.wait_ge(sem(name + "_rstd"), 1)
            r_ = hrs[:, at:at + NT * H].rearrange("p (t h) -> p t h", t=NT)
            link(v.tensor_tensor(src, src, bc(r_.unsqueeze(3), [P, NT, H, w]), ALU.mult))
            if g is not None:
                for t in range(NT):
                    ins = v.tensor_tensor(src[:, t], src[:, t], bc(g.unsqueeze(1), [P, H, w]), ALU.mult)
                link(ins)

        def gain_tables(c, s, table_, g, half, blocks, scale):
            w = 2 * half * blocks
            dst_c, dst_s = gtab[:, :, c, :], gtab[:, :, s, :]
            v.tensor_tensor(dst_c, table_[:, :, 0, :], bc(g[:, 0:w].unsqueeze(1), [P, NT, w]), ALU.mult)
            for b in range(blocks):
                for h in range(2):
                    o, i = b * 2 * half + h * half, b * 2 * half + (1 - h) * half
                    ins = v.tensor_tensor(dst_s[:, :, o:o + half], table_[:, :, 1, o:o + half],
                                          bc(g[:, i:i + half].unsqueeze(1), [P, NT, half]), ALU.mult)
            link(ins)
            if scale != 1.0:
                v.tensor_scalar(dst_c, dst_c, scale, None, ALU.mult)
                link(v.tensor_scalar(dst_s, dst_s, scale, None, ALU.mult))

        def rotate_axial(src, dst, c, s, H):
            cos, sin = gtab[:, :, c, :], gtab[:, :, s, :]
            t_ = tm(H).rearrange("p t h (b c) -> p t h b c", b=4)
            s_ = src.rearrange("p t h (b c) -> p t h b c", b=4)
            for b in range(4):
                ins = v.tensor_tensor(t_[:, :, :, b, :], s_[:, :, :, b ^ 1, :],
                                      bc(sin[:, :, 16 * b:16 * b + 16].unsqueeze(2), [P, NT, H, 16]), ALU.mult)
            link(ins)
            link(v.tensor_tensor(src, src, bc(cos.unsqueeze(2), [P, NT, H, HD]), ALU.mult))
            for d_ in dst:
                link(v.tensor_tensor(d_, src, tm(H), ALU.add))

        qa, ka = heads(z2[:, :, 0:512]), heads(z2[:, :, 512:1024])
        qb, kb = heads(z2[:, :, 1536:2048]), heads(z2[:, :, 2048:2176])
        chunk("w_in_e_2", 0, z2)
        head_stats("qa", 0, 8, HD, qa)
        link(v.tensor_scalar(gain("gq_a_2"), gain("gq_a_2"), SCALE, None, ALU.mult))
        gain_tables(0, 1, rope_ax, gain("gq_b_2"), 16, 2, SCALE)
        gain_tables(2, 3, rope_ax, gain("gk_b_2"), 16, 2, 1.0)
        head_scale("qa", 0, 8, HD, qa, gain("gq_a_2"))
        dve.sem_inc(sem("qa_ready"), 1)
        chunk("w_in_e_2", 1, z2)
        head_stats("ka", 16, 8, HD, ka)
        split(LAST["w_in_e_2", 2] + AHEAD)
        head_scale("ka", 16, 8, HD, ka, gain("gk_a_2"))
        dve.sem_inc(sem("ka_ready"), 1)
        chunk("w_in_e_2", 2, z2)
        drain("prep2", range(0, 2))
        chunk("w_in_e_2", 3, z2)
        head_stats("qb", 32, 8, HD, qb)
        drain("prep2", range(2, 4))
        chunk("w_in_e_2", 4, z2)
        head_scale("qb", 32, 8, HD, qb)
        head_stats("kb", 48, 2, HD, kb)
        dve.wait_ge(sem("kb_rstd"), 1)
        rotate_axial(qb, [qb], 0, 1, 8)
        dve.sem_inc(sem("qb_ready"), 1)
        head_scale("kb", 48, 2, HD, kb)
        rotate_axial(kb, [kb_dup[:, :, :, 0, :], kb_dup[:, :, :, 1, :]], 2, 3, 2)
        dve.sem_inc(sem("kb_ready"), 1)
        split(LAST["w_in_e_2", 6] + AHEAD)
        drain("prep2", range(4, 7))
        attention("attn2")
        projection_out("w_out_e_2", 6)
        norm(6, EPS_2)
        norm_low("norm6")
        chunk("w_in_o_2", 0, z3)
        for t in range(NT):
            for k, (lo, w) in enumerate(((0, 256), (256, 128))):
                link(v.tensor_tensor_reduce(out=tmp[:, 0:w], in0=z3[:, t, lo:lo + w], in1=z3[:, t, lo:lo + w],
                                            scale=1.0 / w, scalar=0.0, op0=ALU.mult, op1=ALU.add,
                                            accum_out=hss[:, 2 * t + k:2 * t + k + 1]))
        signal(v.tensor_scalar(hss[:, 0:4], hss[:, 0:4], EPS_2, None, ALU.add), "lora_ms")
        for k in range(2):
            link(v.tensor_tensor_reduce(out=tmp[:, 0:HD], in0=gain(f"lam_q{k + 1}_2"), in1=gain(f"lam_k{k + 1}_2"),
                                        scale=1.0, scalar=0.0, op0=ALU.mult, op1=ALU.add,
                                        accum_out=ldot[:, k:k + 1]))
        dve.sem_inc(sem("lam_dots"), 1)
        dve.wait_ge(sem("lora_rstd"), 1)
        for t in range(NT):
            for k, (lo, w, gn) in enumerate(((0, 256, "g_cq_2"), (256, 128, "g_ckv_2"))):
                ins = v.scalar_tensor_tensor(out=z3[:, t, lo:lo + w], in0=z3[:, t, lo:lo + w],
                                             scalar=hrs[:, 2 * t + k:2 * t + k + 1], in1=gain(gn),
                                             op0=ALU.mult, op1=ALU.mult)
        signal(ins, "lora_ready")
        qd_, kd_ = heads(z3[:, :, 416:928]), heads(z3[:, :, 928:1440])
        chunk("w_in_o_2", 1, z3)
        head_stats("qd", 4, 8, HD, qd_)
        for k in range(2):
            f = FILL["lora"] + k
            dve.wait_ge(sem("lora_hi"), k + 1)
            v.tensor_tensor(lr_lo[:, 2 * k:2 * k + 2, :].rearrange("p b t -> p (b t)"), ps[:, TB + f % 2, :],
                            lr_hi[:, 2 * k:2 * k + 2, :].rearrange("p b t -> p (b t)").bitcast(F32), ALU.subtract)\
             .then_inc(t_drained[f % 2], 1)
        link(v.tensor_scalar(gain("gq_c_2"), gain("gq_c_2"), float(MLA_D) ** -0.5, None, ALU.mult))
        link(v.tensor_scalar(gain("gq_d_2"), gain("gq_d_2"), SCALE, None, ALU.mult))
        link(v.tensor_scalar(gsub[:, :], gsub[:, :], 1.0 - LAM_INIT, None, ALU.mult))
        head_scale("qd", 4, 8, HD, qd_, gain("gq_d_2"))
        rotate(qd_[:, :, :, 0:16], [qd_[:, :, :, 0:16]], rope_part, 8, 8)
        dve.sem_inc(sem("qd_ready"), 1)
        chunk("w_in_o_2", 2, z3)
        head_stats("kd", 20, 8, HD, kd_)
        split(LAST["w_cq_b_2", 0] + AHEAD)
        for c, (lo, w) in enumerate(cut(0, 768)):
            take(DENSE["w_cq_b_2"] + c, lo_q, lo, w, LAST["w_cq_b_2", 0])
        head_scale("kd", 20, 8, HD, kd_, gain("gk_d_2"))
        rotate(kd_[:, :, :, 0:16], [kd_[:, :, :, 0:16]], rope_part, 8, 8)
        dve.sem_inc(sem("kd_ready"), 1)
        split(LAST["w_ckv_b_2", 0] + AHEAD)
        for c, (lo, w) in enumerate(cut(0, 1024)):
            take(DENSE["w_ckv_b_2"] + c, lo_kv, lo, w, LAST["w_ckv_b_2", 0])
        wait_taken("w_ckv_b_2", 2)
        dve.wait_ge(sem("lam_exp"), 1)
        link(v.tensor_tensor(lam[:, 3:4], lam[:, 1:2], lam[:, 0:1], ALU.subtract))
        link(v.tensor_scalar(lam[:, 2:3], lam[:, 3:4], -LAM_INIT, None, ALU.add))
        split(LAST["w_in_o_2", 3] + AHEAD)
        take(DENSE["w_in_o_2b"], z3, *COLS["w_in_o_2"][0][3], LAST["w_in_o_2", 3])
        drain("prep3", range(0, 4))
        v.tensor_copy(kcat[:, :, :, 0:64], lo_kv.rearrange("p t (h d) -> p t h d", d=128)[:, :, :, 0:64])
        link(v.tensor_copy(kcat[:, :, :, 64:96], bc(z3[:, :, 384:416].unsqueeze(2), [P, NT, 8, 32])))
        qh = heads(lo_q, MLA_D)
        for name, src, at in (("qc", qh, 0), ("kc", kcat, 16)):
            dve.sem_inc(sem(name + "_in"), 1)
            dve.wait_ge(sem(name + "_sq"), 1)
            link(v.tensor_reduce(out=hss[:, at:at + 16].rearrange("p (t h) -> p t h", t=NT), in_=tmp_heads(src),
                                 axis=AX.X, op=ALU.add))
        signal(v.tensor_scalar(hss[:, 0:32], hss[:, 0:32], 1.0 / MLA_D, EPS_2, ALU.mult, ALU.add), "mla_ms")
        split(LAST["w_in_o_2", 4] + AHEAD)
        dve.wait_ge(sem("mla_rstd"), 1)
        for src, ro, gn in ((qh, 0, "gq_c_2"), (kcat, 16, "gk_c_2")):
            r_ = hrs[:, ro:ro + 16].rearrange("p (t h) -> p t h", t=NT)
            link(v.tensor_tensor(src, src, bc(r_.unsqueeze(3), [P, NT, 8, MLA_D]), ALU.mult))
            for t in range(NT):
                ins = v.tensor_tensor(src[:, t], src[:, t], bc(gain(gn).unsqueeze(1), [P, 8, MLA_D]), ALU.mult)
            link(ins)
            rotate(src[:, :, :, 64:96], [src[:, :, :, 64:96]], rope_mla, 8, 16)
            dve.sem_inc(sem("mla_ready"), 1)
        split(LAST["w_in_o_2", 5] + AHEAD)
        drain("prep3", range(4, 12))

        def sub_norm(s):
            for hf in range(2):
                if s == 14 + 2 * hf:
                    if hf == 0:
                        dve.wait_ge(mix_hi, PAIR0["attn3"] + 4)
                        link(v.memset(ones, 1.0))
                    o_ = od[:, 2 * hf:2 * hf + 2, :]
                    sq = tmp[:, 512:1024].rearrange("p (h t) -> p h t", h=2)
                    signal(v.tensor_tensor(sq, o_, o_, ALU.mult), "od_sq", hf + 1)
                if s == 15 + 2 * hf:
                    dve.wait_ge(sem("od_sum"), hf + 1)
                    var = tmp[:, 1024:1536]
                    signal(v.tensor_scalar(var, ps[:, SUM, :], 1.0 / P, EPS_2, ALU.mult, ALU.add), "od_ms", hf + 1)
                    dve.wait_ge(sem("od_rms"), hf + 1)
                    link(v.reciprocal(var, var))
                    o_ = od[:, 2 * hf:2 * hf + 2, :].rearrange("p h t -> p (h t)")
                    g_ = gT[:, 4 + 2 * hf:6 + 2 * hf, :].rearrange("p h t -> p (h t)")
                    link(v.tensor_tensor(var, var, o_, ALU.mult))
                    link(v.scalar_tensor_tensor(out=o_, in0=var, scalar=gsub[:, 0:1], in1=g_, op0=ALU.mult,
                                                op1=ALU.mult))
                    hi_ = hT_hi[:, 4 + 2 * hf:6 + 2 * hf, :].rearrange("p h t -> p (h t)")
                    lo_ = hT_lo[:, 4 + 2 * hf:6 + 2 * hf, :].rearrange("p h t -> p (h t)")
                    link(v.tensor_copy(hi_, o_))
                    signal(v.tensor_tensor(lo_, o_, hi_.bitcast(F32), ALU.subtract), "od_done", hf + 1)

        attention("attn3", sub_norm)
        projection_out("w_out_o_2", None)
        dve.sem_inc(sem("x_final"), 1)

    @block.tensor
    def _(pe):
        m = nc.tensor

        def open_fill(f):
            if f >= 2:
                pe.wait_ge(t_drained[f % 2], f // 2)

        def drained(f):
            pe.wait_ge(t_drained[0], (f + 2) // 2)
            pe.wait_ge(t_drained[1], (f + 1) // 2)

        def transpose_blocks(stage, fills):
            for k in fills:
                f = FILL[stage] + k
                open_fill(f)
                for b, (kind, i) in enumerate(PREP[stage][2 * k:2 * k + 2]):
                    for t in range(NT):
                        src = source(kind, i, t)
                        ins = m.transpose(ps[0:src.shape[1], TB + f % 2, b * T + t * P:b * T + t * P + P], src, ident)
                ins.then_inc(t_filled, 1)

        def from_norm(k, stage):
            for t in range(NT):
                pe.wait_ge(sem(f"norm{k}_h"), t + 1)
                for q in range(2):
                    f = FILL[stage] + 2 * t + q
                    open_fill(f)
                    for b in range(4):
                        kt = 4 * q + b
                        ins = m.transpose(ps[:, TB + f % 2, b * P:b * P + P], hA[:, t, kt * P:(kt + 1) * P], ident)
                    ins.then_inc(t_filled, 1)
            drained(FILL[stage] + 3)

        def product(o, lhs, rhs, start, stop):
            m.matmul(o, lhs[1], rhs[0], start=start, stop=False)
            m.matmul(o, lhs[0], rhs[0], start=False, stop=False)
            return m.matmul(o, lhs[0], rhs[1], start=False, stop=stop)

        def chunk(name, c, dense, lhs=(hT_hi, hT_lo), tiles=KT):
            for u in range(FIRST[name, c], LAST[name, c]):
                pe.wait_ge(lo_ready, u + 1)
                _, _, k0, ks, w = UNITS[u]
                wh, wl = halves(u)
                for t in range(NT):
                    if k0 == 0 and dense >= 2:
                        pe.wait_ge(acc_free[t], dense - 1)
                    for k in range(ks):
                        kk = k0 + k
                        l = tuple(b[:, kk, t * P:(t + 1) * P] for b in lhs)
                        ins = product(ps[:, 2 * (dense % 2) + t, 0:w], l, (wh[:, k, :], wl[:, k, :]),
                                      kk == 0, kk == tiles - 1)
                ins.then_inc(units_used, 1)

        def wide(name, widths, dense, lhs, tiles):
            for u in range(FIRST[name, 0], LAST[name, 0]):
                pe.wait_ge(lo_ready, u + 1)
                kk = UNITS[u][2]
                wh, wl = halves(u)
                for c, (lo, w) in enumerate(widths):
                    d = dense + c
                    for t in range(NT):
                        if kk == 0:
                            pe.wait_ge(acc_free[t], d - 1)
                        l = tuple(b[:, kk, t * P:(t + 1) * P] for b in lhs)
                        ins = product(ps[:, 2 * (d % 2) + t, 0:w], l, (wh[:, 0, lo:lo + w], wl[:, 0, lo:lo + w]),
                                      kk == 0, kk == tiles - 1)
                ins.then_inc(units_used, 1)

        def gate_chunk(name, c, dense):
            for t in range(NT):
                pe.wait_ge(acc_free[t], dense)
            for u in range(FIRST[name, c], LAST[name, c]):
                pe.wait_ge(lo_ready, u + 1)
                _, _, k0, ks, w = UNITS[u]
                wh, wl = halves(u)
                for b in range(4):
                    d = dense + b // 2
                    for k in range(ks):
                        kk = k0 + k
                        cols = slice(b * P, b * P + P)
                        ins = product(ps[:, 2 * (d % 2) + b % 2, 0:T], (wh[:, k, cols], wl[:, k, cols]),
                                      (hT_hi[:, kk, :], hT_lo[:, kk, :]), kk == 0, kk == KT - 1)
                ins.then_inc(units_used, 1)

        def ffn(layer):
            for c in range(FT // 2):
                first, last = FIRST[f"gu{layer}", c], LAST[f"gu{layer}", c]
                pe.wait_ge(lo_ready, last)
                for j in (2 * c, 2 * c + 1):
                    g = layer * FT + j
                    if j >= 4:
                        pe.wait_ge(hid32_ready, g - 3)
                    for gate in range(2):
                        for u in range(first, last):
                            wh, wl = halves(u)
                            lo = 256 * gate + P * (j % 2)
                            for k in range(2):
                                kk = UNITS[u][2] + k
                                ins = product(ps[:, g % 4, T * gate:T * gate + T],
                                              (wh[:, k, lo:lo + P], wl[:, k, lo:lo + P]),
                                              (hT_hi[:, kk, :], hT_lo[:, kk, :]), kk == 0, kk == KT - 1)
                            if gate and j % 2:
                                ins.then_inc(units_used, 1)
                    if j % 2 == 0:
                        ins.then_inc(even_up, 1)
            d = DENSE[f"down{layer}"]
            for j in range(FT):
                u = FIRST[f"down{layer}", j]
                pe.wait_ge(lo_ready, u + 1)
                if j == 0:
                    pe.wait_ge(hid_ready, (layer + 1) * FT)
                wh, wl = halves(u)
                for half in range(2):
                    for t in range(NT):
                        cols = slice(half * 512, half * 512 + 512)
                        l = tuple(b[:, j, t * P:(t + 1) * P] for b in (hid_hi, hid_lo))
                        ins = product(ps[:, 2 * ((d + half) % 2) + t, :], l, (wh[:, 0, cols], wl[:, 0, cols]),
                                      j == 0, j == FT - 1)
                ins.then_inc(units_used, 1)

        def attention(stage, at_step=None):
            inst, i0, f0 = INST[stage], INST0[stage], FILL[stage]
            for s in range(len(inst) + LAG + 1):
                if s < len(inst):
                    i, it = i0 + s, inst[s]
                    if s >= 3:
                        pe.wait_ge(exp_ready, i - 2)
                    for t in range(NT):
                        w = P * (t + 1) if it["causal"] else T
                        o = ps[:, i % 3, 256 * t:256 * t + w]
                        passes = it["bias"](t) if it["bias"] is not None else []
                        for n_, (idm, b) in enumerate(passes):
                            m.matmul(o, idm, b, start=n_ == 0, stop=False)
                        ins = m.matmul(o, it["q"][:, t * P:(t + 1) * P], it["k"][:, 0:w], start=not passes, stop=True)
                    ins.then_inc(scores_ready, 1)
                j = s - LAG
                if 0 <= j < len(inst):
                    i, f, causal = i0 + j, f0 + j, inst[j]["causal"]
                    pe.wait_ge(probs_ready, i + 1)
                    open_fill(f)
                    for kt in range(NT):
                        for t in range(NT):
                            if not (causal and kt > t):
                                col = column(kt, t, causal)
                                ins = m.transpose(ps[:, TB + f % 2, col:col + P],
                                                  prob[:, i % 3, 256 * t + kt * P:256 * t + kt * P + P], ident)
                    ins.then_inc(t_filled, 1)
                j = s - LAG - 1
                if 0 <= j < len(inst):
                    i, f, it = i0 + j, f0 + j, inst[j]
                    p = inst_pair(stage, j)
                    buf, lo, w = it["v"]
                    rows = slice(64 * it["half"], 64 * it["half"] + w)
                    if it["opens"] and p >= 2:
                        pe.wait_ge(*bank_taken(p - 2))
                    if it["opens"] and stage == "attn0" and it["pair"] < 4:
                        q = it["pair"]
                        m.matmul(ps[:, OB + p % 2, 0:T], vbd[:, q // 2, P * (q % 2):P * (q % 2) + P],
                                 pcT[:, q // 2, :], start=True, stop=False, skip_group_check=True)
                    pe.wait_ge(t_drained[f % 2], f // 2 + 1)
                    o = ps[rows, OB + p % 2, 0:T]
                    m.matmul(o, buf[:, 0, lo:lo + w], probT[:, i % 2, 0:T], start=it["first"], stop=False,
                             skip_group_check=True)
                    if it["causal"]:
                        ins = m.matmul(ps[rows, OB + p % 2, P:T], buf[:, 1, lo:lo + w], probT[:, i % 2, T:T + P],
                                       start=False, stop=it["last"], skip_group_check=True)
                    else:
                        ins = m.matmul(o, buf[:, 1, lo:lo + w], probT[:, i % 2, T:2 * T], start=False,
                                       stop=it["last"], skip_group_check=True)
                    ins.then_inc(pv_done, 1)
                if at_step:
                    at_step(s)

        pe.wait_ge(sem("table_in"), 16)
        from_norm(0, "norm0")
        pe.sem_inc(sem("norm0_used"), 1)
        d = DENSE["w_in_e"]
        chunk("w_in_e", 0, d)
        chunk("w_in_e", 1, d + 1)
        pe.wait_ge(sem("q0_ready"), 1)
        transpose_blocks("prep0", range(0, 4))
        chunk("w_in_e", 2, d + 2)
        pe.wait_ge(sem("cmp_dup"), 1)
        pe.wait_ge(sem("ks_ready"), 1)
        transpose_blocks("prep0", range(4, 7))
        chunk("w_in_e", 3, d + 3)
        pe.wait_ge(sem("kw_ready"), 1)
        transpose_blocks("prep0", range(7, 8))
        chunk("w_in_e", 4, d + 4)
        pe.wait_ge(sem("blocks"), 1)
        for t in range(NT):
            pe.wait_ge(acc_free[t], d + 5)
        for s, name in enumerate(("cmp_k_w1", "cmp_v_w1")):
            for u in range(FIRST[name, 0], LAST[name, 0]):
                pe.wait_ge(lo_ready, u + 1)
                wh, wl = halves(u)
                for f in range(2):
                    for k in range(4):
                        l = UNITS[u][2] + k
                        cols = slice(f * P, f * P + P)
                        ins = product(ps[:, H1[s][f], 0:2 * CMP], (wh[:, k, cols], wl[:, k, cols]),
                                      (bt_hi[:, s, l, :], bt_lo[:, s, l, :]), l == 0, l == 15)
                ins.then_inc(units_used, 1)
        pe.wait_ge(sem("b_ready"), 1)
        transpose_blocks("prep0", range(8, 11))
        pe.wait_ge(sem("h1k"), 1)
        pe.wait_ge(sem("small_in"), 96)
        for f in range(2):
            ins = m.matmul(ps[:, KC, 0:2 * CMP], w2[:, f, 0:128], h1k[:, f, :], start=f == 0, stop=f == 1)
        ins.then_inc(sem("kc"), 1)
        pe.wait_ge(sem("h1v"), 1)
        for u in range(2):
            for f in range(2):
                ins = m.matmul(ps[:, VC, 64 * u:64 * u + 64], h1v[:, f, u, :, :].rearrange("p h c -> p (h c)"),
                               w2[:, f, 128:192], start=f == 0, stop=f == 1)
        ins.then_inc(sem("vc"), 1)
        drained(FILL["prep0"] + 10)
        pe.wait_ge(sem("kc_sb"), 1)
        for u in range(2):
            for t in range(NT):
                for h in range(4):
                    q = pair_row("prep0", "qp", 4 * u + h)
                    lo = HD * (h % 2)
                    col = ((u * 2 + t) * 2 + h // 2) * 32
                    ins = m.matmul(ps[:, CS + h % 2, col:col + CMP], q[:, t * P:(t + 1) * P],
                                   kcT[lo:lo + HD, u * CMP:(u + 1) * CMP], start=True, stop=True)
        ins.then_inc(sem("cmp_scores"), 1)
        pe.wait_ge(sem("pcmp"), 1)
        f = FILL["cmp_p"]
        open_fill(f)
        for u in range(2):
            for t in range(NT):
                ins = m.transpose(ps[:, TB + f % 2, (2 * u + t) * P:(2 * u + t + 1) * P],
                                  pcmp[:, u, t, :, :].rearrange("p h c -> p (h c)"), ident)
        ins.then_inc(t_filled, 1)
        drained(f)
        pe.wait_ge(sem("vc_sb"), 1)
        pe.wait_ge(sem("narrow"), 1)
        attention("attn0")

        def project_out(name, pairs):
            pe.wait_ge(mix_lo, pairs)
            for c in range(2):
                chunk(name, c, DENSE[name] + c)

        project_out("w_out_e", 8)
        from_norm(1, "norm1")
        ffn(0)
        from_norm(2, "norm2")
        for c in range(6):
            chunk("w_qkv_o", c, DENSE["w_qkv_o"] + c)
            if 1 <= c < 5:
                pe.wait_ge(sem("qk1_ready"), c)
                transpose_blocks("prep1", range(2 * c - 2, 2 * c))
        for t in range(NT):
            pe.wait_ge(acc_free[t], DENSE["w_qkv_o"] + 6)
        drained(FILL["prep1"] + 7)
        attention("attn1")
        project_out("w_out_o", 16)
        from_norm(3, "norm3")
        ffn(1)
        from_norm(5, "norm5")
        d = DENSE["w_in_e_2"]
        chunk("w_in_e_2", 0, d)
        chunk("w_in_e_2", 1, d + 1)
        chunk("w_in_e_2", 2, d + 2)
        pe.wait_ge(sem("qa_ready"), 1)
        transpose_blocks("prep2", range(0, 2))
        chunk("w_in_e_2", 3, d + 3)
        pe.wait_ge(sem("ka_ready"), 1)
        transpose_blocks("prep2", range(2, 4))
        chunk("w_in_e_2", 4, d + 4)
        gate_chunk("w_in_e_2", 5, DENSE["gate_e"])
        gate_chunk("w_in_e_2", 6, DENSE["gate_e"] + 2)
        pe.wait_ge(sem("qb_ready"), 1)
        transpose_blocks("prep2", range(4, 6))
        pe.wait_ge(sem("kb_ready"), 1)
        transpose_blocks("prep2", range(6, 7))
        for t in range(NT):
            pe.wait_ge(acc_free[t], DENSE["gate_e"] + 4)
        drained(FILL["prep2"] + 6)
        pe.wait_ge(sem("bias_ready"), 1)
        attention("attn2")
        project_out("w_out_e_2", 24)
        from_norm(6, "norm6")
        d = DENSE["w_in_o_2"]
        chunk("w_in_o_2", 0, d)
        chunk("w_in_o_2", 1, d + 1)
        pe.wait_ge(sem("lora_ready"), 1)
        for k in range(2):
            f = FILL["lora"] + k
            open_fill(f)
            for b in range(2):
                for t in range(NT):
                    c = min(2 * k + b, 2)
                    ins = m.transpose(ps[:, TB + f % 2, b * T + t * P:b * T + t * P + P],
                                      z3[:, t, c * P:(c + 1) * P], ident)
            ins.then_inc(t_filled, 1)
        chunk("w_in_o_2", 2, d + 2)
        drained(FILL["lora"] + 1)
        wide("w_cq_b_2", cut(0, 768), DENSE["w_cq_b_2"], (lr_hi, lr_lo), 2)
        wide("w_ckv_b_2", cut(0, 1024), DENSE["w_ckv_b_2"], (lr_hi[:, 2:3, :], lr_lo[:, 2:3, :]), 1)
        chunk("w_in_o_2", 3, DENSE["w_in_o_2b"])
        pe.wait_ge(sem("qd_ready"), 1)
        transpose_blocks("prep3", range(0, 2))
        pe.wait_ge(sem("kd_ready"), 1)
        transpose_blocks("prep3", range(2, 4))
        gate_chunk("w_in_o_2", 4, DENSE["gate_o"])
        gate_chunk("w_in_o_2", 5, DENSE["gate_o"] + 2)
        pe.wait_ge(sem("mla_ready"), 1)
        transpose_blocks("prep3", range(4, 8))
        pe.wait_ge(sem("mla_ready"), 2)
        transpose_blocks("prep3", range(8, 12))
        for t in range(NT):
            pe.wait_ge(acc_free[t], DENSE["gate_o"] + 4)
        drained(FILL["prep3"] + 11)

        def sub_norm(s):
            for hf in range(2):
                if s == 14 + 2 * hf:
                    pe.wait_ge(sem("od_sq"), hf + 1)
                    m.matmul(ps[:, SUM, :], ones[:, :], tmp[:, 512:1024], start=True, stop=True)\
                     .then_inc(sem("od_sum"), 1)

        attention("attn3", sub_norm)
        pe.wait_ge(sem("od_done"), 2)
        project_out("w_out_o_2", 28)

    ctx.close()


def rotation(angles, signs, scale=1.0):
    t = np.stack([np.cos(angles), np.sin(angles) * signs], axis=1).astype(np.float32) * np.float32(scale)
    return t.reshape(NT, P, -1).transpose(1, 0, 2).reshape(P, -1)


def tables():
    f = np.float32
    pos = np.arange(T, dtype=f)

    def turned(p, dim, theta):
        inv = (1.0 / (f(theta) ** (np.arange(0, dim, 2, dtype=f) / f(dim)))).astype(f)
        a = (p[:, None] * inv[None, :]).astype(f)
        return np.concatenate([a, a], 1), np.concatenate([-np.ones(dim // 2, f), np.ones(dim // 2, f)])

    ar, sg = turned(np.floor(pos / 64).astype(f), 32, 10000.0)
    ac, _ = turned((pos % 64).astype(f), 32, 10000.0)
    i, j = np.arange(T)[:, None], np.arange(T)[None, :]
    causal = np.where(j <= i, 0.0, NEG)
    window = np.where((j <= i) & (i - j < 128), 0.0, NEG)
    count = (i - j <= 128).astype(int) + ((i - j) % 4 == 0) + ((i - j) % 16 == 0)
    dilated = np.where((j <= i) & (count > 0), np.log(np.maximum(count, 1)), NEG)
    c = np.arange(16)[None, :]
    cm = np.where((c * 16 + 31 <= i) & (c < CMP), 0.0, NEG)
    parts = {
        "ident": np.eye(P),
        "masks": np.concatenate([np.concatenate([b[0:P, 0:P], b[P:T, :]], axis=1)
                                 for b in (causal, window, dilated)], axis=1),
        "cmask": cm.reshape(NT, P, 16).transpose(1, 0, 2).reshape(P, -1),
        "rope": rotation(*turned(pos, HD, 10000.0)),
        "rope_q": rotation(*turned(pos, HD, 10000.0), SCALE),
        "rope_ax": rotation(np.concatenate([ar, ac], 1), np.concatenate([sg, sg])),
        "rope_mla": rotation(*turned(pos, 32, 10000.0)),
        "rope_part": rotation(*turned(pos, 16, 500000.0)),
    }
    return np.ascontiguousarray(np.concatenate([parts[name].astype(f) for name in TAB], axis=1))


def kernel(**inputs):
    import concourse.bacc as _bacc
    from concourse.bass_utils import run_bass_kernel_spmd as _run

    arrays = {name: np.ascontiguousarray(v) for name, v in inputs.items() if name not in GAIN}
    for name in ("cmp_pe_k", "cmp_pe_v"):
        arrays[name] = np.ascontiguousarray(arrays[name].reshape(16, P).T)
    arrays["rpb_a_2"] = np.ascontiguousarray(arrays["rpb_a_2"][..., ::-1])
    arrays["gains"] = np.ascontiguousarray(np.concatenate([np.asarray(inputs[n]).reshape(1, -1) for n in GAIN], 1))
    arrays["tables"] = tables()
    nc = _bacc.Bacc("TRN2", target_bir_lowering=False, num_devices=1)
    aps = {name: nc.dram_tensor("in_" + name, v.shape, F32, kind="ExternalInput").ap() for name, v in arrays.items()}
    out = nc.dram_tensor("out_0", (1, T, D), F32, kind="ExternalOutput").ap()
    net(nc, aps, out)
    r = _run(nc, [{"in_" + name: v for name, v in arrays.items()}], core_ids=[0])
    return r.results[0]["out_0"]
```

```python
import numpy as np
import concourse.bass as bass
from concourse import mybir
from contextlib import ExitStack

F32 = mybir.dt.float32
F32R = mybir.dt.float32r
BF16 = mybir.dt.bfloat16
ALU = mybir.AluOpType
ACT = mybir.ActivationFunctionType
AX = mybir.AxisListType

P = 128
T = 256
NT = T // P
D = 1024
KT = D // P
HD = 64
SCALE = HD ** -0.5
FFN = 2816
FT = FFN // P
NEG = -1.0e30
EPS_1, EPS_2 = 1e-5, 1e-6
MLA_D = 96
LAM_INIT = 0.8 - 0.6 * float(np.exp(-0.3))
CMP = T // 16 - 1

UNIT = 1024
RING = 8
AHEAD = 4


def cut(lo, hi):
    return [(a, min(512, hi - a)) for a in range(lo, hi, 512)]


COLS = {
    "w_in_e": (cut(0, 1536) + [(1536, 268), (1804, 268)], []),
    "w_out_e": (cut(0, D), []),
    "w_qkv_o": (cut(0, 3072), []),
    "w_out_o": (cut(0, D), []),
    "w_in_e_2": (cut(0, 2304), cut(2304, 3328)),
    "w_out_e_2": (cut(0, D), []),
    "w_in_o_2": ([(0, 416), (416, 512), (928, 512), (1440, 512)], cut(1952, 2976)),
    "w_out_o_2": (cut(0, D), []),
}


def stream():
    out = []

    def chunk(name, c, tiles, width):
        per = max(k for k in (1, 2, 4, 8) if k * width <= UNIT and tiles % k == 0)
        for k in range(0, tiles, per):
            out.append((name, c, k, per, width))

    def projection(name, which=None):
        tok, feat = COLS[name]
        for c, (_, w) in enumerate(tok + feat):
            if which is None or c in which:
                chunk(name, c, KT, w)

    def ffn(layer):
        for c in range(FT // 2):
            chunk(f"gu{layer}", c, KT, 512)
        for c in range(FT):
            chunk(f"down{layer}", c, 1, D)

    projection("w_in_e")
    chunk("cmp_k_w1", 0, 16, 256)
    chunk("cmp_v_w1", 0, 16, 256)
    projection("w_out_e")
    ffn(0)
    projection("w_qkv_o")
    projection("w_out_o")
    ffn(1)
    projection("w_in_e_2")
    projection("w_out_e_2")
    projection("w_in_o_2", (0, 1, 2))
    chunk("w_cq_b_2", 0, 2, 768)
    chunk("w_ckv_b_2", 0, 1, D)
    projection("w_in_o_2", (3, 4, 5))
    projection("w_out_o_2")
    return out


UNITS = stream()
FIRST, LAST = {}, {}
for _n, _u in enumerate(UNITS):
    FIRST.setdefault(_u[:2], _n)
    LAST[_u[:2]] = _n + 1

DENSE, _d = {}, 0
for _name, _n in [("w_in_e", 5), ("w_out_e", 2), ("down0", 2), ("w_qkv_o", 6), ("w_out_o", 2), ("down1", 2),
                  ("w_in_e_2", 5), ("gate_e", 4), ("w_out_e_2", 2), ("w_in_o_2", 3), ("w_cq_b_2", 2),
                  ("w_ckv_b_2", 2), ("w_in_o_2b", 1), ("gate_o", 4), ("w_out_o_2", 2)]:
    DENSE[_name] = _d
    _d += _n

FILL, _f = {}, 0
for _name, _n in [("norm0", 4), ("prep0", 11), ("cmp_p", 1), ("attn0", 24), ("norm1", 4), ("norm2", 4),
                  ("prep1", 8), ("attn1", 16), ("norm3", 4), ("norm5", 4), ("prep2", 7), ("attn2", 16),
                  ("norm6", 4), ("lora", 2), ("prep3", 12), ("attn3", 16)]:
    FILL[_name] = _f
    _f += _n
NORM_HI = {"norm0": 0, "norm1": 4, "norm2": 8, "norm3": 12, "norm5": 16, "norm6": 20}

STAGES = ("attn0", "attn1", "attn2", "attn3")
INST0 = {"attn0": 0, "attn1": 24, "attn2": 40, "attn3": 56}
PAIR0 = {"attn0": 0, "attn1": 8, "attn2": 16, "attn3": 24}
LAG = 2
TAIL = 4

TAB, _c = {}, 0
for _name, _n in [("ident", 128), ("masks", 1152), ("cmask", 32), ("rope", 256), ("rope_q", 256), ("rope_ax", 256),
                  ("rope_mla", 128), ("rope_part", 64)]:
    TAB[_name] = (_c, _n)
    _c += _n
TABLE_COLS = _c
GAIN, _c = {}, 0
for _name, _n in [("gq_a_2", 64), ("gk_a_2", 64), ("gq_b_2", 64), ("gk_b_2", 64), ("g_cq_2", 256), ("g_ckv_2", 128),
                  ("gq_c_2", 96), ("gk_c_2", 96), ("gq_d_2", 64), ("gk_d_2", 64), ("sinks", 8), ("lam_q1_2", 64),
                  ("lam_k1_2", 64), ("lam_q2_2", 64), ("lam_k2_2", 64)]:
    GAIN[_name] = (_c, _n)
    _c += _n
GAIN_COLS = _c


def net(nc, a, out):
    ctx = ExitStack()
    sems = {}

    def sem(name):
        if name not in sems:
            sems[name] = ctx.enter_context(nc.semaphore(name))
        return sems[name]

    BASE = 16896
    cursor = [BASE]

    def place(name, shape, dtype=F32, at=None):
        size = 2 if dtype == BF16 else 4
        for n in shape[1:]:
            size *= n
        where = cursor[0] if at is None else at
        t = nc.alloc_sbuf_tensor_at(name, shape, dtype, offset=where)
        if at is None:
            cursor[0] = where + (size + 31) // 32 * 32
        return t

    x = place("x", [P, NT, D])
    hT_hi = place("hT_hi", [P, KT, T], F32R)
    hT_lo = place("hT_lo", [P, KT, T], F32R)
    w_hi = place("w_hi", [P, RING, UNIT], F32R)
    w_at = cursor[0]
    w_raw = place("w_raw", [P, RING, UNIT])
    w_lo = place("w_lo", [P, RING, UNIT], F32R, at=w_at)
    table = place("table", [P, TABLE_COLS])
    gains = place("gains", [P, GAIN_COLS])
    gtab = place("gtab", [P, NT, 4, HD])
    gb = place("gb", [P, D])
    negm = place("negm", [P, 72, 2])
    den = place("den", [P, 72, 2])
    fac = place("fac", [P, 72, 2])
    small = place("small", [P, 736])
    w2 = place("w2", [P, 2, 192])
    pe_sb = place("pe_sb", [P, 2, 16])
    gsub = place("gsub", [P, 1])
    mask_b = place("mask_b", [P, 2, 384], BF16)
    ident_b = place("ident_b", [P, P], BF16)
    ident_r = place("ident_r", [P, P], F32R)
    logc = place("logc", [P, 2, 384], F32R)
    phase_at = cursor[0]
    z = place("z", [P, 6656])
    hA = place("hA", [P, NT, D])
    tmp = place("tmp", [P, 1536])
    extra = place("extra", [P, 3584])
    reg = place("reg", [P, 24, T])
    prob_at = cursor[0]
    prob = place("prob", [P, 3, 512])
    probT = place("probT", [P, 2, 512])
    assert cursor[0] <= 229368, cursor[0]
    hid_hi = place("hid_hi", [P, FT, T], F32R, at=phase_at)
    hid_lo = place("hid_lo", [P, FT, T], F32R, at=phase_at + 4 * FT * T)
    silu_g = place("silu_g", [P, 2, T], at=phase_at + 8 * FT * T)
    hid32 = place("hid32", [P, 2, T], at=phase_at + 8 * FT * T + 2048)
    bt_hi = place("bt_hi", [P, 2, 16, 32], F32R, at=prob_at)
    bt_lo = place("bt_lo", [P, 2, 16, 32], F32R, at=prob_at + 4096)
    lr_hi = place("lr_hi", [P, 4, T], F32R, at=prob_at)
    lr_lo = place("lr_lo", [P, 4, T], F32R, at=prob_at + 4096)
    ps = ctx.enter_context(nc.psum_tensor("ps", [P, 8, 512], F32))
    TB, OB, SUM = 4, 6, 3
    OF = (SUM, 2)

    tab = lambda n: table[:, TAB[n][0]:TAB[n][0] + TAB[n][1]]
    ident = tab("ident")
    rt = lambda n, w: tab(n).rearrange("p (t s d) -> p t s d", t=NT, s=2, d=w)
    rope, rope_q, rope_ax = rt("rope", HD), rt("rope_q", HD), rt("rope_ax", HD)
    rope_mla, rope_part = rt("rope_mla", 32), rt("rope_part", 16)
    cmask = tab("cmask").rearrange("p (t c) -> p t c", t=NT)
    masks = tab("masks").rearrange("p (m c) -> p m c", m=3)
    gain = lambda n: gains[:, GAIN[n][0]:GAIN[n][0] + GAIN[n][1]]
    sinks = gain("sinks")
    zw = lambda w: z[:, 0:NT * w].rearrange("p (t n) -> p t n", t=NT)
    z0, z1, z2, z3 = zw(2072), zw(3072), zw(2304), zw(1952)
    gT = z[:, 4608:6656].rearrange("p (k t) -> p k t", k=KT)
    heads = lambda ap, w=HD: ap.rearrange("p t (h d) -> p t h d", d=w)
    kd = extra[:, 0:2560].rearrange("p (t h c d) -> p t h c d", t=NT, h=10, c=2)
    pcmp = extra[:, 2560:3072].rearrange("p (u t h c) -> p u t h c", u=2, t=2, h=4)
    pcT = extra[:, 3072:3584].rearrange("p (u q) -> p u q", u=2)
    bias_na = extra[:, 0:3072].rearrange("p (h u c) -> p h u c", h=8, u=6)
    kb_dup = extra[:, 3072:3584].rearrange("p (t h c d) -> p t h c d", t=2, h=2, c=2)
    lo_q = extra[:, 0:1536].rearrange("p (t n) -> p t n", t=NT)
    lo_kv = extra[:, 1536:3584].rearrange("p (t n) -> p t n", t=NT)
    kcat = hA[:, :, 0:768].rearrange("p t (h d) -> p t h d", d=MLA_D)
    h1v = hA[:, 0, 512:1024].rearrange("p (f u h c) -> p f u h c", f=2, u=2, h=4)
    h1 = tmp[0:32, 1024:1536]
    vbd = hA[:, 1, 512:1024].rearrange("p (u n) -> p u n", u=2)
    od = z[:, 0:1024].rearrange("p (h t) -> p h t", h=4)
    ones = extra[:, 0:P]
    gain_final = prob[:, 0:2, :].rearrange("p b n -> p (b n)")
    tm = lambda h, w=HD: tmp[:, 0:NT * h * w].rearrange("p (t h d) -> p t h d", t=NT, h=h)
    odp = z[:, 0:1024].rearrange("p (f n) -> p f n", f=2)
    od_sq = tmp[:, 512:1536].rearrange("p (f n) -> p f n", f=2)
    tmp_heads = lambda ap: tm(ap.shape[2], ap.shape[3])
    bc = lambda ap, shape: ap.to_broadcast(shape)
    ss, ms, rstd = small[:, 0:4], small[:, 4:6], small[:, 6:8]
    halfs = small[:, 8:72]
    hss, hrs = small[:, 72:136], small[:, 136:200]
    gates = small[:, 200:248].rearrange("p (t h b) -> p t h b", t=NT, h=8)
    esink = small[:, 280:296].rearrange("p (h t) -> p h t", t=NT)
    lam = small[:, 296:300]
    cm, cden, cfac = small[:, 300:316], small[:, 316:332], small[:, 332:348]
    od_rstd = small[:, 696:704]
    cexp = small[:, 352:592]
    nsink, ldot = small[:, 592:600], small[:, 600:602]
    h1k = small[:, 604:664].rearrange("p (f n) -> p f n", f=2)
    kcT = small[:, 664:694]
    H1, HT, KC, VC, CS = 2, 1, 6, 7, 2

    slot_full = [sem(f"slot_full_{s}") for s in range(RING)]
    hi_ready, lo_ready = sem("hi_ready"), sem("lo_ready")
    pool_lo = sem("pool_lo")
    units_used = sem("units_used")
    acc_free = [sem("acc_free_0"), sem("acc_free_1")]
    t_filled = sem("t_filled")
    t_drained = [sem("t_drained_even"), sem("t_drained_odd")]
    t_hi = sem("t_hi")
    scores_ready, max_ready, exp_ready = sem("scores_ready"), sem("max_ready"), sem("exp_ready")
    probs_ready, pv_done = sem("probs_ready"), sem("pv_done")
    mix_prod, mix_hi, mix_lo = sem("mix_prod"), sem("mix_hi"), sem("mix_lo")
    even_up, silu_ready, hid_ready = sem("even_up"), sem("silu_ready"), sem("hid_ready")
    hid32_ready, hid_hi_ready = sem("hid32_ready"), sem("hid_hi_ready")

    def unit_parts(n):
        name, c, k0, ks, w = UNITS[n]
        s = w_raw[:, n % RING, 0:ks * w].rearrange("p (k n) -> p k n", k=ks)
        rows = slice(k0 * P, (k0 + ks) * P)
        if name[:2] == "gu":
            src = a["w_gate_up"][int(name[2])][rows].rearrange("(k p) n -> p k n", p=P)
            return [(s[:, :, 256 * g:256 * g + 256], src[:, :, g * FFN + c * 256:g * FFN + c * 256 + 256])
                    for g in range(2)]
        if name[:4] == "down":
            return [(s, a["w_down"][int(name[4])][c * P:c * P + P].rearrange("(k p) n -> p k n", p=P))]
        src = a[name][0][rows].rearrange("(k p) n -> p k n", p=P)
        if name in COLS:
            lo = (COLS[name][0] + COLS[name][1])[c][0]
            src = src[:, :, lo:lo + w]
        return [(s, src)]

    LANDED = []
    for n in range(len(UNITS)):
        LANDED.append((LANDED[n - RING] if n >= RING else 0) + 16 * len(unit_parts(n)))

    def halves(n):
        _, _, _, ks, w = UNITS[n]
        return tuple(t[:, n % RING, 0:ks * w].rearrange("p (k n) -> p k n", k=ks) for t in (w_hi, w_lo))

    PREP = {
        "prep0": [("qp", i) for i in range(4)] + [("qr", i) for i in range(4)] + [("cmp", i) for i in range(4)]
        + [("ks", i) for i in range(2)] + [("kw", i) for i in range(2)] + [("bq", i) for i in range(4)]
        + [("bk", i) for i in range(2)],
        "prep1": [("q", i) for i in range(8)] + [("k", i) for i in range(8)],
        "prep2": [("qa", i) for i in range(4)] + [("ka", i) for i in range(4)] + [("qb", i) for i in range(4)]
        + [("kb", i) for i in range(2)],
        "prep3": [("qd", i) for i in range(4)] + [("kd", i) for i in range(4)]
        + [("qc", i) for i in range(8)] + [("kc", i) for i in range(8)],
    }
    BLOCK = {s: {key: n for n, key in enumerate(blocks)} for s, blocks in PREP.items()}

    def source(kind, i, t):
        if kind in ("cmp", "ks", "kw", "bk"):
            h = {"cmp": 0, "ks": 4, "kw": 6, "bk": 8}[kind] + i
            return extra[:, t * 1280 + h * P:t * 1280 + (h + 1) * P]
        if kind == "kb":
            return extra[:, 3072 + (t * 2 + i) * P:3072 + (t * 2 + i + 1) * P]
        w, buf, lo = {"qp": (P, z0, 0), "qr": (P, hA, 0), "bq": (P, z0, 1304), "q": (P, z1, 0), "k": (P, z1, 1024),
                      "qa": (P, z2, 0), "ka": (P, z2, 512), "qb": (P, z2, 1536), "qd": (P, z3, 416),
                      "kd": (P, z3, 928), "qc": (MLA_D, lo_q, 0), "kc": (MLA_D, hA, 0)}[kind]
        return buf[:, t, lo + i * w:lo + (i + 1) * w]

    def pair_row(stage, kind, h):
        lo = HD * (h % 2)
        return reg[lo:lo + HD, BLOCK[stage][kind, h // 2], :]

    def dup_row(stage, kind, h, like):
        lo = HD * (like % 2)
        return reg[lo:lo + HD, BLOCK[stage][kind, h], :]

    def mask_passes(m):
        return lambda t: [(ident_b[:, :], mask_b[:, m, P * t:P * t + P * (t + 1)])]

    def count_passes(t):
        return [(ident_r[:, :], logc[:, part, P * t:P * t + P * (t + 1)]) for part in range(2)]

    def bias_passes(h):
        def f(t):
            row = bias_na[:, h, 2 - 2 * t, 63:64]
            return [(ident, bass.AP(row.tensor, row.offset, [row.ap[0], [64, 4], [-1, 64]]))]
        return f

    def instances(stage):
        out = []
        if stage == "attn0":
            for h in range(8):
                for br, (kk, vlo) in enumerate((("ks", 896), ("kw", 1152))):
                    out.append(dict(q=pair_row("prep0", "qr", h), k=dup_row("prep0", kk, h // 4, h),
                                    bias=mask_passes(0), v=(z0, vlo + HD * (h // 4), HD), causal=True, half=h % 2,
                                    pair=h // 2, first=False, last=br == 1, gate=(h, br + 1)))
            for h in range(8):
                out.append(dict(q=pair_row("prep0", "bq", h), k=dup_row("prep0", "bk", h // 4, h),
                                bias=mask_passes(1), v=(z0, 1944 + HD * (h // 4), HD), causal=True, half=h % 2,
                                pair=4 + h // 2, first=True, last=True, sink=h))
        if stage == "attn1":
            for h in range(16):
                out.append(dict(q=pair_row("prep1", "q", h), k=pair_row("prep1", "k", h), bias=count_passes,
                                v=(z1, 2048 + HD * h, HD), causal=True, half=h % 2, pair=h // 2, first=True,
                                last=True))
        if stage == "attn2":
            for h in range(8):
                out.append(dict(q=pair_row("prep2", "qa", h), k=pair_row("prep2", "ka", h), bias=bias_passes(h),
                                v=(z2, 1024 + HD * h, HD), causal=False, half=h % 2, pair=h // 2, first=True,
                                last=True))
            for h in range(8):
                out.append(dict(q=pair_row("prep2", "qb", h), k=dup_row("prep2", "kb", h // 4, h), bias=None,
                                v=(z2, 2176 + HD * (h // 4), HD), causal=False, half=h % 2, pair=4 + h // 2,
                                first=True, last=True))
        if stage == "attn3":
            for h in range(8):
                out.append(dict(q=pair_row("prep3", "qd", h), k=pair_row("prep3", "kd", h), bias=None,
                                v=(z3, 1440 + P * (h // 2), P), causal=False, half=0, pair=h // 2,
                                first=h % 2 == 0, last=h % 2 == 1, lam=h % 2 == 1))
            for h in range(8):
                out.append(dict(q=reg[0:MLA_D, BLOCK["prep3"]["qc", h], :], k=reg[0:MLA_D, BLOCK["prep3"]["kc", h], :],
                                bias=None, v=(lo_kv, P * h + HD, HD), causal=False, half=h % 2, pair=4 + h // 2,
                                first=True, last=True))
        return out

    INST = {s: instances(s) for s in STAGES}
    for s in STAGES:
        for n, i in enumerate(INST[s]):
            i["opens"] = n == 0 or INST[s][n - 1]["pair"] != i["pair"]
            i["ends"] = n + 1 == len(INST[s]) or INST[s][n + 1]["pair"] != i["pair"]

    def inst_pair(stage, e):
        return PAIR0[stage] + INST[stage][e]["pair"]

    def gated(stage, e):
        return stage == "attn2" or stage == "attn3" and e >= 8

    def prods(stage, p):
        return p - PAIR0["attn2"] + 1 if stage == "attn2" else 8 + p - PAIR0["attn3"] - 3

    def lows(p):
        return p + 1 if p < 24 else p - 3

    def mix_tile(stage, p):
        k = p - PAIR0[stage]
        return k if stage != "attn3" else (k + 4) % 8

    def bank_taken(p):
        if p < 16:
            return mix_lo, lows(p)
        if 24 <= p < 28:
            return mix_hi, p + 1
        return mix_prod, prods("attn2" if p < 24 else "attn3", p)

    def column(kt, t, causal):
        if causal:
            return {(0, 0): 0, (0, 1): P, (1, 1): 2 * P}[kt, t]
        return kt * T + t * P

    def next_units(stage):
        return FIRST[{"attn0": "w_out_e", "attn1": "w_out_o", "attn2": "w_out_e_2", "attn3": "w_out_o_2"}[stage], 0]

    POOL_UNITS = {st: (next_units(st), next_units(st) + RING) for st in STAGES}
    POOL_UNITS["lora"] = (FIRST["w_cq_b_2", 0], LAST["w_ckv_b_2", 0])
    POOL_UNITS["gate_o"] = (FIRST["w_in_o_2", 5], LAST["w_in_o_2", 5])

    def by_pool(u):
        return any(lo <= u < hi for lo, hi in POOL_UNITS.values())

    def low_ready(u):
        pool_count = sum(by_pool(w) for w in range(u + 1))
        return (pool_lo, pool_count) if by_pool(u) else (lo_ready, u + 1 - pool_count)

    NORM_G = [("attn_norm", 0), ("ffn_norm", 0), ("attn_norm", 1), ("ffn_norm", 1), ("final_norm", 0),
              ("norm_e_2", 0), ("norm_o_2", 0)]

    def norm_dst(buf, k):
        t, k4 = k // 2, 4 * (k % 2)
        return buf[:, k4:k4 + 4, t * P:(t + 1) * P]

    block = ctx.enter_context(nc.Block())

    @block.sync
    def _(sp):
        for t in range(NT):
            sp.dma_start(x[:, t, :], a["x"][0, t * P:(t + 1) * P, :]).then_inc(sem(f"x{t}_in"), 16)
        for n in range(len(UNITS)):
            if n >= RING:
                sp.wait_ge(units_used, n - RING + 1)
            for dst, src in unit_parts(n):
                sp.dma_start(dst, src).then_inc(slot_full[n % RING], 16)
        for c in range(2):
            for t in range(NT):
                sp.wait_ge(acc_free[t], DENSE["w_out_o_2"] + c + 1)
                cols = slice(c * 512, c * 512 + 512)
                sp.dma_start(out[0, t * P:(t + 1) * P, cols], x[:, t, cols]).then_inc(sem("stored"), 16)
        sp.wait_ge(sem("stored"), 64)

    @block.gpsimd
    def _(pool):
        g = nc.gpsimd
        chain = [0]

        def link(ins):
            chain[0] += 1
            ins.then_inc(sem("pool_chain"), 1)
            pool.wait_ge(sem("pool_chain"), chain[0])

        def power(name, o, i, n):
            pool.wait_ge(sem(name + "_ms"), 1)
            g.tensor_tensor(o, i, halfs[:, 0:n], ALU.pow).then_inc(sem(name + "_rstd"), 1)

        def split(which):
            for u in range(*POOL_UNITS[which]):
                pool.wait_ge(hi_ready, u + 1)
                size = UNITS[u][3] * UNITS[u][4]
                g.tensor_tensor(w_lo[:, u % RING, 0:size], w_raw[:, u % RING, 0:size],
                                w_hi[:, u % RING, 0:size].bitcast(F32), ALU.subtract).then_inc(pool_lo, 1)

        def norm_power(k):
            for t in range(NT):
                pool.wait_ge(sem(f"norm{k}_ms"), t + 1)
                g.tensor_tensor(rstd[:, t:t + 1], ms[:, t:t + 1], halfs[:, 0:1], ALU.pow)\
                 .then_inc(sem(f"norm{k}_rstd"), 1)

        link(g.memset(halfs, -0.5))
        norm_power(0)
        for s, name in ((0, "cmp_k_w2"), (1, "cmp_k_w2"), (2, "cmp_v_w2")):
            pool.dma_start(w2[:, :, s * 64:s * 64 + 64], a[name][0].rearrange("(f p) n -> p f n", p=P))\
                .then_inc(sem("small_in"), 16)
        pool.dma_start(pe_sb[:, 0, :], a["cmp_pe_k"]).then_inc(sem("small_in"), 16)
        pool.dma_start(pe_sb[:, 1, :], a["cmp_pe_v"]).then_inc(sem("small_in"), 16)
        pool.dma_start(gsub[:, :], a["g_sub_d_2"].rearrange("o n -> n o")).then_inc(sem("small_in"), 16)
        pool.dma_start(gains[:, :], a["gains"].partition_broadcast(P)).then_inc(sem("gains_in"), 16)
        g.memset(extra[:, 2560:3072], 0.0).then_inc(sem("zeros"), 1)
        pool.wait_ge(t_filled, FILL["norm0"] + 4)
        g.memset(hA[:, :, 512:1024], 0.0).then_inc(sem("zeros"), 1)
        for t in range(NT):
            pool.wait_ge(acc_free[t], DENSE["w_in_e"] + 2)
            src = z0[:, t, 512:768].rearrange("p (h d) -> p h d", d=HD)
            for c in range(2):
                ins = g.tensor_copy(kd[:, t, 0:4, c, :], src)
        ins.then_inc(sem("cmp_dup"), 1)
        split("attn0")
        norm_power(1)
        norm_power(2)
        split("attn1")
        norm_power(3)
        for t in range(NT):
            for k in (4, 5):
                pool.wait_ge(sem(f"norm{k}_ms"), t + 1)
                g.tensor_tensor(rstd[:, t:t + 1], ms[:, t:t + 1], halfs[:, 0:1], ALU.pow)\
                 .then_inc(sem(f"norm{k}_rstd"), 1)
        rp = a["rpb_a_2"]
        n_bias = 0
        for half in range(2):
            for u in range(6):
                dr = u - 2 - half
                src = bass.AP(rp.tensor, rp.offset + (dr + 7) * 31 + 15 - 63, [[1, 64], [15 * 31, 8], [1, 64]])
                pool.dma_start(bias_na[64 * half:64 * half + 64, :, u, :], src).then_inc(sem("bias_in"), 16)
                n_bias += 16

        def window(h):
            for half in range(2):
                part = bias_na[64 * half:64 * half + 64, h]
                lo = part[:, :, 16:64]
                link(g.affine_select(out=lo, in_=lo, compare_op=ALU.is_ge, fill=NEG, base=8 + 47,
                                     pattern=[[0, 6], [-1, 48]], channel_multiplier=-1))
                hi = part[:, :, 0:48]
                link(g.affine_select(out=hi, in_=hi, compare_op=ALU.is_ge, fill=NEG, base=7 - 63,
                                     pattern=[[0, 6], [1, 48]], channel_multiplier=1))
            pool.sem_inc(sem("bias_ready"), 1)

        power("qa", hrs[:, 0:16], hss[:, 0:16], 16)
        pool.wait_ge(sem("bias_in"), n_bias)
        window(0)
        power("ka", hrs[:, 16:32], hss[:, 16:32], 16)
        window(1)
        window(2)
        power("qb", hrs[:, 32:48], hss[:, 32:48], 16)
        power("kb", hrs[:, 48:52], hss[:, 48:52], 4)
        for h in range(3, 8):
            window(h)
        split("attn2")
        norm_power(6)
        power("lora", hrs[:, 0:4], hss[:, 0:4], 4)
        power("qd", hrs[:, 4:20], hss[:, 4:20], 16)
        split("lora")
        power("kd", hrs[:, 20:36], hss[:, 20:36], 16)
        power("mla", hrs[:, 0:32], hss[:, 0:32], 32)
        split("gate_o")
        pool.wait_ge(sem("gsub_ready"), 1)
        for t in range(NT):
            pool.wait_ge(acc_free[t], DENSE["gate_o"] + 4)
        gd = gT[:, 4:8, :].rearrange("p (f h) t -> p f (h t)", f=2)
        link(g.tensor_scalar(gd, gd, gsub[:, 0:1], None, ALU.mult))
        split("attn3")
        for hf in range(2):
            pool.wait_ge(mix_hi, PAIR0["attn3"] + 2 * hf + 2)
            if hf == 0:
                link(g.memset(ones, 1.0))
            link(g.tensor_tensor(od_sq[:, hf, :], odp[:, hf, :], odp[:, hf, :], ALU.mult))
            pool.sem_inc(sem("od_sq"), 1)
        pool.wait_ge(sem("od_ms"), 1)
        g.tensor_tensor(od_rstd, od_rstd, halfs[:, 0:8], ALU.pow).then_inc(sem("od_rstd"), 1)
        g.tensor_tensor(odp, odp, gd, ALU.mult).then_inc(sem("od_gated"), 1)

    @block.scalar
    def _(act):
        n = nc.scalar
        split_to = [0]

        def split(upto):
            for u in range(split_to[0], min(upto, len(UNITS))):
                act.wait_ge(slot_full[u % RING], LANDED[u])
                if u >= RING:
                    act.wait_ge(units_used, u - RING + 1)
                size = UNITS[u][3] * UNITS[u][4]
                n.activation(w_hi[:, u % RING, 0:size], w_raw[:, u % RING, 0:size], ACT.Copy).then_inc(hi_ready, 1)
            split_to[0] = max(split_to[0], min(upto, len(UNITS)))

        def load_gain(k, wait, dst=None):
            name, r = NORM_G[k]
            src = a[name][r:r + 1, :] if name != "final_norm" else a[name].rearrange("(o n) -> o n", o=1)
            if wait is not None:
                act.wait_ge(sem(f"norm{wait}_h"), 4)
            act.dma_start(gb[:, :] if dst is None else dst, src.partition_broadcast(P))\
               .then_inc(sem(f"gain{k}_in"), 16)

        def square(k, t, c, ready, count):
            act.wait_ge(ready, count)
            cols = slice(c * 512, c * 512 + 512)
            n.activation(hA[:, t, cols], x[:, t, cols], ACT.Square, scale=D ** -0.5,
                         accum_out=ss[:, 2 * t + c:2 * t + c + 1]).then_inc(sem(f"norm{k}_ss"), 1)

        def high(k, t):
            for q in range(2):
                f = FILL[f"norm{k}"] + 2 * t + q
                act.wait_ge(t_filled, f + 1)
                n.activation(norm_dst(hT_hi, 2 * t + q), ps[:, TB + f % 2, :].rearrange("p (b t) -> p b t", b=4),
                             ACT.Copy).then_inc(t_hi, 1)

        def norm_out(name, k):
            for c in range(2):
                for t in range(NT):
                    square(k, t, c, acc_free[t], DENSE[name] + c + 1)
                    if c:
                        high(k, t)

        def norm_down(layer, k):
            for t in range(NT):
                for c in range(2):
                    square(k, t, c, acc_free[t], DENSE[f"down{layer}"] + c + 1)
                high(k, t)

        def drain(stage, fills):
            for k in fills:
                f = FILL[stage] + k
                if f % 2 == 0:
                    act.wait_ge(t_filled, f + 1)
                    rows = MLA_D if stage == "prep3" and k >= 4 else P
                    n.activation(reg[0:rows, 2 * k:2 * k + 2, :].rearrange("p b t -> p (b t)"),
                                 ps[0:rows, TB, :], ACT.Copy).then_inc(t_drained[0], 1)

        def take(name, c, dst, dense=None, done=None):
            d = DENSE[name] + c if dense is None else dense
            act.wait_ge(units_used, done)
            lo, w = dst[1:]
            n.activation(dst[0][:, 0, lo:lo + w], ps[:, 2 * (d % 2), 0:w], ACT.Copy).then_inc(acc_free[0], 1)

        def chunk(name, c, buf):
            done = LAST[name, c]
            split(done + AHEAD)
            take(name, c, (buf, *COLS[name][0][c]), done=done)

        def gate_chunks(name, which, dense):
            for g, c in enumerate(which):
                done = LAST[name, c]
                split(done + AHEAD)
                act.wait_ge(units_used, done)
                for b in range(4):
                    d = dense + 2 * g + b // 2
                    n.activation(gT[:, 4 * g + b, :], ps[:, 2 * (d % 2) + b % 2, 0:T], ACT.Silu)\
                     .then_inc(acc_free[b % 2], 1)

        def ffn(layer):
            for j in range(FT):
                g = layer * FT + j
                done = LAST[f"gu{layer}", j // 2]
                if j % 2 == 0:
                    split(done + AHEAD)
                    act.wait_ge(even_up, layer * FT // 2 + j // 2 + 1)
                else:
                    act.wait_ge(units_used, done)
                if g >= 2:
                    act.wait_ge(hid32_ready, g - 1)
                n.activation(silu_g[:, g % 2, :], ps[:, g % 4, 0:T], ACT.Silu).then_inc(silu_ready, 1)
                act.wait_ge(hid32_ready, g + 1)
                n.activation(hid_hi[:, j, :], hid32[:, g % 2, :], ACT.Copy).then_inc(hid_hi_ready, 1)
            for j in range(FT):
                split(LAST[f"down{layer}", j] + AHEAD)

        def attention(stage):
            inst, i0, f0 = INST[stage], INST0[stage], FILL[stage]
            base = next_units(stage)
            for s in range(len(inst) + LAG + 5):
                if s < len(inst):
                    i, it = i0 + s, inst[s]
                    act.wait_ge(max_ready, i + 1)
                    if s >= 3:
                        act.wait_ge(t_filled, f0 + s - 2)
                    w = P if it["causal"] else T
                    n.activation(prob[:, i % 3, 0:w], ps[:, i % 3, 0:w], ACT.Exp, bias=negm[:, i, 0:1],
                                 accum_out=den[:, i, 0:1])
                    n.activation(prob[:, i % 3, 256:512], ps[:, i % 3, 256:512], ACT.Exp, bias=negm[:, i, 1:2],
                                 accum_out=den[:, i, 1:2]).then_inc(exp_ready, 1)
                    if "sink" in it:
                        h = it["sink"]
                        act.wait_ge(sem("sink_shift"), h + 1)
                        n.activation(esink[:, h, :], esink[:, h, :], ACT.Exp).then_inc(sem("esink"), 1)
                j = s - LAG
                if 0 <= j < len(inst) and (f0 + j) % 2 == 0:
                    i, f = i0 + j, f0 + j
                    w = 384 if inst[j]["causal"] else 512
                    act.wait_ge(t_filled, f + 1)
                    if j >= 2:
                        act.wait_ge(pv_done, i - 1)
                    n.activation(probT[:, i % 2, 0:w], ps[:, TB, 0:w], ACT.Copy).then_inc(t_drained[0], 1)
                e = s - LAG - (3 if gated(stage, s - LAG - 3) else 2)
                if 0 <= e < len(inst) and inst[e]["ends"]:
                    mix_high(stage, e)
                if s >= 3 and s % 2:
                    split(base + min(RING, (0 if stage == "attn0" else AHEAD) + (s - 1) // 2))
                if stage == "attn3" and s in (18, 19):
                    hf = s - 18
                    act.wait_ge(sem("od_normed"), hf + 1)
                    n.activation(hT_hi[:, 4 + 2 * hf:6 + 2 * hf, :].rearrange("p h t -> p (h t)"), odp[:, hf, :],
                                 ACT.Copy).then_inc(sem("od_hi"), 1)

        def mix_high(stage, e):
            p = inst_pair(stage, e)
            if stage in ("attn0", "attn1"):
                act.wait_ge(pv_done, INST0[stage] + e + 1)
                src = ps[:, OB + p % 2, 0:T]
            elif stage == "attn3" and p - PAIR0[stage] < 4:
                k = p - PAIR0[stage]
                act.wait_ge(pv_done, INST0[stage] + e + 1)
                n.activation(od[:, k, :], ps[:, OB + p % 2, 0:T], ACT.Copy).then_inc(mix_hi, 1)
                return
            else:
                act.wait_ge(mix_prod, prods(stage, p))
                src = tmp[:, (p % 2) * T:(p % 2) * T + T]
            n.activation(hT_hi[:, mix_tile(stage, p), :], src, ACT.Copy).then_inc(mix_hi, 1)

        load_gain(0, None)
        act.dma_start(ident, a["tables"][:, 0:P]).then_inc(sem("ident_in"), 16)
        act.dma_start(table[:, P:], a["tables"][:, P:]).then_inc(sem("table_in"), 16)
        for t in range(NT):
            for c in range(2):
                square(0, t, c, sem(f"x{t}_in"), 16)
        high(0, 0)
        split(4)
        high(0, 1)
        load_gain(1, 0)
        chunk("w_in_e", 0, z0)
        act.wait_ge(sem("table_in"), 16)
        n.activation(ident_b[:, :], ident, ACT.Copy)
        n.activation(ident_r[:, :], ident, ACT.Copy)
        n.activation(mask_b[:, :, :], masks[:, 0:2, :], ACT.Copy)
        n.activation(logc[:, 0, :], masks[:, 2, :], ACT.Copy).then_inc(sem("narrow"), 1)
        chunk("w_in_e", 1, z0)
        drain("prep0", range(0, 4))
        chunk("w_in_e", 2, z0)
        drain("prep0", range(4, 7))
        act.wait_ge(acc_free[1], DENSE["w_in_e"] + 3)
        n.activation(small[:, 200:248].rearrange("p (t n) -> p t n", t=2), z0[:, :, 1280:1304], ACT.Exp, scale=-1.0)\
         .then_inc(sem("gate_exp"), 1)
        chunk("w_in_e", 3, z0)
        drain("prep0", range(7, 8))
        chunk("w_in_e", 4, z0)
        done = LAST["cmp_k_w1", 0]
        split(done + AHEAD)
        act.wait_ge(units_used, done)
        n.activation(h1[:, 0:256], ps[0:32, H1, 0:256], ACT.Silu).then_inc(sem("h1"), 1)
        done = LAST["cmp_v_w1", 0]
        split(done + AHEAD)
        act.wait_ge(units_used, done)
        n.activation(h1[:, 256:512], ps[0:32, H1 + 1, 0:256], ACT.Silu).then_inc(sem("h1"), 1)
        drain("prep0", range(8, 11))
        act.wait_ge(sem("cmp_shift"), 1)
        n.activation(cexp, cexp, ACT.Exp).then_inc(sem("cmp_exp"), 1)
        attention("attn0")

        def projection_out(name):
            for c in range(2):
                split(LAST[name, c] + AHEAD)

        projection_out("w_out_e")
        norm_out("w_out_e", 1)
        load_gain(2, 1)
        ffn(0)
        norm_down(0, 2)
        load_gain(3, 2)
        for c in range(6):
            chunk("w_qkv_o", c, z1)
            if 1 <= c < 5:
                drain("prep1", range(2 * c - 2, 2 * c))
        attention("attn1")
        projection_out("w_out_o")
        norm_out("w_out_o", 3)
        load_gain(5, 3)
        load_gain(4, 3, dst=gain_final)
        ffn(1)
        for t in range(NT):
            for c in range(2):
                square(4, t, c, acc_free[t], DENSE["down1"] + c + 1)
            for c in range(2):
                square(5, t, c, sem("norm4_h"), 2 * t + c + 1)
            if t == 0:
                high(5, 0)
        high(5, 1)
        load_gain(6, 5)

        def squares(name, src, count):
            act.wait_ge(sem(name + "_in"), 1)
            n.activation(tmp_heads(src), src, ACT.Square).then_inc(sem(name + "_sq"), 1)

        chunk("w_in_e_2", 0, z2)
        squares("qa", heads(z2[:, :, 0:512]), 8)
        chunk("w_in_e_2", 1, z2)
        squares("ka", heads(z2[:, :, 512:1024]), 8)
        chunk("w_in_e_2", 2, z2)
        drain("prep2", range(0, 2))
        chunk("w_in_e_2", 3, z2)
        squares("qb", heads(z2[:, :, 1536:2048]), 8)
        drain("prep2", range(2, 4))
        chunk("w_in_e_2", 4, z2)
        squares("kb", heads(z2[:, :, 2048:2176]), 2)
        gate_chunks("w_in_e_2", (5, 6), DENSE["gate_e"])
        drain("prep2", range(4, 7))
        attention("attn2")
        projection_out("w_out_e_2")
        norm_out("w_out_e_2", 6)
        chunk("w_in_o_2", 0, z3)
        chunk("w_in_o_2", 1, z3)
        squares("qd", heads(z3[:, :, 416:928]), 8)
        for k in range(2):
            f = FILL["lora"] + k
            act.wait_ge(t_filled, f + 1)
            n.activation(lr_hi[:, 2 * k:2 * k + 2, :].rearrange("p b t -> p (b t)"), ps[:, TB + f % 2, :], ACT.Copy)\
             .then_inc(sem("lora_hi"), 1)
        chunk("w_in_o_2", 2, z3)
        squares("kd", heads(z3[:, :, 928:1440]), 8)
        split(LAST["w_cq_b_2", 0] + AHEAD)
        act.wait_ge(units_used, LAST["w_cq_b_2", 0])
        for c, (lo, w) in enumerate(cut(0, 768)):
            d = DENSE["w_cq_b_2"] + c
            n.activation(lo_q[:, 0, lo:lo + w], ps[:, 2 * (d % 2), 0:w], ACT.Copy).then_inc(acc_free[0], 1)
        split(LAST["w_ckv_b_2", 0] + AHEAD)
        act.wait_ge(units_used, LAST["w_ckv_b_2", 0])
        for c, (lo, w) in enumerate(cut(0, 1024)):
            d = DENSE["w_ckv_b_2"] + c
            n.activation(lo_kv[:, 0, lo:lo + w], ps[:, 2 * (d % 2), 0:w], ACT.Copy).then_inc(acc_free[0], 1)
        act.wait_ge(sem("lam_dots"), 1)
        n.activation(lam[:, 0:2], ldot, ACT.Exp).then_inc(sem("lam_exp"), 1)
        split(LAST["w_in_o_2", 3] + AHEAD)
        take("w_in_o_2b", 0, (z3, *COLS["w_in_o_2"][0][3]), done=LAST["w_in_o_2", 3])
        drain("prep3", range(0, 4))
        for name, src in (("qc", heads(lo_q, MLA_D)), ("kc", kcat)):
            act.wait_ge(sem(name + "_in"), 1)
            n.activation(tmp_heads(src), src, ACT.Square).then_inc(sem(name + "_sq"), 1)
        gate_chunks("w_in_o_2", (4, 5), DENSE["gate_o"])
        drain("prep3", range(4, 12))
        attention("attn3")
        projection_out("w_out_o_2")

    @block.vector
    def _(dve):
        v = nc.vector
        chain = [0]
        split_to = [0]

        def link(ins):
            chain[0] += 1
            ins.then_inc(sem("dve_chain"), 1)
            dve.wait_ge(sem("dve_chain"), chain[0])

        def signal(ins, name, k=1):
            ins.then_inc(sem(name), 1)
            dve.wait_ge(sem(name), k)

        def split(upto):
            for u in range(split_to[0], min(upto, len(UNITS))):
                if by_pool(u):
                    continue
                dve.wait_ge(hi_ready, u + 1)
                size = UNITS[u][3] * UNITS[u][4]
                v.tensor_tensor(w_lo[:, u % RING, 0:size], w_raw[:, u % RING, 0:size],
                                w_hi[:, u % RING, 0:size].bitcast(F32), ALU.subtract).then_inc(lo_ready, 1)
            split_to[0] = max(split_to[0], min(upto, len(UNITS)))

        def stats(k, t, eps, pieces):
            dve.wait_ge(sem(f"norm{k}_ss"), pieces)
            v.scalar_tensor_tensor(out=ms[:, t:t + 1], in0=ss[:, 2 * t:2 * t + 1], scalar=eps,
                                   in1=ss[:, 2 * t + 1:2 * t + 2], op0=ALU.add, op1=ALU.add)\
             .then_inc(sem(f"norm{k}_ms"), 1)

        def scale(k, t, q, dst=None, g=None):
            dve.wait_ge(sem(f"norm{k}_rstd"), t + 1)
            if t == 0 and q == 0:
                dve.wait_ge(sem(f"gain{k}_in"), 16)
            cols = slice(q * 512, q * 512 + 512)
            v.scalar_tensor_tensor(out=(hA if dst is None else dst)[:, t, cols], in0=x[:, t, cols],
                                   scalar=rstd[:, t:t + 1], in1=(gb if g is None else g)[:, cols],
                                   op0=ALU.mult, op1=ALU.mult).then_inc(sem(f"norm{k}_h"), 1)

        def low(k, fill):
            f = FILL[f"norm{k}"] + fill
            dve.wait_ge(t_hi, NORM_HI[f"norm{k}"] + fill + 1)
            v.tensor_tensor(norm_dst(hT_lo, fill), ps[:, TB + f % 2, :].rearrange("p (b t) -> p b t", b=4),
                            norm_dst(hT_hi, fill).bitcast(F32), ALU.subtract).then_inc(t_drained[f % 2], 1)

        def norm_first(k, eps, pieces):
            stats(k, 0, eps, pieces)
            scale(k, 0, 0)
            scale(k, 0, 1)

        def norm_second(k, eps):
            stats(k, 1, eps, 4)
            for q in range(2):
                scale(k, 1, q)
            split(LAST["w_in_e", 0])
            for q in range(2):
                low(k, 2 + q)

        def drain(stage, fills):
            for k in fills:
                f = FILL[stage] + k
                if f % 2:
                    dve.wait_ge(t_filled, f + 1)
                    rows = MLA_D if stage == "prep3" and k >= 4 else P
                    v.tensor_copy(reg[0:rows, 2 * k:2 * k + 2, :].rearrange("p b t -> p (b t)"),
                                  ps[0:rows, TB + 1, :]).then_inc(t_drained[1], 1)

        def wait_taken(name, count):
            for t in range(NT):
                dve.wait_ge(acc_free[t], DENSE[name] + count)

        def take(d, buf, lo, w, done):
            dve.wait_ge(units_used, done)
            v.tensor_copy(buf[:, 1, lo:lo + w], ps[:, 2 * (d % 2) + 1, 0:w]).then_inc(acc_free[1], 1)

        def chunk(name, c, buf):
            done = LAST[name, c]
            split(done + AHEAD)
            take(DENSE[name] + c, buf, *COLS[name][0][c], done)
            wait_taken(name, c + 1)

        def add(name, t, c):
            d = DENSE[name] + c
            cols = slice(c * 512, c * 512 + 512)
            v.tensor_tensor(x[:, t, cols], x[:, t, cols], ps[:, 2 * (d % 2) + t, :], ALU.add)\
             .then_inc(acc_free[t], 1)

        def added(name, t):
            dve.wait_ge(acc_free[t], DENSE[name] + 2)

        def add_down(layer, t):
            name = f"down{layer}"
            if t == 0:
                dve.wait_ge(sem("down_first"), layer + 1)
            else:
                dve.wait_ge(units_used, LAST[name, FT - 1])
            add(name, t, 0)
            add(name, t, 1)
            added(name, t)

        def rotate(src, dst_list, rt_, H, half):
            t_ = tm(H, 2 * half)
            cos, sin = rt_[:, :, 0, :], rt_[:, :, 1, :]
            sh = [P, NT, H, half]
            v.tensor_tensor(t_[:, :, :, 0:half], src[:, :, :, half:2 * half],
                            bc(sin[:, :, 0:half].unsqueeze(2), sh), ALU.mult)
            link(v.tensor_tensor(t_[:, :, :, half:2 * half], src[:, :, :, 0:half],
                                 bc(sin[:, :, half:2 * half].unsqueeze(2), sh), ALU.mult))
            first = dst_list[0]
            link(v.tensor_tensor(first, src, bc(cos.unsqueeze(2), [P, NT, H, 2 * half]), ALU.mult))
            for dst in reversed(dst_list):
                link(v.tensor_tensor(dst, first, t_, ALU.add))

        def ffn(layer):
            for j in range(FT):
                g = layer * FT + j
                if j % 2 == 0:
                    split(LAST[f"gu{layer}", j // 2] + AHEAD)
                dve.wait_ge(silu_ready, g + 1)
                v.tensor_tensor(hid32[:, g % 2, :], silu_g[:, g % 2, :], ps[:, g % 4, T:2 * T], ALU.mult)\
                 .then_inc(hid32_ready, 1)
                dve.wait_ge(hid_hi_ready, g + 1)
                v.tensor_tensor(hid_lo[:, j, :], hid32[:, g % 2, :], hid_hi[:, j, :].bitcast(F32), ALU.subtract)\
                 .then_inc(hid_ready, 1)
            for j in range(FT):
                split(LAST[f"down{layer}", j] + AHEAD)

        def attention(stage, at_step=None):
            inst, i0, f0 = INST[stage], INST0[stage], FILL[stage]
            for s in range(len(inst) + LAG + 5):
                if s < len(inst):
                    i, it = i0 + s, inst[s]
                    dve.wait_ge(scores_ready, i + 1)
                    logits = ps[:, i % 3, :].rearrange("p (t k) -> p t k", t=2)
                    if it["causal"]:
                        v.tensor_reduce(out=negm[:, i, 0:1], in_=logits[:, 0, 0:P], axis=AX.X, op=ALU.max, negate=True)
                        ins = v.tensor_reduce(out=negm[:, i, 1:2], in_=logits[:, 1, :], axis=AX.X, op=ALU.max,
                                              negate=True)
                    else:
                        ins = v.tensor_reduce(out=negm[:, i, :], in_=logits, axis=AX.X, op=ALU.max, negate=True)
                    if "sink" in it:
                        h = it["sink"]
                        link(ins)
                        v.tensor_tensor(negm[:, i, :], negm[:, i, :], bc(nsink[:, h:h + 1], [P, 2]), ALU.min)\
                         .then_inc(max_ready, 1)
                        dve.wait_ge(max_ready, i + 1)
                        v.tensor_tensor(esink[:, h, :], negm[:, i, :], bc(sinks[:, h:h + 1], [P, 2]), ALU.add)\
                         .then_inc(sem("sink_shift"), 1)
                    else:
                        ins.then_inc(max_ready, 1)
                j = s - 1
                if 0 <= j < len(inst):
                    scale_probs(stage, j)
                j = s - LAG
                if 0 <= j < len(inst) and (f0 + j) % 2:
                    f, i = f0 + j, i0 + j
                    w = 384 if inst[j]["causal"] else 512
                    dve.wait_ge(t_filled, f + 1)
                    if j >= 2:
                        dve.wait_ge(pv_done, i - 1)
                    v.tensor_copy(probT[:, i % 2, 0:w], ps[:, TB + 1, 0:w]).then_inc(t_drained[1], 1)
                e = s - LAG - 2
                if 0 <= e < len(inst) and inst[e]["ends"] and gated(stage, e):
                    mix_product(stage, e)
                e = s - LAG - (4 if gated(stage, s - LAG - 4) else 3)
                if 0 <= e < len(inst) and inst[e]["ends"]:
                    mix_low(stage, e)
                if at_step:
                    at_step(s)

        def scale_probs(stage, j):
            i, it = INST0[stage] + j, INST[stage][j]
            dve.wait_ge(exp_ready, i + 1)
            if "sink" in it:
                dve.wait_ge(sem("esink"), it["sink"] + 1)
                link(v.tensor_tensor(den[:, i, :], den[:, i, :], esink[:, it["sink"], :], ALU.add))
            link(v.reciprocal(fac[:, i, :], den[:, i, :]))
            if "gate" in it:
                h, br = it["gate"]
                link(v.tensor_tensor(fac[:, i, :], fac[:, i, :], gates[:, :, h, br], ALU.mult))
            if it.get("lam"):
                link(v.tensor_tensor(fac[:, i, :], fac[:, i, :], bc(lam[:, 2:3], [P, 2]), ALU.mult))
            w = P if it["causal"] else T
            v.tensor_scalar(prob[:, i % 3, 0:w], prob[:, i % 3, 0:w], fac[:, i, 0:1], None, ALU.mult)
            v.tensor_scalar(prob[:, i % 3, 256:512], prob[:, i % 3, 256:512], fac[:, i, 1:2], None, ALU.mult)\
             .then_inc(probs_ready, 1)

        def mix_product(stage, e):
            p = inst_pair(stage, e)
            dve.wait_ge(pv_done, INST0[stage] + e + 1)
            if prods(stage, p) > 2:
                dve.wait_ge(mix_lo, lows(p) - 2)
            v.tensor_tensor(tmp[:, (p % 2) * T:(p % 2) * T + T], ps[:, OB + p % 2, 0:T], gT[:, mix_tile(stage, p), :],
                            ALU.mult).then_inc(mix_prod, 1)

        def mix_low(stage, e):
            p = inst_pair(stage, e)
            if 24 <= p < 28:
                return
            src = tmp[:, (p % 2) * T:(p % 2) * T + T] if gated(stage, e) else ps[:, OB + p % 2, 0:T]
            dve.wait_ge(mix_hi, p + 1)
            k = mix_tile(stage, p)
            v.tensor_tensor(hT_lo[:, k, :], src, hT_hi[:, k, :].bitcast(F32), ALU.subtract).then_inc(mix_lo, 1)

        norm_first(0, EPS_1, 2)
        low(0, 0)
        low(0, 1)
        split(1)
        norm_second(0, EPS_1)
        chunk("w_in_e", 0, z0)
        dve.wait_ge(sem("table_in"), 16)
        rotate(heads(z0[:, :, 0:512]), [heads(hA[:, :, 0:512])], rope_q, 8, 32)
        dve.sem_inc(sem("q0_ready"), 1)
        dve.wait_ge(sem("narrow"), 1)
        link(v.tensor_tensor(logc[:, 1, :], masks[:, 2, :], logc[:, 0, :].bitcast(F32), ALU.subtract))
        chunk("w_in_e", 1, z0)
        rotate(heads(z0[:, :, 768:896]), [kd[:, :, 4:6, 0, :], kd[:, :, 4:6, 1, :]], rope, 2, 32)
        dve.sem_inc(sem("ks_ready"), 1)
        drain("prep0", range(0, 4))
        chunk("w_in_e", 2, z0)
        rotate(heads(z0[:, :, 1024:1152]), [kd[:, :, 6:8, 0, :], kd[:, :, 6:8, 1, :]], rope, 2, 32)
        dve.sem_inc(sem("kw_ready"), 1)
        drain("prep0", range(4, 7))
        dve.wait_ge(t_drained[0], (FILL["prep0"] + 6 + 1) // 2)
        dve.wait_ge(t_drained[1], (FILL["prep0"] + 6) // 2)
        dve.wait_ge(sem("small_in"), 96)
        split(LAST["w_in_e", 3] + 2)
        bt32 = tmp[:, 0:1024].rearrange("p (s l n) -> p s l n", s=2, l=16)
        v.memset(bt32[:, :, :, 2 * CMP:32], 0.0)
        for s in range(2):
            for u in range(2):
                for l2 in range(2):
                    pr = slice(64 * l2, 64 * l2 + 64)
                    blk = reg[pr, BLOCK["prep0"]["cmp", 2 * s + u], :]
                    src = bass.AP(blk.tensor, blk.offset + l2, [blk.ap[0], [2, 16], [16, CMP]])
                    ins = v.tensor_tensor(bt32[pr, s, :, u * CMP:(u + 1) * CMP], src,
                                          bc(pe_sb[pr, s, :].unsqueeze(2), [64, 16, CMP]), ALU.add)
        link(ins)
        link(v.tensor_copy(bt_hi[:, :, :, :], bt32))
        signal(v.tensor_tensor(bt_lo[:, :, :, :], bt32, bt_hi[:, :, :, :].bitcast(F32), ALU.subtract), "blocks")
        chunk("w_in_e", 3, z0)
        drain("prep0", range(7, 8))
        chunk("w_in_e", 4, z0)
        split(LAST["cmp_v_w1", 0])
        rotate(heads(z0[:, :, 1304:1816]), [heads(z0[:, :, 1304:1816])], rope_q, 8, 32)
        rotate(heads(z0[:, :, 1816:1944]), [kd[:, :, 8:10, 0, :], kd[:, :, 8:10, 1, :]], rope, 2, 32)
        dve.sem_inc(sem("b_ready"), 1)
        dve.wait_ge(sem("gains_in"), 16)
        link(v.tensor_scalar(nsink, sinks, -1.0, None, ALU.mult))
        dve.wait_ge(sem("gate_exp"), 1)
        link(v.tensor_scalar(small[:, 200:248], small[:, 200:248], 1.0, None, ALU.add))
        link(v.reciprocal(small[:, 200:248], small[:, 200:248]))
        split(LAST["cmp_v_w1", 0])
        drain("prep0", range(8, 11))
        dve.wait_ge(sem("h1_T"), 1)
        dve.wait_ge(sem("zeros"), 2)
        for f in range(2):
            ins = v.tensor_copy(h1k[:, f, :], ps[:, HT, 32 * f:32 * f + 2 * CMP])
        ins.then_inc(sem("h1k"), 1)
        for f in range(2):
            for u in range(2):
                lo = 64 + 32 * f + CMP * u
                ins = v.tensor_copy(h1v[:, f, u, :, 0:CMP], bc(ps[:, HT, lo:lo + CMP].unsqueeze(1), [P, 4, CMP]))
        ins.then_inc(sem("h1v"), 1)
        dve.wait_ge(sem("kc"), 1)
        v.tensor_scalar(kcT, ps[:, KC, 0:2 * CMP], SCALE, None, ALU.mult).then_inc(sem("kc_sb"), 1)
        dve.wait_ge(sem("vc"), 1)
        for u in range(2):
            for h in range(4):
                ins = v.tensor_copy(vbd[32 * h:32 * h + 32, u, 64 * h:64 * h + 64],
                                    ps[32 * h:32 * h + 32, VC, 64 * u:64 * u + 64])
        ins.then_inc(sem("vc_sb"), 1)
        dve.wait_ge(sem("cmp_scores"), 1)
        ce = cexp.rearrange("p (g c) -> p g c", c=CMP)
        cs = cexp.rearrange("p (u t h o c) -> p u t h o c", u=2, t=2, h=2, o=2)
        for odd in range(2):
            sc = ps[:, CS + odd, 0:256].rearrange("p (u t h c) -> p u t h c", u=2, t=2, h=2)
            for u in range(2):
                ins = v.tensor_tensor(cs[:, u, :, :, odd, :], sc[:, u, :, :, 0:CMP],
                                      bc(cmask[:, :, 0:CMP].unsqueeze(2), [P, 2, 2, CMP]), ALU.add)
        link(ins)
        link(v.tensor_reduce(out=cm, in_=ce, axis=AX.X, op=ALU.max))
        link(v.tensor_scalar(cm, cm, NEG / 2, None, ALU.max))
        signal(v.tensor_tensor(ce, ce, bc(cm.unsqueeze(2), [P, 16, CMP]), ALU.subtract), "cmp_shift")
        dve.wait_ge(sem("cmp_exp"), 1)
        link(v.tensor_reduce(out=cden, in_=ce, axis=AX.X, op=ALU.add))
        link(v.tensor_scalar(cden, cden, 1e-30, None, ALU.max))
        link(v.reciprocal(cfac, cden))
        for u in range(2):
            ins = v.tensor_tensor(cfac[:, 8 * u:8 * u + 8].rearrange("p (t h) -> p t h", t=2),
                                  cfac[:, 8 * u:8 * u + 8].rearrange("p (t h) -> p t h", t=2),
                                  gates[:, :, 4 * u:4 * u + 4, 0], ALU.mult)
        link(ins)
        signal(v.tensor_tensor(pcmp.rearrange("p u t h c -> p (u t h) c")[:, :, 0:CMP], ce,
                               bc(cfac.unsqueeze(2), [P, 16, CMP]), ALU.mult), "pcmp")

        def take_compressed(s):
            if s == 1:
                f = FILL["cmp_p"]
                dve.wait_ge(t_filled, f + 1)
                v.tensor_copy(pcT.rearrange("p u q -> p (u q)"), ps[:, TB + f % 2, :]).then_inc(t_drained[f % 2], 1)

        attention("attn0", take_compressed)

        def projection_out(name, index, k, eps):
            split(LAST[name, 1] + AHEAD)
            dve.wait_ge(units_used, LAST[name, 0])
            for t in range(NT):
                add(name, t, 0)
            dve.wait_ge(sem("out_first"), index)
            add(name, 0, 1)
            if k is not None:
                added(name, 0)
                norm_first(k, eps, 3)
                low(k, 0)
                low(k, 1)
            dve.wait_ge(units_used, LAST[name, 1])
            add(name, 1, 1)
            if k is not None:
                added(name, 1)
                norm_second(k, eps)

        projection_out("w_out_e", 1, 1, EPS_1)
        ffn(0)
        add_down(0, 0)
        norm_first(2, EPS_1, 2)
        low(2, 0)
        low(2, 1)
        add_down(0, 1)
        norm_second(2, EPS_1)
        for c in range(6):
            chunk("w_qkv_o", c, z1)
            if c < 4:
                sec = heads(z1[:, :, 512 * c:512 * c + 512])
                rotate(sec, [sec], rope_q if c < 2 else rope, 8, 32)
                dve.sem_inc(sem("qk1_ready"), 1)
            if 1 <= c < 5:
                drain("prep1", range(2 * c - 2, 2 * c))
        attention("attn1")
        projection_out("w_out_o", 2, 3, EPS_1)
        ffn(1)
        for t in range(NT):
            add_down(1, t)
            if t:
                low(5, 0)
                low(5, 1)
            stats(4, t, EPS_1, 2 * t + 2)
            scale(4, t, 0, dst=x, g=gain_final)
            scale(4, t, 1, dst=x, g=gain_final)
            if t == 0:
                dve.wait_ge(sem("norm4_h"), 2)
                norm_first(5, EPS_2, 2)
        dve.wait_ge(sem("norm4_h"), 4)
        norm_second(5, EPS_2)

        def head_stats(name, at, H, w, src):
            dve.sem_inc(sem(name + "_in"), 1)
            dve.wait_ge(sem(name + "_sq"), 1)
            sq = tmp_heads(src)
            link(v.tensor_reduce(out=hss[:, at:at + NT * H].rearrange("p (t h) -> p t h", t=NT), in_=sq, axis=AX.X,
                                 op=ALU.add))
            signal(v.tensor_scalar(hss[:, at:at + NT * H], hss[:, at:at + NT * H], 1.0 / w, EPS_2, ALU.mult, ALU.add),
                   name + "_ms")

        def head_scale(name, at, H, w, src, g=None):
            dve.wait_ge(sem(name + "_rstd"), 1)
            r_ = hrs[:, at:at + NT * H].rearrange("p (t h) -> p t h", t=NT)
            link(v.tensor_tensor(src, src, bc(r_.unsqueeze(3), [P, NT, H, w]), ALU.mult))
            if g is not None:
                for t in range(NT):
                    ins = v.tensor_tensor(src[:, t], src[:, t], bc(g.unsqueeze(1), [P, H, w]), ALU.mult)
                link(ins)

        def gain_tables(c, s, table_, g, half, blocks, scale):
            w = 2 * half * blocks
            dst_c, dst_s = gtab[:, :, c, :], gtab[:, :, s, :]
            v.tensor_tensor(dst_c, table_[:, :, 0, :], bc(g[:, 0:w].unsqueeze(1), [P, NT, w]), ALU.mult)
            for b in range(blocks):
                for h in range(2):
                    o, i = b * 2 * half + h * half, b * 2 * half + (1 - h) * half
                    ins = v.tensor_tensor(dst_s[:, :, o:o + half], table_[:, :, 1, o:o + half],
                                          bc(g[:, i:i + half].unsqueeze(1), [P, NT, half]), ALU.mult)
            link(ins)
            if scale != 1.0:
                v.tensor_scalar(dst_c, dst_c, scale, None, ALU.mult)
                link(v.tensor_scalar(dst_s, dst_s, scale, None, ALU.mult))

        def rotate_axial(src, dst, c, s, H):
            cos, sin = gtab[:, :, c, :], gtab[:, :, s, :]
            t_ = tm(H).rearrange("p t h (b c) -> p t h b c", b=4)
            s_ = src.rearrange("p t h (b c) -> p t h b c", b=4)
            for b in range(4):
                ins = v.tensor_tensor(t_[:, :, :, b, :], s_[:, :, :, b ^ 1, :],
                                      bc(sin[:, :, 16 * b:16 * b + 16].unsqueeze(2), [P, NT, H, 16]), ALU.mult)
            link(ins)
            link(v.tensor_tensor(src, src, bc(cos.unsqueeze(2), [P, NT, H, HD]), ALU.mult))
            for d_ in dst:
                link(v.tensor_tensor(d_, src, tm(H), ALU.add))

        qa, ka = heads(z2[:, :, 0:512]), heads(z2[:, :, 512:1024])
        qb, kb = heads(z2[:, :, 1536:2048]), heads(z2[:, :, 2048:2176])
        chunk("w_in_e_2", 0, z2)
        head_stats("qa", 0, 8, HD, qa)
        link(v.tensor_scalar(gain("gq_a_2"), gain("gq_a_2"), SCALE, None, ALU.mult))
        gain_tables(0, 1, rope_ax, gain("gq_b_2"), 16, 2, SCALE)
        gain_tables(2, 3, rope_ax, gain("gk_b_2"), 16, 2, 1.0)
        head_scale("qa", 0, 8, HD, qa, gain("gq_a_2"))
        dve.sem_inc(sem("qa_ready"), 1)
        chunk("w_in_e_2", 1, z2)
        head_stats("ka", 16, 8, HD, ka)
        split(LAST["w_in_e_2", 2] + AHEAD)
        head_scale("ka", 16, 8, HD, ka, gain("gk_a_2"))
        dve.sem_inc(sem("ka_ready"), 1)
        chunk("w_in_e_2", 2, z2)
        drain("prep2", range(0, 2))
        chunk("w_in_e_2", 3, z2)
        head_stats("qb", 32, 8, HD, qb)
        drain("prep2", range(2, 4))
        chunk("w_in_e_2", 4, z2)
        head_scale("qb", 32, 8, HD, qb)
        head_stats("kb", 48, 2, HD, kb)
        dve.wait_ge(sem("kb_rstd"), 1)
        rotate_axial(qb, [qb], 0, 1, 8)
        dve.sem_inc(sem("qb_ready"), 1)
        head_scale("kb", 48, 2, HD, kb)
        rotate_axial(kb, [kb_dup[:, :, :, 0, :], kb_dup[:, :, :, 1, :]], 2, 3, 2)
        dve.sem_inc(sem("kb_ready"), 1)
        split(LAST["w_in_e_2", 6] + AHEAD)
        drain("prep2", range(4, 7))
        attention("attn2")
        projection_out("w_out_e_2", 3, 6, EPS_2)
        chunk("w_in_o_2", 0, z3)
        for t in range(NT):
            for k, (lo, w) in enumerate(((0, 256), (256, 128))):
                link(v.tensor_tensor_reduce(out=tmp[:, 0:w], in0=z3[:, t, lo:lo + w], in1=z3[:, t, lo:lo + w],
                                            scale=1.0 / w, scalar=0.0, op0=ALU.mult, op1=ALU.add,
                                            accum_out=hss[:, 2 * t + k:2 * t + k + 1]))
        signal(v.tensor_scalar(hss[:, 0:4], hss[:, 0:4], EPS_2, None, ALU.add), "lora_ms")
        for k in range(2):
            link(v.tensor_tensor_reduce(out=tmp[:, 0:HD], in0=gain(f"lam_q{k + 1}_2"), in1=gain(f"lam_k{k + 1}_2"),
                                        scale=1.0, scalar=0.0, op0=ALU.mult, op1=ALU.add,
                                        accum_out=ldot[:, k:k + 1]))
        dve.sem_inc(sem("lam_dots"), 1)
        dve.wait_ge(sem("lora_rstd"), 1)
        for t in range(NT):
            for k, (lo, w, gn) in enumerate(((0, 256, "g_cq_2"), (256, 128, "g_ckv_2"))):
                ins = v.scalar_tensor_tensor(out=z3[:, t, lo:lo + w], in0=z3[:, t, lo:lo + w],
                                             scalar=hrs[:, 2 * t + k:2 * t + k + 1], in1=gain(gn),
                                             op0=ALU.mult, op1=ALU.mult)
        signal(ins, "lora_ready")
        qd_, kd_ = heads(z3[:, :, 416:928]), heads(z3[:, :, 928:1440])
        chunk("w_in_o_2", 1, z3)
        head_stats("qd", 4, 8, HD, qd_)
        for k in range(2):
            f = FILL["lora"] + k
            dve.wait_ge(sem("lora_hi"), k + 1)
            v.tensor_tensor(lr_lo[:, 2 * k:2 * k + 2, :].rearrange("p b t -> p (b t)"), ps[:, TB + f % 2, :],
                            lr_hi[:, 2 * k:2 * k + 2, :].rearrange("p b t -> p (b t)").bitcast(F32), ALU.subtract)\
             .then_inc(t_drained[f % 2], 1)
        link(v.tensor_scalar(gain("gq_c_2"), gain("gq_c_2"), float(MLA_D) ** -0.5, None, ALU.mult))
        link(v.tensor_scalar(gain("gq_d_2"), gain("gq_d_2"), SCALE, None, ALU.mult))
        link(v.tensor_scalar(gsub[:, :], gsub[:, :], 1.0 - LAM_INIT, None, ALU.mult))
        dve.sem_inc(sem("gsub_ready"), 1)
        head_scale("qd", 4, 8, HD, qd_, gain("gq_d_2"))
        rotate(qd_[:, :, :, 0:16], [qd_[:, :, :, 0:16]], rope_part, 8, 8)
        dve.sem_inc(sem("qd_ready"), 1)
        chunk("w_in_o_2", 2, z3)
        head_stats("kd", 20, 8, HD, kd_)
        split(LAST["w_cq_b_2", 0] + AHEAD)
        for c, (lo, w) in enumerate(cut(0, 768)):
            take(DENSE["w_cq_b_2"] + c, lo_q, lo, w, LAST["w_cq_b_2", 0])
        head_scale("kd", 20, 8, HD, kd_, gain("gk_d_2"))
        rotate(kd_[:, :, :, 0:16], [kd_[:, :, :, 0:16]], rope_part, 8, 8)
        dve.sem_inc(sem("kd_ready"), 1)
        split(LAST["w_ckv_b_2", 0] + AHEAD)
        for c, (lo, w) in enumerate(cut(0, 1024)):
            take(DENSE["w_ckv_b_2"] + c, lo_kv, lo, w, LAST["w_ckv_b_2", 0])
        wait_taken("w_ckv_b_2", 2)
        dve.wait_ge(sem("lam_exp"), 1)
        link(v.tensor_tensor(lam[:, 3:4], lam[:, 1:2], lam[:, 0:1], ALU.subtract))
        link(v.tensor_scalar(lam[:, 2:3], lam[:, 3:4], -LAM_INIT, None, ALU.add))
        split(LAST["w_in_o_2", 3] + AHEAD)
        take(DENSE["w_in_o_2b"], z3, *COLS["w_in_o_2"][0][3], LAST["w_in_o_2", 3])
        drain("prep3", range(0, 4))
        v.tensor_copy(kcat[:, :, :, 0:64], lo_kv.rearrange("p t (h d) -> p t h d", d=128)[:, :, :, 0:64])
        link(v.tensor_copy(kcat[:, :, :, 64:96], bc(z3[:, :, 384:416].unsqueeze(2), [P, NT, 8, 32])))
        qh = heads(lo_q, MLA_D)
        for name, src, at in (("qc", qh, 0), ("kc", kcat, 16)):
            dve.sem_inc(sem(name + "_in"), 1)
            dve.wait_ge(sem(name + "_sq"), 1)
            link(v.tensor_reduce(out=hss[:, at:at + 16].rearrange("p (t h) -> p t h", t=NT), in_=tmp_heads(src),
                                 axis=AX.X, op=ALU.add))
        signal(v.tensor_scalar(hss[:, 0:32], hss[:, 0:32], 1.0 / MLA_D, EPS_2, ALU.mult, ALU.add), "mla_ms")
        split(LAST["w_in_o_2", 4] + AHEAD)
        dve.wait_ge(sem("mla_rstd"), 1)
        for src, ro, gn in ((qh, 0, "gq_c_2"), (kcat, 16, "gk_c_2")):
            r_ = hrs[:, ro:ro + 16].rearrange("p (t h) -> p t h", t=NT)
            link(v.tensor_tensor(src, src, bc(r_.unsqueeze(3), [P, NT, 8, MLA_D]), ALU.mult))
            for t in range(NT):
                ins = v.tensor_tensor(src[:, t], src[:, t], bc(gain(gn).unsqueeze(1), [P, 8, MLA_D]), ALU.mult)
            link(ins)
            rotate(src[:, :, :, 64:96], [src[:, :, :, 64:96]], rope_mla, 8, 16)
            dve.sem_inc(sem("mla_ready"), 1)
        drain("prep3", range(4, 12))

        def sub_norm(s):
            if s == 14:
                dve.wait_ge(sem("od_sum"), 1)
                v.tensor_scalar(od_rstd, ps[:, SUM, 0:8], 1.0 / P, EPS_2, ALU.mult, ALU.add).then_inc(sem("od_ms"), 1)
            if s == 16:
                dve.wait_ge(sem("od_rstd"), 1)
                for k in range(8):
                    ins = v.tensor_scalar(od_sq[:, k // 4, P * (k % 4):P * (k % 4) + P], ident, od_rstd[:, k:k + 1],
                                          None, ALU.mult)
                ins.then_inc(sem("od_diag"), 1)
            if s == 18:
                dve.wait_ge(sem("od_gated"), 1)
                for hf in range(2):
                    dve.wait_ge(sem("od_factor"), hf + 1)
                    v.tensor_tensor(odp[:, hf, :], odp[:, hf, :], ps[:, OF[hf], :], ALU.mult)\
                     .then_inc(sem("od_normed"), 1)
            if s == 19:
                for hf in range(2):
                    dve.wait_ge(sem("od_hi"), hf + 1)
                    hi_, lo_ = (b[:, 4 + 2 * hf:6 + 2 * hf, :].rearrange("p h t -> p (h t)") for b in (hT_hi, hT_lo))
                    v.tensor_tensor(lo_, odp[:, hf, :], hi_.bitcast(F32), ALU.subtract).then_inc(sem("od_done"), 1)

        attention("attn3", sub_norm)
        projection_out("w_out_o_2", 4, None, None)

    @block.tensor
    def _(pe):
        m = nc.tensor

        def open_fill(f):
            if f >= 2:
                pe.wait_ge(t_drained[f % 2], f // 2)

        def drained(f):
            pe.wait_ge(t_drained[0], (f + 2) // 2)
            pe.wait_ge(t_drained[1], (f + 1) // 2)

        def transpose_blocks(stage, fills):
            for k in fills:
                f = FILL[stage] + k
                open_fill(f)
                for b, (kind, i) in enumerate(PREP[stage][2 * k:2 * k + 2]):
                    for t in range(NT):
                        src = source(kind, i, t)
                        ins = m.transpose(ps[0:src.shape[1], TB + f % 2, b * T + t * P:b * T + t * P + P], src, ident)
                ins.then_inc(t_filled, 1)

        def norm_tile(k, t):
            for q in range(2):
                pe.wait_ge(sem(f"norm{k}_h"), 2 * t + q + 1)
                f = FILL[f"norm{k}"] + 2 * t + q
                open_fill(f)
                for b in range(4):
                    kt = 4 * q + b
                    ins = m.transpose(ps[:, TB + f % 2, b * P:b * P + P], hA[:, t, kt * P:(kt + 1) * P], ident)
                ins.then_inc(t_filled, 1)

        def tile_ready(k, t, kk):
            if kk in (0, 4):
                drained(FILL[f"norm{k}"] + 2 * t + kk // 4)

        def product(o, lhs, rhs, start, stop):
            m.matmul(o, lhs[1], rhs[0], start=start, stop=False)
            m.matmul(o, lhs[0], rhs[0], start=False, stop=False)
            return m.matmul(o, lhs[0], rhs[1], start=False, stop=stop)

        def chunk(name, c, dense, lhs=(hT_hi, hT_lo), tiles=KT, ready=None):
            for u in range(FIRST[name, c], LAST[name, c]):
                pe.wait_ge(*low_ready(u))
                _, _, k0, ks, w = UNITS[u]
                wh, wl = halves(u)
                for t in range(NT):
                    if k0 == 0 and dense >= 2:
                        pe.wait_ge(acc_free[t], dense - 1)
                    for k in range(ks):
                        kk = k0 + k
                        if ready and t == 0:
                            ready(kk)
                        l = tuple(b[:, kk, t * P:(t + 1) * P] for b in lhs)
                        ins = product(ps[:, 2 * (dense % 2) + t, 0:w], l, (wh[:, k, :], wl[:, k, :]),
                                      kk == 0, kk == tiles - 1)
                ins.then_inc(units_used, 1)

        def first_chunk(name, k):
            d = DENSE[name]
            for t in range(NT):
                if d >= 2:
                    pe.wait_ge(acc_free[t], d - 1)
                for u in range(FIRST[name, 0], LAST[name, 0]):
                    if t == 0 and u == LAST[name, 0] - 1:
                        norm_tile(k, 1)
                    pe.wait_ge(*low_ready(u))
                    _, _, k0, ks, w = UNITS[u]
                    wh, wl = halves(u)
                    for i in range(ks):
                        kk = k0 + i
                        tile_ready(k, t, kk)
                        l = tuple(b[:, kk, t * P:(t + 1) * P] for b in (hT_hi, hT_lo))
                        ins = product(ps[:, 2 * (d % 2) + t, 0:w], l, (wh[:, i, :], wl[:, i, :]), kk == 0, kk == KT - 1)
                    if t:
                        ins.then_inc(units_used, 1)

        def wide(name, widths, dense, lhs, tiles):
            for u in range(FIRST[name, 0], LAST[name, 0]):
                pe.wait_ge(*low_ready(u))
                kk = UNITS[u][2]
                wh, wl = halves(u)
                for c, (lo, w) in enumerate(widths):
                    d = dense + c
                    for t in range(NT):
                        if kk == 0:
                            pe.wait_ge(acc_free[t], d - 1)
                        l = tuple(b[:, kk, t * P:(t + 1) * P] for b in lhs)
                        ins = product(ps[:, 2 * (d % 2) + t, 0:w], l, (wh[:, 0, lo:lo + w], wl[:, 0, lo:lo + w]),
                                      kk == 0, kk == tiles - 1)
                ins.then_inc(units_used, 1)

        def gate_chunk(name, c, dense):
            for t in range(NT):
                pe.wait_ge(acc_free[t], dense)
            for u in range(FIRST[name, c], LAST[name, c]):
                pe.wait_ge(*low_ready(u))
                _, _, k0, ks, w = UNITS[u]
                wh, wl = halves(u)
                for b in range(4):
                    d = dense + b // 2
                    for k in range(ks):
                        kk = k0 + k
                        cols = slice(b * P, b * P + P)
                        ins = product(ps[:, 2 * (d % 2) + b % 2, 0:T], (wh[:, k, cols], wl[:, k, cols]),
                                      (hT_hi[:, kk, :], hT_lo[:, kk, :]), kk == 0, kk == KT - 1)
                ins.then_inc(units_used, 1)

        def ffn(layer):
            for c in range(FT // 2):
                first, last = FIRST[f"gu{layer}", c], LAST[f"gu{layer}", c]
                pe.wait_ge(*low_ready(last - 1))
                for j in (2 * c, 2 * c + 1):
                    g = layer * FT + j
                    if j >= 4:
                        pe.wait_ge(hid32_ready, g - 3)
                    for gate in range(2):
                        for u in range(first, last):
                            wh, wl = halves(u)
                            lo = 256 * gate + P * (j % 2)
                            for k in range(2):
                                kk = UNITS[u][2] + k
                                if c == j == gate == 0:
                                    tile_ready(1 + 2 * layer, 1, kk)
                                ins = product(ps[:, g % 4, T * gate:T * gate + T],
                                              (wh[:, k, lo:lo + P], wl[:, k, lo:lo + P]),
                                              (hT_hi[:, kk, :], hT_lo[:, kk, :]), kk == 0, kk == KT - 1)
                            if gate and j % 2:
                                ins.then_inc(units_used, 1)
                    if j % 2 == 0:
                        ins.then_inc(even_up, 1)
            d = DENSE[f"down{layer}"]

            def down(j, t):
                u = FIRST[f"down{layer}", j]
                pe.wait_ge(*low_ready(u))
                pe.wait_ge(hid_ready, layer * FT + j + 1)
                wh, wl = halves(u)
                for half in range(2):
                    if j == 0:
                        bank = 2 * ((d + half) % 2) + t
                        pe.wait_ge(hid32_ready, max(g for g in range((layer + 1) * FT) if g % 4 == bank) + 1)
                    cols = slice(half * 512, half * 512 + 512)
                    l = tuple(b[:, j, t * P:(t + 1) * P] for b in (hid_hi, hid_lo))
                    ins = product(ps[:, 2 * ((d + half) % 2) + t, :], l, (wh[:, 0, cols], wl[:, 0, cols]),
                                  j == 0, j == FT - 1)
                return ins

            for j in range(FT - TAIL):
                for t in range(NT):
                    ins = down(j, t)
                ins.then_inc(units_used, 1)
            for j in range(FT - TAIL, FT):
                ins = down(j, 0)
            ins.then_inc(sem("down_first"), 1)
            for j in range(FT - TAIL, FT):
                if j == FT - 1 and layer == 0:
                    norm_tile(2, 0)
                down(j, 1).then_inc(units_used, 1)

        def attention(stage, at_step=None):
            inst, i0, f0 = INST[stage], INST0[stage], FILL[stage]
            for s in range(len(inst) + LAG + 1):
                if s < len(inst):
                    i, it = i0 + s, inst[s]
                    if s >= 3:
                        pe.wait_ge(exp_ready, i - 2)
                    if stage == "attn2" and s < 8:
                        pe.wait_ge(sem("bias_ready"), s + 1)
                    for t in range(NT):
                        w = P * (t + 1) if it["causal"] else T
                        o = ps[:, i % 3, 256 * t:256 * t + w]
                        passes = it["bias"](t) if it["bias"] is not None else []
                        for n_, (idm, b) in enumerate(passes):
                            m.matmul(o, idm, b, start=n_ == 0, stop=False)
                        ins = m.matmul(o, it["q"][:, t * P:(t + 1) * P], it["k"][:, 0:w], start=not passes, stop=True)
                    ins.then_inc(scores_ready, 1)
                j = s - LAG
                if 0 <= j < len(inst):
                    i, f, causal = i0 + j, f0 + j, inst[j]["causal"]
                    pe.wait_ge(probs_ready, i + 1)
                    open_fill(f)
                    for kt in range(NT):
                        for t in range(NT):
                            if not (causal and kt > t):
                                col = column(kt, t, causal)
                                ins = m.transpose(ps[:, TB + f % 2, col:col + P],
                                                  prob[:, i % 3, 256 * t + kt * P:256 * t + kt * P + P], ident)
                    ins.then_inc(t_filled, 1)
                j = s - LAG - 1
                if 0 <= j < len(inst):
                    i, f, it = i0 + j, f0 + j, inst[j]
                    p = inst_pair(stage, j)
                    buf, lo, w = it["v"]
                    rows = slice(64 * it["half"], 64 * it["half"] + w)
                    if it["opens"] and p >= 2:
                        pe.wait_ge(*bank_taken(p - 2))
                    if it["opens"] and stage == "attn0" and it["pair"] < 4:
                        q = it["pair"]
                        m.matmul(ps[:, OB + p % 2, 0:T], vbd[:, q // 2, P * (q % 2):P * (q % 2) + P],
                                 pcT[:, q // 2, :], start=True, stop=False, skip_group_check=True)
                    pe.wait_ge(t_drained[f % 2], f // 2 + 1)
                    o = ps[rows, OB + p % 2, 0:T]
                    m.matmul(o, buf[:, 0, lo:lo + w], probT[:, i % 2, 0:T], start=it["first"], stop=False,
                             skip_group_check=True)
                    if it["causal"]:
                        ins = m.matmul(ps[rows, OB + p % 2, P:T], buf[:, 1, lo:lo + w], probT[:, i % 2, T:T + P],
                                       start=False, stop=it["last"], skip_group_check=True)
                    else:
                        ins = m.matmul(o, buf[:, 1, lo:lo + w], probT[:, i % 2, T:2 * T], start=False,
                                       stop=it["last"], skip_group_check=True)
                    ins.then_inc(pv_done, 1)
                if at_step:
                    at_step(s)

        pe.wait_ge(sem("ident_in"), 16)
        norm_tile(0, 0)
        d = DENSE["w_in_e"]
        first_chunk("w_in_e", 0)
        chunk("w_in_e", 1, d + 1)
        pe.wait_ge(sem("q0_ready"), 1)
        transpose_blocks("prep0", range(0, 4))
        chunk("w_in_e", 2, d + 2)
        pe.wait_ge(sem("cmp_dup"), 1)
        pe.wait_ge(sem("ks_ready"), 1)
        transpose_blocks("prep0", range(4, 7))
        chunk("w_in_e", 3, d + 3)
        pe.wait_ge(sem("kw_ready"), 1)
        transpose_blocks("prep0", range(7, 8))
        chunk("w_in_e", 4, d + 4)
        pe.wait_ge(sem("blocks"), 1)
        for t in range(NT):
            pe.wait_ge(acc_free[t], d + 4)
        for s, name in enumerate(("cmp_k_w1", "cmp_v_w1")):
            for u in range(FIRST[name, 0], LAST[name, 0]):
                pe.wait_ge(*low_ready(u))
                wh, wl = halves(u)
                for k in range(4):
                    l = UNITS[u][2] + k
                    ins = product(ps[0:32, H1 + s, 0:256], (bt_hi[:, s, l, :], bt_lo[:, s, l, :]),
                                  (wh[:, k, :], wl[:, k, :]), l == 0, l == 15)
                ins.then_inc(units_used, 1)
        pe.wait_ge(sem("b_ready"), 1)
        transpose_blocks("prep0", range(8, 11))
        for t in range(NT):
            pe.wait_ge(acc_free[t], d + 5)
        pe.wait_ge(sem("h1"), 2)
        for s in range(2):
            for f in range(2):
                lo = 32 * (2 * s + f)
                ins = m.transpose(ps[:, HT, lo:lo + 32], h1[:, 256 * s + P * f:256 * s + P * f + P], ident[0:32, 0:32])
        ins.then_inc(sem("h1_T"), 1)
        pe.wait_ge(sem("h1k"), 1)
        pe.wait_ge(sem("small_in"), 96)
        for f in range(2):
            ins = m.matmul(ps[:, KC, 0:2 * CMP], w2[:, f, 0:128], h1k[:, f, :], start=f == 0, stop=f == 1)
        ins.then_inc(sem("kc"), 1)
        pe.wait_ge(sem("h1v"), 1)
        for u in range(2):
            for f in range(2):
                ins = m.matmul(ps[:, VC, 64 * u:64 * u + 64], h1v[:, f, u, :, :].rearrange("p h c -> p (h c)"),
                               w2[:, f, 128:192], start=f == 0, stop=f == 1)
        ins.then_inc(sem("vc"), 1)
        drained(FILL["prep0"] + 10)
        pe.wait_ge(sem("kc_sb"), 1)
        for u in range(2):
            for t in range(NT):
                for h in range(4):
                    q = pair_row("prep0", "qp", 4 * u + h)
                    lo = HD * (h % 2)
                    col = ((u * 2 + t) * 2 + h // 2) * 32
                    ins = m.matmul(ps[:, CS + h % 2, col:col + CMP], q[:, t * P:(t + 1) * P],
                                   kcT[lo:lo + HD, u * CMP:(u + 1) * CMP], start=True, stop=True)
        ins.then_inc(sem("cmp_scores"), 1)

        def compressed(s):
            if s == 1:
                pe.wait_ge(sem("pcmp"), 1)
                f = FILL["cmp_p"]
                open_fill(f)
                for u in range(2):
                    for t in range(NT):
                        ins = m.transpose(ps[:, TB + f % 2, (2 * u + t) * P:(2 * u + t + 1) * P],
                                          pcmp[:, u, t, :, :].rearrange("p h c -> p (h c)"), ident)
                ins.then_inc(t_filled, 1)
            if s == 2:
                drained(FILL["cmp_p"])
                pe.wait_ge(sem("vc_sb"), 1)

        pe.wait_ge(sem("narrow"), 1)
        attention("attn0", compressed)

        def project_out(name, stage, norm=None):
            def ready(kk):
                if stage != "attn3":
                    pe.wait_ge(mix_lo, lows(PAIR0[stage] + kk))
                elif kk < 4:
                    pe.wait_ge(mix_lo, lows(PAIR0[stage] + 4 + kk))
                else:
                    pe.wait_ge(sem("od_done"), kk // 2 - 1)

            chunk(name, 0, DENSE[name], ready=ready)
            d = DENSE[name] + 1
            for t in range(NT):
                pe.wait_ge(acc_free[t], d - 1)
                for u in range(FIRST[name, 1], LAST[name, 1]):
                    pe.wait_ge(*low_ready(u))
                    wh, wl = halves(u)
                    for k in range(2):
                        if t and u == LAST[name, 1] - 1 and k == 1 and norm is not None:
                            norm_tile(norm, 0)
                        kk = UNITS[u][2] + k
                        l = tuple(b[:, kk, t * P:(t + 1) * P] for b in (hT_hi, hT_lo))
                        ins = product(ps[:, 2 * (d % 2) + t, :], l, (wh[:, k, :], wl[:, k, :]), kk == 0, kk == KT - 1)
                    if t:
                        ins.then_inc(units_used, 1)
                if t == 0:
                    ins.then_inc(sem("out_first"), 1)

        project_out("w_out_e", "attn0", 1)
        norm_tile(1, 1)
        ffn(0)
        first_chunk("w_qkv_o", 2)
        for c in range(6):
            if c:
                chunk("w_qkv_o", c, DENSE["w_qkv_o"] + c)
            if 1 <= c < 5:
                pe.wait_ge(sem("qk1_ready"), c)
                transpose_blocks("prep1", range(2 * c - 2, 2 * c))
        for t in range(NT):
            pe.wait_ge(acc_free[t], DENSE["w_qkv_o"] + 6)
        drained(FILL["prep1"] + 7)
        attention("attn1")
        project_out("w_out_o", "attn1", 3)
        norm_tile(3, 1)
        ffn(1)
        norm_tile(5, 0)
        d = DENSE["w_in_e_2"]
        first_chunk("w_in_e_2", 5)
        chunk("w_in_e_2", 1, d + 1)
        chunk("w_in_e_2", 2, d + 2)
        pe.wait_ge(sem("qa_ready"), 1)
        transpose_blocks("prep2", range(0, 2))
        chunk("w_in_e_2", 3, d + 3)
        pe.wait_ge(sem("ka_ready"), 1)
        transpose_blocks("prep2", range(2, 4))
        chunk("w_in_e_2", 4, d + 4)
        gate_chunk("w_in_e_2", 5, DENSE["gate_e"])
        gate_chunk("w_in_e_2", 6, DENSE["gate_e"] + 2)
        pe.wait_ge(sem("qb_ready"), 1)
        transpose_blocks("prep2", range(4, 6))
        pe.wait_ge(sem("kb_ready"), 1)
        transpose_blocks("prep2", range(6, 7))
        for t in range(NT):
            pe.wait_ge(acc_free[t], DENSE["gate_e"] + 4)
        drained(FILL["prep2"] + 6)
        attention("attn2")
        project_out("w_out_e_2", "attn2", 6)
        d = DENSE["w_in_o_2"]
        first_chunk("w_in_o_2", 6)
        chunk("w_in_o_2", 1, d + 1)
        pe.wait_ge(sem("lora_ready"), 1)
        for k in range(2):
            f = FILL["lora"] + k
            open_fill(f)
            for b in range(2):
                for t in range(NT):
                    c = min(2 * k + b, 2)
                    ins = m.transpose(ps[:, TB + f % 2, b * T + t * P:b * T + t * P + P],
                                      z3[:, t, c * P:(c + 1) * P], ident)
            ins.then_inc(t_filled, 1)
        chunk("w_in_o_2", 2, d + 2)
        drained(FILL["lora"] + 1)
        wide("w_cq_b_2", cut(0, 768), DENSE["w_cq_b_2"], (lr_hi, lr_lo), 2)
        wide("w_ckv_b_2", cut(0, 1024), DENSE["w_ckv_b_2"], (lr_hi[:, 2:3, :], lr_lo[:, 2:3, :]), 1)
        chunk("w_in_o_2", 3, DENSE["w_in_o_2b"])
        pe.wait_ge(sem("qd_ready"), 1)
        transpose_blocks("prep3", range(0, 2))
        pe.wait_ge(sem("kd_ready"), 1)
        transpose_blocks("prep3", range(2, 4))
        gate_chunk("w_in_o_2", 4, DENSE["gate_o"])
        gate_chunk("w_in_o_2", 5, DENSE["gate_o"] + 2)
        pe.wait_ge(sem("mla_ready"), 1)
        transpose_blocks("prep3", range(4, 8))
        pe.wait_ge(sem("mla_ready"), 2)
        transpose_blocks("prep3", range(8, 12))
        for t in range(NT):
            pe.wait_ge(acc_free[t], DENSE["gate_o"] + 4)
        drained(FILL["prep3"] + 11)

        def sub_norm(s):
            if s == 13:
                pe.wait_ge(sem("od_sq"), 2)
                for k in range(8):
                    ins = m.matmul(ps[:, SUM, k:k + 1], od_sq[:, k // 4, P * (k % 4):P * (k % 4) + P], ones[:, 0:1],
                                   start=True, stop=True)
                ins.then_inc(sem("od_sum"), 1)
            if s == 17:
                pe.wait_ge(sem("od_diag"), 1)
                pe.wait_ge(exp_ready, INST0["attn3"] + 16)
                for hf in range(2):
                    m.matmul(ps[:, OF[hf], :], ones[:, :], od_sq[:, hf, :], start=True, stop=True)\
                     .then_inc(sem("od_factor"), 1)

        attention("attn3", sub_norm)
        project_out("w_out_o_2", "attn3")

    ctx.close()


def rotation(angles, signs, scale=1.0):
    t = np.stack([np.cos(angles), np.sin(angles) * signs], axis=1).astype(np.float32) * np.float32(scale)
    return t.reshape(NT, P, -1).transpose(1, 0, 2).reshape(P, -1)


def tables():
    f = np.float32
    pos = np.arange(T, dtype=f)

    def turned(p, dim, theta):
        inv = (1.0 / (f(theta) ** (np.arange(0, dim, 2, dtype=f) / f(dim)))).astype(f)
        a = (p[:, None] * inv[None, :]).astype(f)
        return np.concatenate([a, a], 1), np.concatenate([-np.ones(dim // 2, f), np.ones(dim // 2, f)])

    ar, sg = turned(np.floor(pos / 64).astype(f), 32, 10000.0)
    ac, _ = turned((pos % 64).astype(f), 32, 10000.0)
    i, j = np.arange(T)[:, None], np.arange(T)[None, :]
    causal = np.where(j <= i, 0.0, NEG)
    window = np.where((j <= i) & (i - j < 128), 0.0, NEG)
    count = (i - j <= 128).astype(int) + ((i - j) % 4 == 0) + ((i - j) % 16 == 0)
    dilated = np.where((j <= i) & (count > 0), np.log(np.maximum(count, 1)), NEG)
    c = np.arange(16)[None, :]
    cm = np.where((c * 16 + 31 <= i) & (c < CMP), 0.0, NEG)
    parts = {
        "ident": np.eye(P),
        "masks": np.concatenate([np.concatenate([b[0:P, 0:P], b[P:T, :]], axis=1)
                                 for b in (causal, window, dilated)], axis=1),
        "cmask": cm.reshape(NT, P, 16).transpose(1, 0, 2).reshape(P, -1),
        "rope": rotation(*turned(pos, HD, 10000.0)),
        "rope_q": rotation(*turned(pos, HD, 10000.0), SCALE),
        "rope_ax": rotation(np.concatenate([ar, ac], 1), np.concatenate([sg, sg])),
        "rope_mla": rotation(*turned(pos, 32, 10000.0)),
        "rope_part": rotation(*turned(pos, 16, 500000.0)),
    }
    return np.ascontiguousarray(np.concatenate([parts[name].astype(f) for name in TAB], axis=1))


def kernel(**inputs):
    import concourse.bacc as _bacc
    from concourse.bass_utils import run_bass_kernel_spmd as _run

    arrays = {name: np.ascontiguousarray(v) for name, v in inputs.items() if name not in GAIN}
    for name in ("cmp_pe_k", "cmp_pe_v"):
        arrays[name] = np.ascontiguousarray(arrays[name].reshape(16, P).T)
    arrays["rpb_a_2"] = np.ascontiguousarray(arrays["rpb_a_2"][..., ::-1])
    arrays["gains"] = np.ascontiguousarray(np.concatenate([np.asarray(inputs[n]).reshape(1, -1) for n in GAIN], 1))
    arrays["tables"] = tables()
    nc = _bacc.Bacc("TRN2", target_bir_lowering=False, num_devices=1)
    aps = {name: nc.dram_tensor("in_" + name, v.shape, F32, kind="ExternalInput").ap() for name, v in arrays.items()}
    out = nc.dram_tensor("out_0", (1, T, D), F32, kind="ExternalOutput").ap()
    net(nc, aps, out)
    r = _run(nc, [{"in_" + name: v for name, v in arrays.items()}], core_ids=[0])
    return r.results[0]["out_0"]
```
